# Optimizing a Trainium2 kernel written in Bass

```python
import math
import jax
import jax.numpy as jnp
from jax import lax
import numpy as np

D_MODEL = 1024
BATCH = 1
SEQ = 256
DEPTH = 2

GRID_W = 64
CTX_LEN = 256
N_MIXERS = 4
ALPHA = (2 * DEPTH) ** 0.25
BETA = (8 * DEPTH) ** -0.25
LN_EPS = 1e-5
SHORT_CONV = 3
MOD_CHUNKS = 6

HY_ORDER = 2
HY_BANDS = 8
HY_EMB = 1 + 2 * HY_BANDS
HY_FILTER_W = 64
HY_TARGET = 1e-2
HY_FAST = 0.3
HY_SLOW = 1.5

RW_HEAD = 64
RW_HEADS = D_MODEL // RW_HEAD
RW_DECAY_LORA = 64
RW_AAA_LORA = 64
RW_GATE_LORA = 160
RW_GN_EPS = 64e-5

SSD_INNER = 2 * D_MODEL
SSD_HEAD = 64
SSD_HEADS = SSD_INNER // SSD_HEAD
SSD_STATE = 128
SSD_GROUPS = 4
SSD_CHUNK = 64

GDN_HEAD = 128
GDN_QK_HEADS = D_MODEL // GDN_HEAD
GDN_V_HEADS = 2 * GDN_QK_HEADS
GDN_CHUNK = 64

FFN_DENSE = 2816
N_EXPERTS = 8
TOP_K = 2
FFN_EXPERT = 3584

F32 = jnp.float32

kernel_name = 'hybrid_hyena_rwkv7_ssd_gdn_moe_trunk'

def layer_norm(x, g, b):
    xf = x.astype(F32)
    xc = xf - jnp.mean(xf, -1, keepdims=True)
    var = jnp.mean(xc * xc, -1, keepdims=True)
    return (xc * lax.rsqrt(var + LN_EPS) * g.astype(F32) + b.astype(F32)).astype(x.dtype)

def rms_norm(x, g, eps=1e-6):
    xf = x.astype(F32)
    return (xf * lax.rsqrt(jnp.mean(xf * xf, -1, keepdims=True) + eps) * g.astype(F32)).astype(x.dtype)

def l2_normalize(x, eps=1e-6):
    xf = x.astype(F32)
    return xf * lax.rsqrt(jnp.sum(xf * xf, -1, keepdims=True) + eps)

def dwconv_centred(x, w, b=None):
    pad = w.shape[0] // 2
    y = lax.conv_general_dilated(x, w[:, None, :].astype(x.dtype), window_strides=(1,),
                                 padding=[(pad, pad)], dimension_numbers=('NWC', 'WIO', 'NWC'),
                                 feature_group_count=x.shape[-1])
    return y if b is None else y + b.astype(x.dtype)

def flip_tokens(t):
    return t[:, ::-1]

def keep_tokens(t):
    return t

def raster_to_column(x):
    B, L, C = x.shape
    rows = L // GRID_W
    return x.reshape(B, rows, GRID_W, C).transpose(0, 2, 1, 3).reshape(B, L, C)

def column_to_raster(x):
    B, L, C = x.shape
    rows = L // GRID_W
    return x.reshape(B, GRID_W, rows, C).transpose(0, 2, 1, 3).reshape(B, L, C)

def modulation(c, w, b):
    return jnp.split(jax.nn.silu(c) @ w + b, MOD_CHUNKS, axis=-1)

def hyena_filters(L, f_w1, f_b1, f_w2, f_b2, f_freq, f_w3, decay):
    pos = jnp.arange(L, dtype=F32)
    t01 = pos / max(L - 1, 1)
    bands = jnp.linspace(1e-4, HY_BANDS - 1, HY_BANDS, dtype=F32)
    ang = (2.0 * math.pi / L) * pos[:, None] * bands[None, :]
    feats = jnp.concatenate([t01[:, None], jnp.cos(ang), -jnp.sin(ang)], axis=-1)
    h = jnp.sin(f_freq[0].astype(F32) * (feats @ f_w1.astype(F32) + f_b1.astype(F32)))
    h = jnp.sin(f_freq[1].astype(F32) * (h @ f_w2.astype(F32) + f_b2.astype(F32)))
    k = (h @ f_w3.astype(F32)).reshape(L, 2 * HY_ORDER, D_MODEL)
    return k * jnp.exp(-t01[:, None, None] * jnp.abs(decay.astype(F32)))

def bidir_long_conv(z, k_fwd, k_bwd, skip):
    L = z.shape[1]
    kern = jnp.concatenate([k_fwd, jnp.zeros_like(k_fwd[:1]), k_bwd[:0:-1]], axis=0)
    kf = jnp.fft.rfft(kern, axis=0)
    zf = jnp.fft.rfft(z.astype(F32), n=2 * L, axis=1)
    y = jnp.fft.irfft(zf * kf[None], n=2 * L, axis=1)[:, :L]
    return (y + z.astype(F32) * skip.astype(F32)).astype(z.dtype)

def hyena_branch(u, w_in, b_in, conv_w, conv_b, f_w1, f_b1, f_w2, f_b2, f_freq, f_w3, decay, skip,
                 w_out, b_out):
    L = u.shape[1]
    proj = dwconv_centred(u @ w_in + b_in, conv_w, conv_b)
    v, x1, x2 = jnp.split(proj, 3, axis=-1)
    k = hyena_filters(L, f_w1, f_b1, f_w2, f_b2, f_freq, f_w3, decay)
    z = x1 * bidir_long_conv(v, k[:, 0], k[:, 1], skip[0])
    z = x2 * bidir_long_conv(z, k[:, 2], k[:, 3], skip[1])
    return z @ w_out + b_out

def hyena_mixer(uc, ux, with_ctx_out, *p):
    yx = hyena_branch(ux, *p)
    yc = hyena_branch(uc, *p) if with_ctx_out else None
    return yc, yx

def rwkv7_prep(u, mu, w_rkv, w0, w1, w2, a0, a1, a2, g1, g2, k_k, k_a):
    B, L, _ = u.shape
    H, N = RW_HEADS, RW_HEAD
    up = jnp.pad(u, ((0, 0), (1, 1), (0, 0)))
    xx = 0.5 * (up[:, :-2] + up[:, 2:]) - u
    xr, xw, xk, xv, xa, xg = [u + xx * mu[j] for j in range(6)]

    def heads(t):
        return t.astype(F32).reshape(B, L, H, N)

    r = heads(xr @ w_rkv[0])
    k = heads(xk @ w_rkv[1])
    v = heads(xv @ w_rkv[2])
    g = jax.nn.sigmoid(xg @ g1) @ g2
    kk = l2_normalize(k * k_k.astype(F32).reshape(H, N))
    dirs = []
    for d in range(2):
        logw = -jax.nn.softplus(-heads(w0[d] + jnp.tanh(xw @ w1[d]) @ w2[d])) - 0.5
        a = jax.nn.sigmoid(heads(a0[d] + (xa @ a1[d]) @ a2[d]))
        kd = k * (1.0 + (a - 1.0) * k_a.astype(F32).reshape(H, N))
        dirs.append((jnp.exp(-jnp.exp(logw)), kd, -kk, kk * a))
    return r, v, g, dirs

def wkv7_scan(S0, r, w, k, v, a, b):
    def step(S, inp):
        r_t, w_t, k_t, v_t, a_t, b_t = inp
        sa = jnp.einsum('bhvk,bhk->bhv', S, a_t)
        S = S * w_t[:, :, None, :] + sa[..., None] * b_t[:, :, None, :] + v_t[..., None] * k_t[:, :, None, :]
        return S, jnp.einsum('bhvk,bhk->bhv', S, r_t)
    xs = tuple(jnp.swapaxes(t, 0, 1) for t in (r, w, k, v, a, b))
    S, y = lax.scan(step, S0, xs)
    return S, jnp.swapaxes(y, 0, 1)

def rwkv7_mixer(uc, ux, with_ctx_out, mu, w_rkv, w0, w1, w2, a0, a1, a2, g1, g2, k_k, k_a, r_k,
                lnx_g, lnx_b, w_out):
    H, N = RW_HEADS, RW_HEAD
    rc, vc, gc, dirs_c = rwkv7_prep(uc, mu, w_rkv, w0, w1, w2, a0, a1, a2, g1, g2, k_k, k_a)
    rx, vx, gx, dirs_x = rwkv7_prep(ux, mu, w_rkv, w0, w1, w2, a0, a1, a2, g1, g2, k_k, k_a)
    S0 = jnp.zeros((ux.shape[0], H, N, N), F32)
    yc_sum, yx_sum = 0.0, 0.0
    for d in range(2):
        fl = flip_tokens if d == 1 else keep_tokens
        wc, kc, ac, bc = dirs_c[d]
        wx, kx, ax, bx = dirs_x[d]
        Sc, yc = wkv7_scan(S0, fl(rc), fl(wc), fl(kc), fl(vc), fl(ac), fl(bc))
        _, yx = wkv7_scan(Sc, fl(rx), fl(wx), fl(kx), fl(vx), fl(ax), fl(bx))
        yc_sum = yc_sum + fl(yc)
        yx_sum = yx_sum + fl(yx)

    def finish(y, r, v, g, dirs, dtype):
        B, L = y.shape[:2]
        yc0 = y - jnp.mean(y, -1, keepdims=True)
        var = jnp.mean(yc0 * yc0, -1, keepdims=True)
        y = yc0 * lax.rsqrt(var + RW_GN_EPS) * lnx_g.astype(F32).reshape(H, N) + lnx_b.astype(F32).reshape(H, N)
        rk = r_k.astype(F32)
        bonus = (jnp.sum(r * dirs[0][1] * rk, -1, keepdims=True) * v
                 + jnp.sum(r * dirs[1][1] * rk, -1, keepdims=True) * v)
        y = (y + bonus).reshape(B, L, D_MODEL).astype(dtype)
        return (y * g) @ w_out

    yx = finish(yx_sum, rx, vx, gx, dirs_x, ux.dtype)
    yc = finish(yc_sum, rc, vc, gc, dirs_c, uc.dtype) if with_ctx_out else None
    return yc, yx

def ssd_prep(u, w_in, conv_w, conv_b, dt_bias):
    B, L, _ = u.shape
    G, R, P, N = SSD_GROUPS, SSD_HEADS // SSD_GROUPS, SSD_HEAD, SSD_STATE
    z, xbc, dt = jnp.split(u @ w_in, [SSD_INNER, 2 * SSD_INNER + 2 * G * N], axis=-1)
    xbc = jax.nn.silu(dwconv_centred(xbc, conv_w, conv_b))
    xs, Bm, Cm = jnp.split(xbc, [SSD_INNER, SSD_INNER + G * N], axis=-1)
    xs = xs.astype(F32).reshape(B, L, G, R, P)
    Bm = Bm.astype(F32).reshape(B, L, G, N)
    Cm = Cm.astype(F32).reshape(B, L, G, N)
    dt = jax.nn.softplus(dt.astype(F32).reshape(B, L, 2, G, R) + dt_bias.astype(F32).reshape(2, G, R))
    return z, xs, Bm, Cm, dt

def ssd_scan(S0, x, Bm, Cm, dt, A):
    Bsz, L = x.shape[:2]
    nc = L // SSD_CHUNK

    def chunks(t):
        return jnp.moveaxis(t.reshape(Bsz, nc, SSD_CHUNK, *t.shape[2:]), 1, 0)

    tri = jnp.tril(jnp.ones((SSD_CHUNK, SSD_CHUNK), bool))[None, :, :, None, None]

    def step(S, inp):
        xq, Bq, Cq, dtq = inp
        cum = jnp.cumsum(dtq * A, axis=1)
        decay = jnp.exp(jnp.where(tri, cum[:, :, None] - cum[:, None], -jnp.inf))
        scores = jnp.einsum('bign,bjgn->bijg', Cq, Bq)[..., None] * decay * dtq[:, None]
        y = (jnp.einsum('bijgr,bjgrp->bigrp', scores, xq)
             + jnp.einsum('bign,bgrpn->bigrp', Cq, S) * jnp.exp(cum)[..., None])
        w_end = jnp.exp(cum[:, -1:] - cum) * dtq
        S = S * jnp.exp(cum[:, -1])[..., None, None] + jnp.einsum('bjgr,bjgn,bjgrp->bgrpn', w_end, Bq, xq)
        return S, y

    S, y = lax.scan(step, S0, tuple(chunks(t) for t in (x, Bm, Cm, dt)))
    return S, jnp.moveaxis(y, 0, 1).reshape(x.shape)

def ssd_mixer(uc, ux, with_ctx_out, w_in, conv_w, conv_b, dt_bias, A_log, d_skip, norm_g, w_out):
    G, R, P, N = SSD_GROUPS, SSD_HEADS // SSD_GROUPS, SSD_HEAD, SSD_STATE
    zc, xs_c, Bc, Cc, dtc = ssd_prep(uc, w_in, conv_w, conv_b, dt_bias)
    zx, xs_x, Bx, Cx, dtx = ssd_prep(ux, w_in, conv_w, conv_b, dt_bias)
    A = -jnp.exp(A_log.astype(F32)).reshape(2, G, R)
    d_gr = d_skip.astype(F32).reshape(G, R, 1)
    yc_sum, yx_sum = xs_c * d_gr, xs_x * d_gr
    S0 = jnp.zeros((ux.shape[0], G, R, P, N), F32)
    for d in range(2):
        fl = flip_tokens if d == 1 else keep_tokens
        Sc, yc = ssd_scan(S0, fl(xs_c), fl(Bc), fl(Cc), fl(dtc[:, :, d]), A[d])
        _, yx = ssd_scan(Sc, fl(xs_x), fl(Bx), fl(Cx), fl(dtx[:, :, d]), A[d])
        yc_sum = yc_sum + fl(yc)
        yx_sum = yx_sum + fl(yx)

    def finish(y, z):
        B, L = z.shape[:2]
        y = y.reshape(B, L, SSD_INNER).astype(z.dtype) * jax.nn.silu(z)
        y = rms_norm(y.reshape(B, L, G, SSD_INNER // G), norm_g.reshape(G, SSD_INNER // G))
        return y.reshape(B, L, SSD_INNER) @ w_out

    yx = finish(yx_sum, zx)
    yc = finish(yc_sum, zc) if with_ctx_out else None
    return yc, yx

def gdn_prep(u, w_in, conv_w, dt_bias, A_log):
    B, L, _ = u.shape
    Hk, Hv, Dh = GDN_QK_HEADS, GDN_V_HEADS, GDN_HEAD
    QK, VW = Hk * Dh, Hv * Dh
    qkv, z, ab = jnp.split(u @ w_in, [2 * QK + VW, 2 * QK + 2 * VW], axis=-1)
    qkv = jax.nn.silu(dwconv_centred(qkv, conv_w))
    q, k, v = jnp.split(qkv, [QK, 2 * QK], axis=-1)
    rep = Hv // Hk
    q = jnp.repeat(l2_normalize(q.reshape(B, L, Hk, Dh)), rep, axis=2) * (Dh ** -0.5)
    k = jnp.repeat(l2_normalize(k.reshape(B, L, Hk, Dh)), rep, axis=2)
    v = v.astype(F32).reshape(B, L, Hv, Dh)
    ab = ab.astype(F32).reshape(B, L, 2, 2, Hv)
    g = -jnp.exp(A_log.astype(F32)) * jax.nn.softplus(ab[:, :, 0] + dt_bias.astype(F32))
    beta = jax.nn.sigmoid(ab[:, :, 1])
    return q, k, v, z, g, beta

def gdn_scan(S0, q, k, v, g, beta):
    Bsz, L, H, Kd = k.shape
    Vd = v.shape[-1]
    C = GDN_CHUNK
    nc = L // C

    def chunks(t):
        t = t.reshape(Bsz, nc, C, H, *t.shape[3:])
        return jnp.moveaxis(jnp.moveaxis(t, 1, 0), 3, 2)

    eye = jnp.eye(C, dtype=F32)
    strict = jnp.tril(jnp.ones((C, C), bool), -1)
    incl = jnp.tril(jnp.ones((C, C), bool))

    def seg(Gq, mask):
        return jnp.exp(jnp.where(mask, Gq[..., :, None] - Gq[..., None, :], -jnp.inf))

    def step(S, inp):
        qn, kn, vn, gn, bn = inp
        Gn = jnp.cumsum(gn, axis=-1)
        kb = kn * bn[..., None]
        A = jnp.einsum('bhik,bhjk->bhij', kb, kn) * seg(Gn, strict)
        rhs = jnp.concatenate([vn * bn[..., None], kb * jnp.exp(Gn)[..., None]], axis=-1)
        sol = lax.linalg.triangular_solve(eye + A, rhs, left_side=True, lower=True, unit_diagonal=True)
        u = sol[..., :Vd] - jnp.einsum('bhck,bhkv->bhcv', sol[..., Vd:], S)
        attn = jnp.einsum('bhik,bhjk->bhij', qn, kn) * seg(Gn, incl)
        o = (jnp.einsum('bhck,bhkv->bhcv', qn * jnp.exp(Gn)[..., None], S)
             + jnp.einsum('bhij,bhjv->bhiv', attn, u))
        S = (S * jnp.exp(Gn[..., -1])[..., None, None]
             + jnp.einsum('bhck,bhcv->bhkv', kn * jnp.exp(Gn[..., -1:] - Gn)[..., None], u))
        return S, o

    S, o = lax.scan(step, S0, tuple(chunks(t) for t in (q, k, v, g, beta)))
    o = jnp.moveaxis(jnp.moveaxis(o, 0, 1), 2, 3).reshape(Bsz, L, H, Vd)
    return S, o

def gdn_mixer(uc, ux, with_ctx_out, w_in, conv_w, dt_bias, A_log, norm_g, w_out):
    Hv, Dh = GDN_V_HEADS, GDN_HEAD
    qc, kc, vc, zc, gc, bc = gdn_prep(uc, w_in, conv_w, dt_bias, A_log)
    qx, kx, vx, zx, gx, bx = gdn_prep(ux, w_in, conv_w, dt_bias, A_log)
    S0 = jnp.zeros((ux.shape[0], Hv, Dh, Dh), F32)
    oc_sum, ox_sum = 0.0, 0.0
    for d in range(2):
        fl = flip_tokens if d == 1 else keep_tokens
        Sc, oc = gdn_scan(S0, fl(qc), fl(kc), fl(vc), fl(gc[:, :, d]), fl(bc[:, :, d]))
        _, ox = gdn_scan(Sc, fl(qx), fl(kx), fl(vx), fl(gx[:, :, d]), fl(bx[:, :, d]))
        oc_sum = oc_sum + fl(oc)
        ox_sum = ox_sum + fl(ox)

    def finish(o, z):
        B, L = z.shape[:2]
        o = rms_norm(o, norm_g).astype(z.dtype) * jax.nn.silu(z.reshape(B, L, Hv, Dh))
        return o.reshape(B, L, Hv * Dh) @ w_out

    yx = finish(ox_sum, zx)
    yc = finish(oc_sum, zc) if with_ctx_out else None
    return yc, yx

def swiglu(h, w13, w2):
    gate, up = jnp.split(h @ w13, 2, axis=-1)
    return (jax.nn.silu(gate) * up) @ w2

def moe_swiglu(h, router, w13, w2):
    logits = (h @ router).astype(F32)
    top_val, top_idx = lax.top_k(logits, TOP_K)
    weights = jax.nn.softmax(top_val, axis=-1)
    combine = jnp.einsum('blk,blke->ble', weights,
                         jax.nn.one_hot(top_idx, N_EXPERTS, dtype=F32)).astype(h.dtype)
    out = jnp.zeros_like(h)
    for e in range(N_EXPERTS):
        out = out + combine[..., e:e + 1] * swiglu(h, w13[e], w2[e])
    return out

def channel_mixer(h, i, ffn_w13, ffn_w2, moe_router, moe_w13, moe_w2):
    if i % 2 == 0:
        return swiglu(h, ffn_w13[i // 2], ffn_w2[i // 2])
    return moe_swiglu(h, moe_router[i // 2], moe_w13[i // 2], moe_w2[i // 2])

def setup_inputs(seed: int = 0) -> dict:
    key = jax.random.key(seed)
    keys = iter(jax.random.split(key, 96))
    D = D_MODEL

    def nrm(shape, scale):
        return scale * jax.random.normal(next(keys), shape, F32)

    def gain(shape):
        return 1.0 + nrm(shape, 0.05)

    def dt_bias_init(shape):
        dt = jnp.exp(jax.random.uniform(next(keys), shape, F32, math.log(1e-3), math.log(1e-1)))
        return dt + jnp.log(-jnp.expm1(-dt))

    def a_log_init(shape):
        return jnp.log(jax.random.uniform(next(keys), shape, F32, 1.0, 16.0))

    n_dense = (DEPTH + 1) // 2
    n_moe = DEPTH // 2
    hy_rates = jnp.abs(jnp.linspace(math.log(HY_TARGET) / HY_SLOW, math.log(HY_TARGET) / HY_FAST, D, dtype=F32))
    rw_n = jnp.arange(D, dtype=F32) / (D - 1)
    rw_speed = -7.0 + 5.0 * rw_n ** (0.85 + (1.0 / (DEPTH - 1)) ** 0.5) + 0.5
    G, N = SSD_GROUPS, SSD_STATE
    ssd_in = 2 * SSD_INNER + 2 * G * N + 2 * SSD_HEADS
    qk_w, v_w = GDN_QK_HEADS * GDN_HEAD, GDN_V_HEADS * GDN_HEAD
    gdn_in = 2 * qk_w + 2 * v_w + 4 * GDN_V_HEADS
    return {
        'x': nrm((BATCH, SEQ, D), 1.0),
        'c': nrm((BATCH, D), 1.0),
        'ctx': nrm((BATCH, CTX_LEN, D), 1.0),
        'c_ctx': nrm((D,), 1.0),
        'mod_w': nrm((DEPTH, D, MOD_CHUNKS * D), 0.5 * D ** -0.5),
        'mod_b': nrm((DEPTH, MOD_CHUNKS * D), 0.02),
        'ln_g': gain((DEPTH, 2, D)),
        'ln_b': nrm((DEPTH, 2, D), 0.02),
        'hy_w_in': nrm((D, 3 * D), D ** -0.5),
        'hy_b_in': nrm((3 * D,), 0.02),
        'hy_conv_w': nrm((SHORT_CONV, 3 * D), SHORT_CONV ** -0.5),
        'hy_conv_b': nrm((3 * D,), 0.02),
        'hy_f_w1': nrm((HY_EMB, HY_FILTER_W), HY_EMB ** -0.5),
        'hy_f_b1': nrm((HY_FILTER_W,), 0.02),
        'hy_f_w2': nrm((HY_FILTER_W, HY_FILTER_W), HY_FILTER_W ** -0.5),
        'hy_f_b2': nrm((HY_FILTER_W,), 0.02),
        'hy_f_freq': gain((2, HY_FILTER_W)),
        'hy_f_w3': nrm((HY_FILTER_W, 2 * HY_ORDER * D), HY_FILTER_W ** -0.5),
        'hy_decay': hy_rates[None] * gain((2 * HY_ORDER, D)),
        'hy_skip': nrm((HY_ORDER, D), 1.0),
        'hy_w_out': nrm((D, D), BETA * D ** -0.5),
        'hy_b_out': nrm((D,), 0.02),
        'rw_mu': jax.random.uniform(next(keys), (6, D), F32, 0.0, 1.0),
        'rw_w_rkv': nrm((3, D, D), D ** -0.5),
        'rw_w0': rw_speed[None] + nrm((2, D), 0.1),
        'rw_w1': nrm((2, D, RW_DECAY_LORA), D ** -0.5),
        'rw_w2': nrm((2, RW_DECAY_LORA, D), 0.1 * RW_DECAY_LORA ** -0.5),
        'rw_a0': nrm((2, D), 0.1),
        'rw_a1': nrm((2, D, RW_AAA_LORA), D ** -0.5),
        'rw_a2': nrm((2, RW_AAA_LORA, D), 0.1 * RW_AAA_LORA ** -0.5),
        'rw_g1': nrm((D, RW_GATE_LORA), D ** -0.5),
        'rw_g2': nrm((RW_GATE_LORA, D), RW_GATE_LORA ** -0.5),
        'rw_k_k': 0.85 + nrm((D,), 0.05),
        'rw_k_a': gain((D,)),
        'rw_r_k': nrm((RW_HEADS, RW_HEAD), 0.1),
        'rw_lnx_g': gain((D,)),
        'rw_lnx_b': nrm((D,), 0.02),
        'rw_w_out': nrm((D, D), BETA * D ** -0.5),
        'ssd_w_in': nrm((D, ssd_in), D ** -0.5),
        'ssd_conv_w': nrm((SHORT_CONV, SSD_INNER + 2 * G * N), SHORT_CONV ** -0.5),
        'ssd_conv_b': nrm((SSD_INNER + 2 * G * N,), 0.02),
        'ssd_dt_bias': dt_bias_init((2, SSD_HEADS)),
        'ssd_A_log': a_log_init((2, SSD_HEADS)),
        'ssd_d_skip': gain((SSD_HEADS,)),
        'ssd_norm_g': gain((SSD_INNER,)),
        'ssd_w_out': nrm((SSD_INNER, D), BETA * SSD_INNER ** -0.5),
        'gdn_w_in': nrm((D, gdn_in), D ** -0.5),
        'gdn_conv_w': nrm((SHORT_CONV, 2 * qk_w + v_w), SHORT_CONV ** -0.5),
        'gdn_dt_bias': dt_bias_init((2, GDN_V_HEADS)),
        'gdn_A_log': a_log_init((2, GDN_V_HEADS)),
        'gdn_norm_g': gain((GDN_HEAD,)),
        'gdn_w_out': nrm((v_w, D), BETA * v_w ** -0.5),
        'ffn_w13': nrm((n_dense, D, 2 * FFN_DENSE), D ** -0.5),
        'ffn_w2': nrm((n_dense, FFN_DENSE, D), BETA * FFN_DENSE ** -0.5),
        'moe_router': nrm((n_moe, D, N_EXPERTS), D ** -0.5),
        'moe_w13': nrm((n_moe, N_EXPERTS, D, 2 * FFN_EXPERT), D ** -0.5),
        'moe_w2': nrm((n_moe, N_EXPERTS, FFN_EXPERT, D), BETA * FFN_EXPERT ** -0.5),
    }

def reference(x, c, ctx, c_ctx, mod_w, mod_b, ln_g, ln_b,
              hy_w_in, hy_b_in, hy_conv_w, hy_conv_b, hy_f_w1, hy_f_b1, hy_f_w2, hy_f_b2, hy_f_freq,
              hy_f_w3, hy_decay, hy_skip, hy_w_out, hy_b_out,
              rw_mu, rw_w_rkv, rw_w0, rw_w1, rw_w2, rw_a0, rw_a1, rw_a2, rw_g1, rw_g2, rw_k_k, rw_k_a,
              rw_r_k, rw_lnx_g, rw_lnx_b, rw_w_out,
              ssd_w_in, ssd_conv_w, ssd_conv_b, ssd_dt_bias, ssd_A_log, ssd_d_skip, ssd_norm_g, ssd_w_out,
              gdn_w_in, gdn_conv_w, gdn_dt_bias, gdn_A_log, gdn_norm_g, gdn_w_out,
              ffn_w13, ffn_w2, moe_router, moe_w13, moe_w2):
    hx, hc = x, ctx
    for i in range(DEPTH):
        last = i == DEPTH - 1
        sh1x, sc1x, g1x, sh2x, sc2x, g2x = [m[:, None, :] for m in modulation(c, mod_w[i], mod_b[i])]
        sh1c, sc1c, g1c, sh2c, sc2c, g2c = modulation(c_ctx, mod_w[i], mod_b[i])
        ux = hx * (1.0 + sc1x) + sh1x
        uc = hc * (1.0 + sc1c) + sh1c
        kind = i % N_MIXERS
        if kind == 0:
            yc, yx = hyena_mixer(uc, ux, not last, hy_w_in, hy_b_in, hy_conv_w, hy_conv_b, hy_f_w1, hy_f_b1,
                                 hy_f_w2, hy_f_b2, hy_f_freq, hy_f_w3, hy_decay, hy_skip, hy_w_out, hy_b_out)
        elif kind == 1:
            yc, yx = rwkv7_mixer(uc, ux, not last, rw_mu, rw_w_rkv, rw_w0, rw_w1, rw_w2, rw_a0, rw_a1, rw_a2,
                                 rw_g1, rw_g2, rw_k_k, rw_k_a, rw_r_k, rw_lnx_g, rw_lnx_b, rw_w_out)
        elif kind == 2:
            yc, yx = ssd_mixer(uc, raster_to_column(ux), not last, ssd_w_in, ssd_conv_w, ssd_conv_b,
                               ssd_dt_bias, ssd_A_log, ssd_d_skip, ssd_norm_g, ssd_w_out)
            yx = column_to_raster(yx)
        else:
            yc, yx = gdn_mixer(uc, raster_to_column(ux), not last, gdn_w_in, gdn_conv_w, gdn_dt_bias,
                               gdn_A_log, gdn_norm_g, gdn_w_out)
            yx = column_to_raster(yx)
        hx = layer_norm(ALPHA * hx + g1x * yx, ln_g[i, 0], ln_b[i, 0])
        fx = channel_mixer(hx * (1.0 + sc2x) + sh2x, i, ffn_w13, ffn_w2, moe_router, moe_w13, moe_w2)
        hx = layer_norm(ALPHA * hx + g2x * fx, ln_g[i, 1], ln_b[i, 1])
        if not last:
            hc = layer_norm(ALPHA * hc + g1c * yc, ln_g[i, 0], ln_b[i, 0])
            fc = channel_mixer(hc * (1.0 + sc2c) + sh2c, i, ffn_w13, ffn_w2, moe_router, moe_w13, moe_w2)
            hc = layer_norm(ALPHA * hc + g2c * fc, ln_g[i, 1], ln_b[i, 1])
    return hx


_drawn_inputs = setup_inputs


def setup_inputs(seed=0):
    import zlib

    import numpy as np

    out = dict(_drawn_inputs(seed))
    spreads = {}
    factors = {'ctx': 2.764,
     'hy_b_out': 8.0,
     'rw_w1': 8.0,
     'rw_w2': 8.0,
     'rw_a0': 8.0,
     'rw_a1': 8.0,
     'rw_a2': 8.0,
     'rw_k_k': 6.301,
     'rw_k_a': 7.407,
     'rw_lnx_g': 23.55,
     'rw_lnx_b': 52.457}
    for name, (base, spread) in spreads.items():
        noise = np.random.default_rng([zlib.crc32(name.encode()), seed]).standard_normal(out[name].shape)
        drawn = base * np.exp(spread * noise) if base else spread * noise
        out[name] = jnp.asarray(drawn.astype(out[name].dtype))
    for name, factor in factors.items():
        out[name] = (out[name] * factor).astype(out[name].dtype)
    return out
```

```python
from contextlib import ExitStack
import math

import numpy as np

import concourse.bass as bass
from concourse import mybir

F32 = mybir.dt.float32
I32 = mybir.dt.int32
U32 = mybir.dt.uint32
ALU = mybir.AluOpType
ACT = mybir.ActivationFunctionType
AXX = mybir.AxisListType.X

P = 128
D = 1024
KT = D // P
SEQ = 256
T = 2 * SEQ
NB = T // P
DEPTH = 2
ALPHA = (2 * DEPTH) ** 0.25
LN_EPS = 1e-5
HY_BANDS = 8
HY_EMB = 1 + 2 * HY_BANDS
HY_W = 64
FFN = 2816
FT = FFN // P
C = 64
HN = 64
RW_GN_EPS = 64e-5
DECAY = math.exp(-0.5)
GATE_LORA = 160
N_EXP = 8
FE = 3584
EJ = FE // 512

LEVELS = (1, 2, 4, 8, 16, 32)

RS = 2048
RN = 6
ERN = 7

ROWS = {}


def _rows():
    at = 0
    for tile, names in enumerate([
        [("mod_b0", 48), ("mod_b1", 48)],
        [("ln_g", 32), ("ln_b", 32), ("hy_b_in", 24), ("hy_conv_b", 24)],
        [("hy_conv_w", 72), ("hy_b_out", 8), ("rw_mu", 48)],
        [("rw_w0", 16), ("rw_a0", 16), ("rw_k_k", 8), ("rw_k_a", 8), ("rw_r_k", 8), ("rw_lnx_g", 8),
         ("rw_lnx_b", 8), ("c", 8), ("c_ctx", 8)],
    ]):
        at = 0
        for name, n in names:
            ROWS[name] = (tile, at, n)
            at += n
    return ROWS


_rows()
ROW_FILL = [96, 112, 128, 88]


def constants():
    f64 = np.float64
    i = np.arange(P)
    ident = np.eye(P)
    mean = np.full((P, P), 1.0 / D)
    same_head = (i[:, None] // HN == i[None, :] // HN).astype(f64)
    common = np.concatenate([ident, mean, same_head, same_head / HN, np.ones((P, P)),
                             np.tile(np.arange(N_EXP), (P, 1))], 1)

    L = SEQ
    t = np.arange(L, dtype=f64)
    w = 2 * np.pi * (np.arange(L) + 0.5) / (2 * L)
    ang = t[:, None] * w[None, :]
    fwd = np.concatenate([np.cos(ang), -np.sin(ang)], 1)
    fwd = fwd.reshape(2, P, 2 * L).transpose(1, 0, 2).reshape(P, -1)
    inv = np.concatenate([np.cos(ang).T, -np.sin(ang).T], 0) / L
    inv = inv.reshape(4, P, L).transpose(1, 0, 2).reshape(P, -1)
    t01 = np.arange(L, dtype=np.float32) / np.float32(max(L - 1, 1))
    bands = np.linspace(1e-4, HY_BANDS - 1, HY_BANDS, dtype=np.float32)
    a32 = (np.float32(2.0 * math.pi / L) * np.arange(L, dtype=np.float32)[:, None] * bands[None, :]).astype(f64)
    feats = np.zeros((P, L))
    feats[:HY_EMB] = np.concatenate([t01[:, None], np.cos(a32), -np.sin(a32)], 1).T
    negt = np.zeros((P, L))
    negt[0] = -t01
    notfirst = (i > 0).astype(f64)[:, None]
    layer0 = np.concatenate([fwd, inv, feats, negt, notfirst], 1)

    row, col = i[:, None], i[None, :]
    block = row // C == col // C
    lower, upper = block & (col < row), block & (col > row)
    strict = [lower, upper]
    incl_t = [block & (row <= col), block & (row >= col)]

    def level(b, after_rows):
        pair = row // (2 * b) == col // (2 * b)
        r2, c2 = row // b % 2, col // b % 2
        return pair & (r2 == 1) & (c2 == 0) if after_rows else pair & (r2 == 0) & (c2 == 1)

    pos = np.arange(T) % C
    reset = [np.tile(pos != 0, (P, 1)), np.tile(pos != C - 1, (P, 1))]
    layer1 = np.concatenate([*strict, *incl_t, *reset, (row[:, :] % HN == np.arange(HN)[None, :])], 1)
    bits = np.concatenate([level(b, a) for b in LEVELS for a in (True, False)], 1)
    return (common.astype(np.float32), layer0.astype(np.float32), layer1.astype(np.float32),
            bits.astype(np.int32))


PER = dict(proj=8, k_copied=1, sg=2, rate=2, r_copied=1, v_copied=1, g_copied=1, ksq=1, ksum=1, kstd=1,
           vt_full=1, vt_ready=1, decayed=2, excl=2, e_incl=2, e_inv=2, e_excl=2, kk_ready=1, b_raw=2,
           a_t=2, b_t=2, k_t=2, r_t=2, tr_full=6, q_ready=4, bk_ready=4, sc=16, sc_taken=16, t_reset=4,
           y_full=20, y_ready=20, z_full=20, merged=20, z1_full=4, z1_ready=4, wu_full=4, wu_ready=4,
           m_full=2, n_full=2, g_full=2, mo_ready=2, nd_ready=2, gt_ready=2, y_local=2, st_full=12,
           st_ready=14, out_y=1, y_copied=1, gn_mean=1, gn_cent=1, gn_sq=1, gn_var=1, gn_std=1,
           bonus_in=1, bonus_full=1, pair_done=1, kk_raw=1, rate_used=2)


DVE_LINKS = 12


GROUPS = dict(gates=("sg", "rate"), exps=("e_incl", "e_inv", "e_excl"), decayed_all=("r_t", "k_t", "b_t", "a_t"),
              chunk_full=("m_full", "n_full", "g_full", "y_local"), chunk_taken=("mo_ready", "nd_ready", "gt_ready"))
IN_GROUP = {name: (group, n, len(names)) for group, names in GROUPS.items() for n, name in enumerate(names)}


class Chain:

    def __init__(self, eng, sem):
        self.eng, self.sem, self.n, self.base, self.off = eng, sem, 0, 0, 0

    def __call__(self, ins):
        self.n += 1
        ins.then_inc(self.sem, 1)
        self.eng.wait_ge(self.sem, self.off + self.base + self.n)

    def enter(self, i, per):
        self.base, self.n, self.per, self.off = self.base + self.n, 0, per, i * per

    def leave(self, count):
        assert self.n == self.per, (self.n, self.per)
        self.base, self.n, self.off = self.base + count * self.per, 0, 0


class Ring:

    def __init__(self, eng, loaded):
        self.eng, self.loaded, self.n, self.it16, self.free = eng, loaded, 0, 0, {}

    def slot_to_load(self, done):
        slot, self.n = self.n % RN, self.n + 1
        if slot in self.free:
            self.eng.wait_ge(*self.free[slot])
        self.free[slot] = done
        return slot

    def loaded_slot(self):
        n, self.n = self.n, self.n + 1
        self.eng.wait_ge(self.loaded[n % RN], self.it16 + 16 * (n // RN + 1))
        return n % RN

    def load_loop(self, chunks, done, body):
        rounds = chunks // RN
        start = self.n
        for c in range(RN):
            body(c, self.slot_to_load(done(c)))
        with self.eng.Fori(1, rounds) as i:
            for j in range(RN):
                self.eng.wait_ge(*done((i - 1) * RN + j))
                body(i * RN + j, (start + j) % RN)
        for j in range(RN):
            self.free[(start + j) % RN] = done((rounds - 1) * RN + j)
        self.n = start + rounds * RN
        for c in range(rounds * RN, chunks):
            body(c, self.slot_to_load(done(c)))

    def read_loop(self, chunks, body):
        rounds, start = chunks // RN, self.n
        with self.eng.Fori(0, rounds) as i:
            self.it16 = i * 16
            for j in range(RN):
                body(i * RN + j)
        self.it16, self.n = 0, start + rounds * RN
        for c in range(rounds * RN, chunks):
            body(c)


def with_loop(eng, n, body):
    rounds, rest = divmod(n, RN)
    with eng.Fori(0, rounds) as i:
        for j in range(RN):
            body(i * RN + j, j)
    for j in range(rest):
        body(rounds * RN + j, j)


def build(nc, a, out, consts, upto=99, dump=None):
    ctx = ExitStack()
    with ctx, nc.allow_non_contiguous_dma(reason="a few short columns"):
        sems = {}

        def sem(name):
            name = IN_GROUP.get(name, (name,))[0]
            if name not in sems:
                sems[name] = ctx.enter_context(nc.semaphore(name))
            return sems[name]

        arena = ctx.enter_context(nc.sbuf_tensor("arena", [P, 53000], F32))
        bank = [ctx.enter_context(nc.psum_tensor(f"bank{i}", [P, 512], F32)) for i in range(8)]
        at = [0]

        def mark(n=None):
            if n is not None:
                at[0] = n
            return at[0]

        def sb(*shape):
            n = int(np.prod(shape))
            v = arena[:, at[0]:at[0] + n]
            at[0] += n
            assert at[0] <= 53000, at[0]
            if len(shape) == 2:
                v = v.rearrange("p (a b) -> p a b", b=shape[1])
            if len(shape) == 3:
                v = v.rearrange("p (a b c) -> p a b c", b=shape[1], c=shape[2])
            return v

        common = sb(5 * P + N_EXP)
        expert_no = common[:, 5 * P:5 * P + N_EXP]
        ident, meanm, heads1, heads64, ones = (common[:, P * j:P * (j + 1)] for j in range(5))
        vec = sb(4 * P)
        modv = [sb(48, 2), sb(48, 2)]
        silu_c = sb(KT, 2)
        eps = sb(4)
        XT = sb(KT, T)
        table = mark()
        sb(3400)
        UT = sb(KT, T)
        ring_at = mark()
        ring = [sb(RS) for _ in range(RN)]
        work = mark()

        mark(table)
        fwd, inv = sb(2, T), sb(4, SEQ)
        feats, negt, notfirst = sb(SEQ), sb(SEQ), sb(1)
        hw1, hw2, hcol = sb(HY_W), sb(HY_W), sb(4)
        mark(work)
        X1, X2 = sb(KT, T), sb(KT, T)
        ZT = sb(NB, D)
        KSP = sb(8, D)
        tmp_at = mark()
        pad = [sb(2, SEQ + 2) for _ in range(2)]
        cv = [sb(T) for _ in range(2)]
        pr = [sb(T) for _ in range(4)]
        win = [sb(T) for _ in range(2)]
        gate_t = sb(T)
        cv_spare = sb(T)
        dec = KSP[:, 4:8, :].rearrange("p a b -> p (a b)")
        rows = KSP[:, 0:1, 0:512].rearrange("p a (r c) -> p (a r) c", c=P)
        xin = X2.rearrange("p a b -> p (a b)").rearrange("p (a b) -> p a b", b=D)
        skip = X1.rearrange("p a b -> p (a b)")[:, 0:2 * D]
        hargs = [X1[:, 4 + j, 0:SEQ] for j in range(4)]
        w3 = ZT.rearrange("p a b -> p (a b)")
        kcs = UT.rearrange("p a b -> p (a b)").rearrange("p (s t d) -> p s t d", s=2, t=2)
        Y = UT.rearrange("p a b -> p (a b)").rearrange("p (s f d) -> p s f d", s=2, f=4)
        mod_rows0 = X1.rearrange("p a b -> p (a b)")
        mod_rows0 = arena[:, work:work + 6 * D]
        mark(work)
        Hf = sb(FT * T)
        H = Hf.rearrange("p (f t) -> p f t", t=T)
        SQ = sb(KT, T)
        sil = [sb(T), sb(T)]
        rt = [sb(T), sb(T)]
        std, rstd = sb(T), sb(T)
        mod_rows1 = sb(6 * D)

        mark(table)
        strict, incl_t = [sb(P), sb(P)], [sb(P), sb(P)]
        reset = [sb(T), sb(T)]
        eye64 = sb(HN)
        bits = [[sb(P).bitcast(I32) for _ in range(2)] for _ in LEVELS]
        bits_at = mark() - len(LEVELS) * 2 * P
        mark(work)
        UP = sb(KT, 2, SEQ + 2)
        XX, XM = sb(KT, T), sb(KT, T)
        pair_end = mark()
        XK, XV, XR = sb(KT, T), sb(KT, T), sb(KT, SEQ)
        HW, HA, G1a, G1b = sb(T), sb(T), sb(SEQ), sb(SEQ)
        YT = sb(KT, SEQ)
        mark(ring_at)
        lw1, la1, lg1 = sb(KT, P), sb(KT, P), sb(KT, GATE_LORA)

        mark(table + 3400)
        wst = sb(3, KT, P)
        w2s, a2s, g2a, g2b = sb(P), sb(P), sb(P), sb(P)
        one_ka = sb(KT)
        mark(ring_at)
        Kf, KK, KS, Vf, Vt, Rf, Gf = sb(T), sb(T), sb(T), sb(T), sb(NB, P), sb(SEQ), sb(SEQ)
        At, Bt, Kt = ([sb(T), sb(T)] for _ in range(3))
        Rt = [sb(SEQ), sb(SEQ)]
        DC, KD = [sb(8), sb(8)], sb(SEQ)
        SG, AS = [sb(T), sb(T)], [sb(T), sb(T)]
        CS, EP, EN, EX = sb(T), sb(T), sb(T), sb(T)
        Btok, Ktok = sb(NB, P), sb(NB, P)
        Aab = [sb(NB, P) for _ in range(2)]
        AakT = [sb(NB, P) for _ in range(2)]
        ARR = [sb(NB, P) for _ in range(2)]
        TM = [sb(NB, P) for _ in range(2)]
        TT = [sb(NB, P) for _ in range(2)]
        Yb = [sb(NB, P) for _ in range(2)]
        Q = [sb(NB, P) for _ in range(2)]
        WU = TM
        MO, ND = [sb(8, C) for _ in range(2)], [sb(8, C) for _ in range(2)]
        GT = [sb(SEQ) for _ in range(2)]
        ST = [sb(8, C) for _ in range(2)]
        YF, YS, YN = sb(SEQ), sb(SEQ), sb(SEQ)
        assert mark() <= pair_end, (mark(), pair_end)

        mark(table)
        XTOK = sb(2, D)
        rt_w, logit, mx, ixf, comb = sb(KT, N_EXP), sb(2, 8), sb(2, 8), sb(2, 8), sb(2, 8)
        ix = sb(16).bitcast(U32)
        hot = sb(2, 8)
        w12 = sb(2, 4)
        stat = sb(2, 4)
        diag = [sb(P), sb(P)]
        mark(ring_at)
        ering = [sb(KT, 512) for _ in range(ERN)]
        OUT = sb(2, D)
        HT = [sb(4, SEQ), sb(4, SEQ)]
        sil2 = [sb(SEQ), sb(SEQ)]
        rowG, rowg, rowb = sb(D), sb(D), sb(D)
        assert mark() <= 53000

        def col(name, j):
            tile, first, n = ROWS[name]
            assert j < n
            return vec[:, tile * P + first + j:tile * P + first + j + 1]

        def mv(layer, chunk, k, s):
            return modv[layer][:, chunk * KT + k, 1 - s:2 - s]

        ring_start = [0, 24 + 16 + FT + 16]
        ffn_start = 24 + 16
        win_f = [gate_t, cv_spare]

        seg = [slice(0, SEQ), slice(SEQ, T)]

        def dcol(name, i):
            tile, first, n = ROWS[name]
            return vec[:, bass.ds(tile * P + first + i, 1)]

        def each4(m):
            return m.unsqueeze(1).to_broadcast([P, 4, P])

        def b4(b):
            return bank[b][:, :].rearrange("p (b c) -> p b c", b=4)

        def c4(b):
            return bank[b][:, 0:4 * C].rearrange("p (b c) -> p b c", b=4)

        def hd(h):
            return slice(HN * h, HN * h + HN)

        def waiter(eng, i):
            def w(name, c):
                if name in IN_GROUP:
                    _, n, size = IN_GROUP[name]
                    eng.wait_ge(sem(name), i * 2 * size + (c - 1) * size + n + 1)
                else:
                    eng.wait_ge(sem(name), i * PER[name] + c)
            return w

        def settle(eng):
            eng.sem_inc(sem("settled"), 1)

        def read_last(q, e):
            j, r = divmod(q, 3)
            return (sem("y_done"), 7 * e + j + 3) if r == 2 else (sem("gu_full"), 28 * e + 4 * j + 4)

        CHUNKS = [[0, 1, 2, 3, 4, 5, 6, 7], [3, 2, 1, 0, 7, 6, 5, 4]]

        block = ctx.enter_context(nc.Block())
        w_loaded = [sem(f"w_loaded{i}") for i in range(RN)]
        up_loaded = [sem(f"up_loaded{i}") for i in range(RN)]

        @block.sync
        def _(sp):
            ld = Ring(sp, w_loaded)

            def load(name, dst, src, n=16):
                sp.dma_start(dst, src).then_inc(sem(name), 16)

            load("ld_common", common, consts[0])
            for name in ROWS:
                tile, first, n = ROWS[name]
                src = {"mod_b0": a["mod_b"][0:1], "mod_b1": a["mod_b"][1:2], "c_ctx": a["c_ctx"],
                       "c": a["c"]}.get(name, a.get(name))
                flat = src
                if len(src.shape) == 2:
                    flat = src.rearrange("a b -> (a b)")
                if len(src.shape) == 3:
                    flat = src.rearrange("a b c -> (a b c)")
                load("ld_rows", rows[first:first + n, tile, :], flat.rearrange("(r p) -> r p", p=P))
            load("ld_x", xin[:, 0:2, :], a["ctx"][0].rearrange("(t p) d -> p t d", p=P))
            load("ld_x", xin[:, 2:4, :], a["x"][0].rearrange("(t p) d -> p t d", p=P))
            load("ld_table", arena[:, table:table + 2 * T + 4 * SEQ + 2 * SEQ + 1], consts[1])
            load("ld_filter", hw1[0:HY_EMB, :], a["hy_f_w1"])
            load("ld_filter", hw2[0:HY_W, :], a["hy_f_w2"])
            for j, s in enumerate([a["hy_f_b1"], a["hy_f_b2"], a["hy_f_freq"][0], a["hy_f_freq"][1]]):
                load("ld_filter", hcol[0:HY_W, j:j + 1], s.rearrange("(p o) -> p o", o=1))
            load("ld_filter", w3[0:HY_W, :], a["hy_f_w3"])
            load("ld_filter", dec[0:1, :], a["hy_decay"].rearrange("a (o b) -> o (a b)", o=1))
            load("ld_filter", skip[0:1, :], a["hy_skip"].rearrange("a (o b) -> o (a b)", o=1))

            def load_mod(layer):
                w = a["mod_w"][layer].rearrange("(k p) n -> p k n", p=P)
                ld.load_loop(24, lambda c: (sem("mod_full"), c + 1 + 24 * layer),
                             lambda c, s: sp.dma_start(ring[s].rearrange("p (k n) -> p k n", n=256),
                                                       w[:, :, bass.ds(c * 256, 256)]).then_inc(w_loaded[s], 16))

            def load_cols(w, n, name, first=0):
                w = w.rearrange("(k p) n -> p k n", p=P)
                for c in range(n):
                    s = ld.slot_to_load((sem(name), first + 2 * c + 2))
                    sp.dma_start(ring[s].rearrange("p (k n) -> p k n", n=256), w[:, :, c * 256:(c + 1) * 256])\
                        .then_inc(w_loaded[s], 16)

            load_mod(0)
            if upto >= 2:
                load_cols(a["hy_w_in"], 12, "proj_full")
                load_cols(a["hy_w_out"], 4, "out_full")
            if upto >= 3:
                w13 = a["ffn_w13"][0].rearrange("(k p) (h n) -> p k h n", p=P, h=2)

                def load13(f, s):
                    dst = ring[s].rearrange("p (h k n) -> p h k n", h=2, n=P)
                    sp.dma_start(dst[:, 0], w13[:, :, 0, bass.ds(f * P, P)]).then_inc(w_loaded[s], 16)
                    sp.dma_start(dst[:, 1], w13[:, :, 1, bass.ds(f * P, P)]).then_inc(up_loaded[s], 16)
                ld.load_loop(FT, lambda f: (sem("hidden_full"), f + 1), load13)
                w2 = a["ffn_w2"][0].rearrange("(g k p) n -> p g k n", p=P, g=2)
                for m in range(KT):
                    for g in range(2):
                        s = ld.slot_to_load((sem("out_full"), 8 + m + 1))
                        sp.dma_start(ring[s][:, 0:11 * P].rearrange("p (k n) -> p k n", n=P),
                                     w2[:, g, :, m * P:(m + 1) * P]).then_inc(w_loaded[s], 16)
                load_mod(1)
            if upto >= 4:
                sp.wait_ge(sem("long_taken"), 32)
                load("ld_table1", arena[:, table:table + 4 * P + 2 * T + HN], consts[2])
                load("ld_table1", arena[:, bits_at:bits_at + len(LEVELS) * 2 * P].bitcast(I32), consts[3])
                sp.wait_ge(sem("mod_full"), 48)
                for d in range(2):
                    load("ld_lora", lw1[:, :, d * HN:(d + 1) * HN], a["rw_w1"][d].rearrange("(k p) n -> p k n", p=P))
                    load("ld_lora", la1[:, :, d * HN:(d + 1) * HN], a["rw_a1"][d].rearrange("(k p) n -> p k n", p=P))
                load("ld_lora", lg1, a["rw_g1"].rearrange("(k p) n -> p k n", p=P))
            if upto >= 5:
                wr = a["rw_w_rkv"].rearrange("j (k p) n -> p (j k) n", p=P)
                w2d = a["rw_w2"].rearrange("d r n -> (d r) n")
                a2d = a["rw_a2"].rearrange("d r n -> (d r) n")
                sp.wait_ge(sem("hidden_full"), FT)
                with sp.Fori(0, KT) as i:
                    sp.wait_ge(sem("stage_free"), i + 1)
                    cols = bass.ds(i * P, P)
                    sp.dma_start(wst.rearrange("p j k n -> p (j k) n"), wr[:, :, cols]).then_inc(sem("ld_pair"), 16)
                    sp.dma_start(w2s, w2d[:, cols]).then_inc(sem("ld_pair"), 16)
                    sp.dma_start(a2s, a2d[:, cols]).then_inc(sem("ld_pair"), 16)
                    sp.dma_start(g2a, a["rw_g2"][0:P, cols]).then_inc(sem("ld_pair"), 16)
                    sp.dma_start(g2b[0:GATE_LORA - P, :], a["rw_g2"][P:GATE_LORA, cols]).then_inc(sem("ld_pair"), 16)
            if upto >= 6:
                sp.wait_ge(sem("pair_done"), KT + 1)
                ld.free = {}
                load_cols(a["rw_w_out"], 4, "out_full", 16)
            if upto >= 7:
                sp.wait_ge(sem("out_full"), 24)
                load("ld_router", rt_w, a["moe_router"][0].rearrange("(k p) e -> p k e", p=P))
                w13 = a["moe_w13"][0].rearrange("e (k p) n -> p (e k) n", p=P)
                w2 = a["moe_w2"][0].rearrange("e (k p) n -> p (e k) n", p=P)
                sp.wait_ge(sem("ln_done"), 24)
                sp.wait_ge(sem("u_ready"), 3)

                def load_expert(e, first):
                    for q in range(21):
                        j, r = divmod(q, 3)
                        if q >= ERN:
                            sp.wait_ge(*read_last(q - ERN, e))
                        elif not first:
                            sp.wait_ge(*read_last(q - ERN + 21, e - 1))
                        if r < 2:
                            src = w13[:, bass.ds(e * KT, KT), r * FE + j * 512:r * FE + j * 512 + 512]
                            dst = ering[q % ERN]
                        else:
                            src = w2[:, bass.ds(e * (FE // P) + 4 * j, 4), :]
                            dst = ering[q % ERN].rearrange("p a b -> p (a b)").rearrange("p (a b) -> p a b", b=D)
                        sp.dma_start(dst, src).then_inc(sem(f"ew_loaded{q % ERN}"), 16)
                load_expert(0, True)
                with sp.Fori(1, N_EXP) as e:
                    load_expert(e, False)
                for tt in range(2):
                    sp.wait_ge(sem("final"), tt + 1)
                    sp.dma_start(out[0, tt * P:(tt + 1) * P, :], OUT[:, tt, :]).then_inc(sem("stored"), 16)
                sp.wait_ge(sem("stored"), 32)
        @block.tensor
        def _(pe):
            rg = Ring(pe, w_loaded)
            pe.wait_ge(sem("ld_common"), 16)
            pe.wait_ge(sem("ld_rows"), 16 * len(ROWS))
            for j, n in enumerate(ROW_FILL):
                last = pe.transpose(bank[0][:, j * P:j * P + n], rows[0:n, j, :], ident[0:n, 0:n])
            last.then_inc(sem("rows_turned"), 1)
            pe.wait_ge(sem("ld_x"), 32)
            for k in range(KT):
                if k >= 4:
                    pe.wait_ge(sem("x_taken"), k - 3)
                for t in range(NB):
                    last = pe.transpose(bank[1 + k % 4][:, t * P:(t + 1) * P], xin[:, t, k * P:(k + 1) * P], ident)
                last.then_inc(sem("x_turned"), 1)

            pe.wait_ge(sem("ld_table"), 16)
            pe.wait_ge(sem("ld_filter"), 16 * 9)
            pe.matmul(bank[5][0:HY_W, 0:SEQ], hw1[0:HY_EMB, :], feats[0:HY_EMB, :], start=True, stop=True)\
                .then_inc(sem("sine_in"), 1)
            pe.wait_ge(sem("sine_out"), 1)
            pe.matmul(bank[6][0:HY_W, 0:SEQ], hw2[0:HY_W, :], hargs[2][0:HY_W, :], start=True, stop=True)\
                .then_inc(sem("sine_in"), 1)
            pe.wait_ge(sem("sine_out"), 2)
            pe.wait_ge(sem("decay_abs"), 1)
            pe.wait_ge(sem("x_taken"), 8)
            pe.wait_ge(sem("vec_ready"), 1)
            for n in range(2):
                for q in range(4):
                    g = 4 * n + q
                    half, tt = q // 2, q % 2
                    b = 4 * (g % 2)
                    if g >= 2:
                        pe.wait_ge(sem("filter_taken"), g - 1)
                    if g == 4:
                        pe.wait_ge(sem("spectrum_taken"), 8)
                    for j in range(2):
                        cs = slice((2 * n + j) * D + half * 512, (2 * n + j) * D + half * 512 + 512)
                        pe.matmul(bank[b + j][:, :], hargs[3][0:HY_W, tt * P:(tt + 1) * P], w3[0:HY_W, cs],
                                  start=True, stop=True)
                        last = pe.matmul(bank[b + 2 + j][:, :], negt[0:1, tt * P:(tt + 1) * P], dec[0:1, cs],
                                         start=True, stop=True)
                    last.then_inc(sem("filter_full"), 1)
                pe.wait_ge(sem("pool_taps"), 4 * (n + 1))
                pe.wait_ge(sem("taps_ready"), 4 * (n + 1))
                for o in range(8):
                    c, f, half = o // 4, o // 2 % 2, o % 2
                    for tt in range(2):
                        last = pe.matmul(bank[o][:, :], fwd[:, tt, c * SEQ + f * P:c * SEQ + (f + 1) * P],
                                         kcs[:, c, tt, half * 512:half * 512 + 512], start=(tt == 0), stop=(tt == 1))
                    last.then_inc(sem("spectrum_full"), 1)

            def modulation(layer):
                dst = [mod_rows0, mod_rows1][layer]
                pe.wait_ge(sem("silu_ready"), 1)
                if layer == 0:
                    pe.wait_ge(sem("spectrum_taken"), 16)
                base = 25 * layer

                def body(c):
                    s = rg.loaded_slot()
                    pe.wait_ge(sem("mod_taken"), c + 1 + 30 * layer)
                    w = ring[s].rearrange("p (k n) -> p k n", n=256)
                    for k in range(KT):
                        last = pe.matmul(bank[s][0:2, 0:256], silu_c[:, k, :], w[:, k, :], start=(k == 0),
                                         stop=(k == KT - 1))
                    last.then_inc(sem("mod_full"), 1)
                rg.read_loop(24, body)
                pe.wait_ge(sem("mod_taken"), 30 * (layer + 1))
                for j in range(48):
                    last = pe.transpose(bank[6][:, 2 * j:2 * j + 2], dst[0:2, j * P:(j + 1) * P], ident[0:2, 0:2])
                last.then_inc(sem("mod_turned"), 1)

            modulation(0)

            def layer_norm(n, width=T):
                cols = slice(T - width, T)
                pe.wait_ge(sem("residual_done"), 8 * n)
                for k in range(KT):
                    last = pe.matmul(bank[0][:, 0:width], meanm, XT[:, k, cols], start=(k == 0), stop=(k == KT - 1))
                last.then_inc(sem("ln_mean"), 1)
                for k in range(KT):
                    pe.wait_ge(sem("ln_square"), 8 * (n - 1) + k + 1)
                    last = pe.matmul(bank[1][:, 0:width], meanm, SQ[:, k, 0:width], start=(k == 0), stop=(k == KT - 1))
                last.then_inc(sem("ln_var"), 1)

            if upto >= 2:
                pe.wait_ge(sem("u_ready"), 1)

                def turn_v(m):
                    pe.wait_ge(sem("conv_done"), m + 1)
                    if m >= 2:
                        pe.wait_ge(sem("v_taken"), m - 1)
                    for t in range(NB):
                        last = pe.transpose(bank[4 + m % 2][:, t * P:(t + 1) * P], cv[m % 2][:, t * P:(t + 1) * P], ident)
                    last.then_inc(sem("v_turned"), 1)

                for m in range(24):
                    if m % 2 == 0:
                        s = rg.loaded_slot()
                    if m >= 4:
                        pe.wait_ge(sem("proj_taken"), m - 3)
                    w = ring[s].rearrange("p (k n) -> p k n", n=256)[:, :, (m % 2) * P:(m % 2 + 1) * P]
                    for k in range(KT):
                        last = pe.matmul(bank[m % 4][:, :], w[:, k, :], UT[:, k, :], start=(k == 0), stop=(k == KT - 1))
                    last.then_inc(sem("proj_full"), 1)
                    if 1 <= m <= KT:
                        turn_v(m - 1)
                for n in range(2):
                    X = [X1, X2][n]
                    if n == 0:
                        pe.wait_ge(sem("v_taken"), 8)
                        pe.wait_ge(sem("conv_done"), 24)
                    else:
                        for k in range(KT):
                            if k >= 4:
                                pe.wait_ge(sem("z_taken"), k - 3)
                            for t in range(NB):
                                last = pe.transpose(bank[k % 4][:, t * P:(t + 1) * P], X1[:, k, t * P:(t + 1) * P], ident)
                            last.then_inc(sem("z_turned"), 1)
                        pe.wait_ge(sem("z_taken"), 8)
                    def forward(g):
                        half, s = g // 2, g % 2
                        if g + 4 * n >= 1:
                            pe.wait_ge(sem("bins_taken"), g + 4 * n)
                        for f in range(4):
                            for tt in range(2):
                                last = pe.matmul(bank[f][:, :], fwd[:, tt, f * P:(f + 1) * P],
                                                 ZT[:, 2 * s + tt, half * 512:half * 512 + 512],
                                                 start=(tt == 0), stop=(tt == 1))
                        last.then_inc(sem("bins_full"), 1)

                    def inverse(g):
                        half, s = g // 2, g % 2
                        pe.wait_ge(sem("product_ready"), 4 * n + g + 1)
                        for ct in range(4):
                            if 16 * n + 4 * g + ct >= 4:
                                pe.wait_ge(sem("long_taken"), 16 * n + 4 * g + ct - 3)
                            for f in range(4):
                                last = pe.matmul(bank[4 + ct][:, 0:SEQ], Y[:, g % 2, f, ct * P:(ct + 1) * P],
                                                 inv[:, f, :], start=(f == 0), stop=(f == 3))
                            last.then_inc(sem("long_full"), 1)

                    for g in range(5):
                        if g < 4:
                            forward(g)
                        if g >= 1:
                            inverse(g - 1)
                    pe.wait_ge(sem("long_taken"), 16 * (n + 1))
                for m in range(KT):
                    if m % 2 == 0:
                        s = rg.loaded_slot()
                    if m >= 4:
                        pe.wait_ge(sem("residual_done"), m - 3)
                    w = ring[s].rearrange("p (k n) -> p k n", n=256)[:, :, (m % 2) * P:(m % 2 + 1) * P]
                    for k in range(KT):
                        last = pe.matmul(bank[m % 4][:, :], w[:, k, :], X2[:, k, :], start=(k == 0), stop=(k == KT - 1))
                    last.then_inc(sem("out_full"), 1)
                layer_norm(1)
            if upto >= 3:
                pe.wait_ge(sem("u_ready"), 2)

                def hidden(f):
                    s = rg.loaded_slot()
                    b = 2 * (s % 2)
                    pe.wait_ge(up_loaded[s], rg.it16 + 16 * ((rg.n - 1 - ffn_start) // RN + 1))
                    pe.wait_ge(sem("hidden_taken"), f + 1)
                    w = ring[s].rearrange("p (h k n) -> p h k n", h=2, n=P)
                    for h in range(2):
                        for k in range(KT):
                            last = pe.matmul(bank[b + h][:, :], w[:, h, k, :], UT[:, k, :], start=(k == 0),
                                             stop=(k == KT - 1))
                    last.then_inc(sem("hidden_full"), 1)
                rg.read_loop(FT, hidden)
                pe.wait_ge(sem("hidden_taken"), FT + 2)
                for m in range(KT):
                    if m >= 4:
                        pe.wait_ge(sem("residual_done"), 8 + m - 3)
                    for g in range(2):
                        s = rg.loaded_slot()
                        w = ring[s][:, 0:11 * P].rearrange("p (k n) -> p k n", n=P)
                        for k in range(11):
                            last = pe.matmul(bank[4 + m % 4][:, :], w[:, k, :], H[:, 11 * g + k, :],
                                             start=(g + k == 0), stop=(g == 1 and k == 10))
                    last.then_inc(sem("out_full"), 1)
                pe.wait_ge(sem("residual_done"), 16)
                modulation(1)
                layer_norm(2)
            if upto >= 4:
                pe.wait_ge(sem("ld_lora"), 16 * 5)
                pe.wait_ge(sem("xm_ready"), 1)
                for k in range(KT):
                    last = pe.matmul(bank[0][:, :], lw1[:, k, :], XM[:, k, :], start=(k == 0), stop=(k == KT - 1))
                last.then_inc(sem("lora_full"), 1)
                pe.wait_ge(sem("xm_ready"), 2)
                for k in range(KT):
                    last = pe.matmul(bank[1][:, :], la1[:, k, :], XM[:, k, :], start=(k == 0), stop=(k == KT - 1))
                last.then_inc(sem("lora_full"), 1)
                pe.wait_ge(sem("xm_ready"), 3)
                for r0, r1 in ((0, P), (P, GATE_LORA)):
                    b = bank[2 + r0 // P]
                    for k in range(KT):
                        last = pe.matmul(b[0:r1 - r0, 0:SEQ], lg1[:, k, r0:r1], XM[:, k, 0:SEQ], start=(k == 0),
                                         stop=(k == KT - 1))
                last.then_inc(sem("lora_full"), 1)
            if upto >= 5:
                pe.sem_inc(sem("stage_free"), 1)
                pe.wait_ge(sem("lora_taken"), 4)
                pe.wait_ge(sem("ld_table1"), 32)
                with pe.Fori(0, KT) as i:
                    w = waiter(pe, i)
                    mm = pe.matmul
                    pe.wait_ge(sem("ld_pair"), i * 80 + 80)
                    w("pair_done", 1)
                    for k in range(KT):
                        last = mm(bank[0][:, :], wst[:, 1, k, :], XK[:, k, :], start=(k == 0), stop=(k == KT - 1))
                    last.then_inc(sem("proj"), 1)
                    for d in range(2):
                        r = hd(d)
                        mm(bank[3 + d][:, :], w2s[r, :], HW[r, :], start=True, stop=True).then_inc(sem("proj"), 1)
                        mm(bank[5 + d][:, :], a2s[r, :], HA[r, :], start=True, stop=True).then_inc(sem("proj"), 1)
                    for k in range(KT):
                        last = mm(bank[2][:, 0:SEQ], wst[:, 0, k, :], XR[:, k, :], start=(k == 0), stop=(k == KT - 1))
                    last.then_inc(sem("proj"), 1)
                    for k in range(KT):
                        last = mm(bank[1][:, :], wst[:, 2, k, :], XV[:, k, :], start=(k == 0), stop=(k == KT - 1))
                    last.then_inc(sem("proj"), 1)
                    mm(bank[7][:, 0:SEQ], g2a, G1a, start=True, stop=False)
                    mm(bank[7][:, 0:SEQ], g2b[0:32, :], G1b[0:32, :], start=False, stop=True).then_inc(sem("proj"), 1)
                    w("k_copied", 1)
                    w("ksq", 1)
                    mm(bank[0][:, :], heads1, KS, start=True, stop=True).then_inc(sem("ksum"), 1)
                    w("v_copied", 1)
                    for b in range(NB):
                        last = pe.transpose(bank[1][:, b * P:(b + 1) * P], Vf[:, b * P:(b + 1) * P], ident)
                    last.then_inc(sem("vt_full"), 1)
                    pe.wait_ge(sem("proj"), i * 8 + 8)
                    pe.sem_inc(sem("stage_free"), 1)
                    w("sg", 2)
                    w("rate", 2)
                    w("r_copied", 1)
                    w("g_copied", 1)
                    w("vt_ready", 1)
                    w("kstd", 1)
                    for d in range(2):
                        for j, (src, name) in enumerate(((At, "a_t"), (Bt, "b_t"), (Kt, "k_t"))):
                            w(name, d + 1)
                            if d == 1:
                                (w("z1_ready", 2), w("wu_ready", 2), w("mo_ready", 1), w("nd_ready", 1), w("gt_ready", 1))
                            for b in range(NB):
                                last = pe.transpose(bank[2 + j][:, b * P:(b + 1) * P], src[d][:, b * P:(b + 1) * P], ident)
                            last.then_inc(sem("tr_full"), 1)
                        w("r_t", d + 1)
                        for h in range(2):
                            r = hd(h)
                            if h == 1:
                                w("q_ready", 2 * d + 2)
                                w("bk_ready", 2 * d + 2)
                            where = [(0, 1, 5, 6), (2, 3, 4, 0)][h]
                            for kind in range(4):
                                if h == 1 and kind == 3:
                                    w("sc_taken", 8 * d + 1)
                                ps = bank[where[kind]]
                                for b in range(NB):
                                    cs = slice(b * P, b * P + P)
                                    rs = slice((b % 2) * P, (b % 2) * P + P)
                                    if kind == 0:
                                        lhs, rhs = At[d][r, cs], Bt[d][r, cs]
                                    elif kind == 1:
                                        lhs, rhs = Bt[d][r, cs], At[d][r, cs]
                                    elif kind == 2:
                                        lhs, rhs = Kt[d][r, cs], At[d][r, cs]
                                    else:
                                        src = (Bt, Kt)[b // 2][d]
                                        lhs, rhs = src[r, SEQ + rs.start:SEQ + rs.stop], Rt[d][r, rs]
                                    last = mm(ps[:, cs], lhs, rhs, start=True, stop=True)
                                last.then_inc(sem("sc"), 1)
                        for lv in range(1, len(LEVELS)):
                            n0 = 10 * d + 2 * (lv - 1)
                            for h in range(2):
                                if lv == 1:
                                    w("sc_taken", 8 * d + 8)
                                else:
                                    w("merged", n0 + h - 1)
                                for b in range(NB):
                                    last = mm(bank[h][:, b * P:b * P + P], Aab[h][:, b, :], TT[h][:, b, :],
                                              start=True, stop=True)
                                last.then_inc(sem("y_full"), 1)
                            for h in range(2):
                                w("y_ready", n0 + h + 1)
                                if lv < len(LEVELS) - 1:
                                    for b in range(NB):
                                        mm(bank[2 + h][:, b * P:b * P + P], Yb[h][:, b, :], TM[h][:, b, :],
                                           start=True, stop=True)
                                for b in range(NB):
                                    last = mm(bank[4 + h][:, b * P:b * P + P], TM[h][:, b, :], Yb[h][:, b, :],
                                              start=True, stop=True)
                                last.then_inc(sem("z_full"), 1)
                        for h in range(2):
                            w("merged", 10 * d + 9 + h)
                            for b in range(NB):
                                last = mm(bank[h][:, b * C:b * C + C], AakT[h][:, b, :], Vt[:, b, hd(h)],
                                          start=True, stop=True)
                            last.then_inc(sem("z1_full"), 1)
                        for h in range(2):
                            w("z1_ready", 2 * d + h + 1)
                            for b in range(NB):
                                last = mm(bank[2 + h][:, b * P:b * P + P], TT[h][:, b, :], Q[h][:, b, :],
                                          start=True, stop=True)
                            last.then_inc(sem("wu_full"), 1)
                        w("wu_ready", 2 * d + 2)
                        settle(pe)
                        for h in range(2):
                            for c in range(8):
                                b, r = c // 2, hd(c % 2)
                                last = mm(bank[4 + c % 2][hd(h), b * C:b * C + C], WU[h][r, b, 0:C], Btok[r, b, hd(h)],
                                          start=True, stop=True)
                        last.then_inc(sem("m_full"), 1)
                        for h in range(2):
                            for c in range(8):
                                b, r = c // 2, hd(c % 2)
                                mm(bank[c % 2][hd(h), b * C:b * C + C], Ktok[r, b, hd(h)], Vt[r, b, hd(h)],
                                   start=True, stop=False, skip_group_check=True)
                                last = mm(bank[c % 2][hd(h), b * C:b * C + C], Btok[r, b, hd(h)], WU[h][r, b, C:P],
                                          start=False, stop=True, skip_group_check=True)
                        last.then_inc(sem("n_full"), 1)
                        for h in range(2):
                            for b in range(2):
                                last = mm(bank[6][hd(h), b * P:b * P + P], WU[h][:, 2 + b, 0:C], ARR[h][:, b, :],
                                          start=True, stop=True)
                        last.then_inc(sem("g_full"), 1)
                        for h in range(2):
                            for b in range(2):
                                mm(bank[7][hd(h), b * P:b * P + P], Vt[:, 2 + b, hd(h)], ARR[h][:, 2 + b, :],
                                   start=(d == 0 and b == 0), stop=False, skip_group_check=True)
                                last = mm(bank[7][hd(h), b * P:b * P + P], WU[h][:, 2 + b, C:P], ARR[h][:, b, :],
                                          start=False, stop=False, skip_group_check=True)
                        last.then_inc(sem("y_local"), 1)
                    w("mo_ready", 2)
                    for st in range(1, 8):
                        for d in range(2):
                            c = CHUNKS[d][st]
                            w("st_ready", 2 * (st - 1) + d + 1)
                            settle(pe)
                            if st < 7:
                                for h in range(2):
                                    last = mm(bank[d][hd(h), 0:C], MO[d][hd(h), c, :], ST[d][hd(h), st, :],
                                              start=True, stop=True)
                                last.then_inc(sem("st_full"), 1)
                            if st >= 4:
                                if st == 4 and d == 0:
                                    w("gt_ready", 2)
                                    settle(pe)
                                x = (c - 4) * C
                                for h in range(2):
                                    last = mm(bank[7][hd(h), x:x + C], ST[d][hd(h), st, :], GT[d][hd(h), x:x + C],
                                              start=False, stop=(st == 7 and d == 1), skip_group_check=True)
                    last.then_inc(sem("out_y"), 1)
                    w("bonus_in", 1)
                    mm(bank[2][:, 0:SEQ], heads1, KD, start=True, stop=True).then_inc(sem("bonus_full"), 1)
                    w("y_copied", 1)
                    mm(bank[0][:, 0:SEQ], heads64, YF, start=True, stop=True).then_inc(sem("gn_mean"), 1)
                    w("gn_sq", 1)
                    mm(bank[1][:, 0:SEQ], heads64, YS, start=True, stop=True).then_inc(sem("gn_var"), 1)
                pe.wait_ge(sem("pair_done"), KT + 1)
            if upto >= 6:
                for m in range(KT):
                    if m % 2 == 0:
                        s = rg.loaded_slot()
                    if m >= 4:
                        pe.wait_ge(sem("residual_done"), 16 + m - 3)
                    w_ = ring[s].rearrange("p (k n) -> p k n", n=256)[:, :, (m % 2) * P:(m % 2 + 1) * P]
                    for k in range(KT):
                        last = pe.matmul(bank[m % 4][:, seg[1]], w_[:, k, :], YT[:, k, :], start=(k == 0), stop=(k == KT - 1))
                    last.then_inc(sem("out_full"), 1)
                layer_norm(3, SEQ)
            if upto >= 7:
                pe.wait_ge(sem("ld_router"), 16)
                pe.wait_ge(sem("u_ready"), 3)
                for tt in range(2):
                    cs = slice(SEQ + tt * P, SEQ + tt * P + P)
                    for k in range(KT):
                        last = pe.matmul(bank[0][:, tt * 8:tt * 8 + 8], UT[:, k, cs], rt_w[:, k, :],
                                         start=(k == 0), stop=(k == KT - 1))
                last.then_inc(sem("logits_full"), 1)
                for tt in range(2):
                    for k in range(KT):
                        last = pe.transpose(bank[1 + 2 * tt + k // 4][:, (k % 4) * P:(k % 4) * P + P],
                                            XT[:, k, SEQ + tt * P:SEQ + tt * P + P], ident)
                last.then_inc(sem("tok_full"), 1)
                for n in range(24):
                    pe.wait_ge(sem("diag_ready"), n + 1)
                    if n == 8:
                        pe.wait_ge(sem("tok_taken"), 4)
                    pe.matmul(bank[[5, 6, 7, 1, 2, 3][n // 4]][:, (n % 4) * P:(n % 4) * P + P], ones, diag[n % 2],
                              start=True, stop=True).then_inc(sem("row_full"), 1)
                pe.wait_ge(sem("row_taken"), 6)
                pe.wait_ge(sem("logits_taken"), 1)
                pe.sem_inc(sem("y_done"), 2)

                def y_part(e, j):
                    pe.wait_ge(sem(f"ew_loaded{(3 * j + 2) % ERN}"), 48 * e + 16 * ((3 * j + 2) // ERN + 1))
                    pe.wait_ge(sem("h_done"), 28 * e + 4 * j + 8)
                    if j == 0:
                        pe.wait_ge(sem("y_taken"), e + 1)
                    w2_ = ering[(3 * j + 2) % ERN].rearrange("p a b -> p (a b)").rearrange("p (a b) -> p a b", b=D)
                    for f in range(4):
                        for tt in range(2):
                            for half in range(2):
                                last = pe.matmul(bank[4 + 2 * tt + half][:, :], HT[j % 2][:, f, tt * P:tt * P + P],
                                                 w2_[:, f, half * 512:half * 512 + 512],
                                                 start=(j == 0 and f == 0), stop=(j == EJ - 1 and f == 3))
                    last.then_inc(sem("y_done"), 1)

                with pe.Fori(0, N_EXP) as e:
                    for j in range(EJ):
                        for r in range(2):
                            pe.wait_ge(sem(f"ew_loaded{(3 * j + r) % ERN}"), 48 * e + 16 * ((3 * j + r) // ERN + 1))
                        for f in range(4):
                            pe.wait_ge(sem("h_done"), 28 * e + 4 * j + f + 1)
                            for r in range(2):
                                wt = ering[(3 * j + r) % ERN]
                                for k in range(KT):
                                    last = pe.matmul(bank[f][:, r * SEQ:r * SEQ + SEQ], wt[:, k, f * P:f * P + P],
                                                     UT[:, k, seg[1]], start=(k == 0), stop=(k == KT - 1))
                            last.then_inc(sem("gu_full"), 1)
                        if j:
                            y_part(e, j - 1)
                    y_part(e, EJ - 1)

        @block.scalar
        def _(act):
            link = Chain(act, sem("act_chain"))
            pe_x = sem("x_turned")
            act.wait_ge(sem("vec_ready"), 1)
            link(act.activation(silu_c[:, :, 0], vec[:, 3 * P + 72:3 * P + 80], ACT.Silu))
            act.activation(silu_c[:, :, 1], vec[:, 3 * P + 80:3 * P + 88], ACT.Silu).then_inc(sem("silu_ready"), 1)
            for k in range(KT):
                act.wait_ge(pe_x, k + 1)
                act.copy(XT[:, k, :], bank[1 + k % 4][:, :]).then_inc(sem("x_taken"), 1)
            act.wait_ge(sem("ld_filter"), 16 * 9)
            act.activation(dec[0:1, :], dec[0:1, :], ACT.Abs).then_inc(sem("decay_abs"), 1)
            for j in range(2):
                act.wait_ge(sem("sine_arg"), j + 1)
                act.activation(hargs[2 + j][0:HY_W, :], hargs[1][0:HY_W, :], ACT.Sin).then_inc(sem("sine_out"), 1)
            for n in range(2):
                for q in range(4):
                    g = 4 * n + q
                    act.wait_ge(sem("filter_full"), g + 1)
                    if g >= 1:
                        act.wait_ge(sem("filter_taken"), g)
                    for j in range(2):
                        act.activation(win_f[j], bank[4 * (g % 2) + 2 + j][:, :], ACT.Exp).then_inc(sem("window"), 1)
                for o in range(8):
                    act.wait_ge(sem("spectrum_full"), 8 * n + o + 1)
                    c, f, half = o // 4, o // 2 % 2, o % 2
                    act.copy(KSP[:, 4 * n + 2 * c + f, half * 512:half * 512 + 512], bank[o][:, :])\
                        .then_inc(sem("spectrum_taken"), 1)

            def modulation(layer):
                dst = [mod_rows0, mod_rows1][layer]
                act.sem_inc(sem("mod_taken"), 6)

                def round_(c0, j):
                    act.wait_ge(sem("mod_full"), c0 + j + 1 + 24 * layer)
                    b = (ring_start[layer] + j) % RN
                    act.copy(dst[0:2, bass.ds((c0 + j) * 256, 256)], bank[b][0:2, 0:256]).then_inc(sem("mod_taken"), 1)
                with act.Fori(0, 4) as i:
                    for j in range(RN):
                        round_(i * RN, j)
            modulation(0)

            def layer_norm(n, layer, j, width=T):
                cols = slice(T - width, T)
                for k in range(KT):
                    act.wait_ge(sem("ln_centred"), 8 * (n - 1) + k + 1)
                    act.activation(SQ[:, k, 0:width], XT[:, k, cols], ACT.Square).then_inc(sem("ln_square"), 1)
                act.wait_ge(sem("ln_var"), n)
                act.activation(std[:, 0:width], bank[1][:, 0:width], ACT.Sqrt, bias=eps[:, 0:1]).then_inc(sem("ln_std"), 1)
                for k in range(KT):
                    act.wait_ge(sem("ln_scaled"), 8 * (n - 1) + k + 1)
                    act.activation(XT[:, k, cols], XT[:, k, cols], ACT.Identity,
                                   bias=col("ln_b", (2 * layer + j) * KT + k)).then_inc(sem("ln_done"), 1)

            if upto >= 2:
                for m in range(24):
                    act.wait_ge(sem("proj_full"), m + 1)
                    if m >= 2:
                        act.wait_ge(sem("conv_done"), m - 1)
                    act.activation(pad[m % 2][:, :, 1:SEQ + 1], bank[m % 4][:, :].rearrange("p (s t) -> p s t", s=2),
                                   ACT.Identity, bias=col("hy_b_in", m)).then_inc(sem("proj_taken"), 1)
                    if 1 <= m <= KT:
                        act.wait_ge(sem("v_turned"), m)
                        act.copy(ZT[:, :, (m - 1) * P:m * P], bank[4 + (m - 1) % 2][:, :].rearrange("p (t c) -> p t c", t=NB))\
                            .then_inc(sem("v_taken"), 1)
                for k in range(KT):
                    act.wait_ge(sem("z_turned"), k + 1)
                    act.copy(ZT[:, :, k * P:(k + 1) * P], bank[k % 4][:, :].rearrange("p (t c) -> p t c", t=NB))\
                        .then_inc(sem("z_taken"), 1)
                layer_norm(1, 0, 0)
            if upto >= 3:
                with_loop(act, FT, lambda f, j: (
                    act.wait_ge(sem("hidden_full"), f + 1),
                    act.wait_ge(sem("sil_free"), f + 1),
                    act.activation(sil[j % 2], bank[2 * ((ffn_start + j) % 2)][:, :], ACT.Silu)
                    .then_inc(sem("sil_ready"), 1)))
                modulation(1)
                layer_norm(2, 0, 1)
            if upto >= 4:
                act.wait_ge(sem("lora_full"), 1)
                act.activation(HW, bank[0][:, :], ACT.Tanh).then_inc(sem("lora_taken"), 1)
                act.wait_ge(sem("lora_full"), 2)
                act.copy(HA, bank[1][:, :]).then_inc(sem("lora_taken"), 1)
                act.wait_ge(sem("lora_full"), 3)
                act.activation(G1a, bank[2][:, 0:SEQ], ACT.Sigmoid).then_inc(sem("lora_taken"), 1)
                act.activation(G1b[0:32, :], bank[3][0:32, 0:SEQ], ACT.Sigmoid).then_inc(sem("lora_taken"), 1)
            if upto >= 5:
                with act.Fori(0, KT) as i:
                    w = waiter(act, i)
                    w("proj", 1)
                    w("pair_done", 1)
                    act.copy(Kf, bank[0][:, :]).then_inc(sem("k_copied"), 1)
                    for d in range(2):
                        w("proj", 2 * d + 2)
                        act.activation(SG[d], bank[3 + d][:, :], ACT.Sigmoid, bias=dcol("rw_w0", i + 8 * d))\
                            .then_inc(sem("sg"), 1)
                        w("proj", 2 * d + 3)
                        act.activation(AS[d], bank[5 + d][:, :], ACT.Sigmoid, bias=dcol("rw_a0", i + 8 * d))\
                            .then_inc(sem("rate"), 1)
                    w("proj", 6)
                    act.copy(Rf, bank[2][:, 0:SEQ]).then_inc(sem("r_copied"), 1)
                    w("proj", 7)
                    act.copy(Vf, bank[1][:, :]).then_inc(sem("v_copied"), 1)
                    w("proj", 8)
                    act.copy(Gf, bank[7][:, 0:SEQ]).then_inc(sem("g_copied"), 1)
                    w("ksum", 1)
                    act.activation(KS, bank[0][:, :], ACT.Sqrt, bias=eps[:, 2:3]).then_inc(sem("kstd"), 1)
                    w("vt_full", 1)
                    act.copy(Vt, b4(1)).then_inc(sem("vt_ready"), 1)
                    for d in range(2):
                        w("decayed", d + 1)
                        if d == 1:
                            w("k_t", 1)
                            w("r_t", 1)
                        act.activation(EP, CS, ACT.Exp, scale=-DECAY).then_inc(sem("e_incl"), 1)
                        act.activation(EN, CS, ACT.Exp, scale=DECAY).then_inc(sem("e_inv"), 1)
                        w("excl", d + 1)
                        act.activation(EX, SG[d], ACT.Exp, scale=-DECAY).then_inc(sem("e_excl"), 1)
                    for d in range(2):
                        w("tr_full", 3 * d + 1)
                        for h in range(2):
                            if d == 1:
                                w("wu_full", h + 1)
                            act.copy(Q[h][:, :, 0:C], b4(2)[:, :, hd(h)]).then_inc(sem("q_ready"), 1)
                        w("tr_full", 3 * d + 2)
                        if d == 1:
                            w("n_full", 1)
                        act.copy(Btok, b4(3)).then_inc(sem("bk_ready"), 1)
                        w("tr_full", 3 * d + 3)
                        act.copy(Ktok, b4(4)).then_inc(sem("bk_ready"), 1)
                        for lv in range(1, len(LEVELS)):
                            for h in range(2):
                                n = 10 * d + 2 * (lv - 1) + h + 1
                                w("y_full", n)
                                if n > 2:
                                    w("z_full", n - 2)
                                act.copy(Yb[h], b4(h)).then_inc(sem("y_ready"), 1)
                        for h in range(2):
                            w("z1_full", 2 * d + h + 1)
                            act.copy(Q[h][:, :, C:P], bank[h][:, 0:NB * C].rearrange("p (b c) -> p b c", b=NB))\
                                .then_inc(sem("z1_ready"), 1)
                        for h in range(2):
                            w("wu_full", 2 * d + h + 1)
                            act.copy(WU[h], b4(2 + h)).then_inc(sem("wu_ready"), 1)
                    w("out_y", 1)
                    act.copy(YF, bank[7][:, 0:SEQ]).then_inc(sem("y_copied"), 1)
                    w("gn_cent", 1)
                    act.activation(YS, YN, ACT.Square).then_inc(sem("gn_sq"), 1)
                    w("gn_var", 1)
                    act.activation(YS, bank[1][:, 0:SEQ], ACT.Sqrt, bias=eps[:, 1:2]).then_inc(sem("gn_std"), 1)
            if upto >= 6:
                layer_norm(3, 1, 0, SEQ)
            if upto >= 7:
                act.wait_ge(sem("tok_full"), 1)
                for tt in range(2):
                    for h in range(2):
                        act.copy(XTOK[:, tt, h * 512:h * 512 + 512], bank[1 + 2 * tt + h][:, :]).then_inc(sem("tok_taken"), 1)
                act.wait_ge(sem("gap"), 1)
                act.activation(w12[:, :, 1:2], w12[:, :, 0:1], ACT.Exp).then_inc(sem("gap_exp"), 1)
                for n in range(6):
                    act.wait_ge(sem("row_full"), 4 * n + 4)
                    row = (rowG, rowg, rowb)[n // 2]
                    act.copy(row[:, (n % 2) * 512:(n % 2) * 512 + 512], bank[[5, 6, 7, 1, 2, 3][n]][:, :])\
                        .then_inc(sem("row_taken"), 1)
                with act.Fori(0, N_EXP) as e:
                    for n in range(28):
                        act.wait_ge(sem("gu_full"), 28 * e + n + 1)
                        act.wait_ge(sem("h_done"), 28 * e + n + 3)
                        act.activation(sil2[n % 2], bank[n % 4][:, 0:SEQ], ACT.Silu).then_inc(sem("sil2_ready"), 1)
                for tt in range(2):
                    act.wait_ge(sem("fin_centred"), tt + 1)
                    act.activation(XTOK[:, tt, :], OUT[:, tt, :], ACT.Square, accum_out=stat[:, tt, 1:2])\
                        .then_inc(sem("fin_square"), 1)
                    act.wait_ge(sem("fin_square"), tt + 1)
                    act.activation(stat[:, tt, 2:3], stat[:, tt, 1:2], ACT.Sqrt, bias=eps[:, 0:1], scale=1.0 / D)\
                        .then_inc(sem("fin_std"), 1)

        @block.gpsimd
        def _(pool):
            for n in range(2):
                for q in range(4):
                    g = 4 * n + q
                    half, tt = q // 2, q % 2
                    pool.wait_ge(sem("taps"), g + 1)
                    if q == 0 and n == 1:
                        pool.wait_ge(sem("spectrum_full"), 8)
                    cs = slice(half * 512, half * 512 + 512)
                    pool.tensor_tensor(kcs[:, 0, tt, cs], pr[0], pr[1], ALU.add).then_inc(sem("pool_taps"), 1)
                    pool.tensor_tensor(kcs[:, 1, tt, cs], pr[0], pr[1], ALU.subtract).then_inc(sem("taps_ready"), 1)
            if upto >= 2:
                for g in range(8):
                    for f in range(2):
                        pool.wait_ge(sem("bins_mult"), 4 * g + 2 * f + 1)
                        if f == 0 and g >= 2:
                            pool.wait_ge(sem("long_full"), 4 * (g - 1))
                        pool.tensor_tensor(Y[:, g % 2, f, :], pr[0], pr[1], ALU.subtract).then_inc(sem("pool_re"), 1)
                        pool.wait_ge(sem("bins_mult"), 4 * g + 2 * f + 2)
                        pool.tensor_tensor(Y[:, g % 2, 2 + f, :], pr[2], pr[3], ALU.add)\
                            .then_inc(sem("pool_im"), 1)
                    pool.wait_ge(sem("pool_re"), 2 * g + 2)
                    pool.wait_ge(sem("pool_im"), 2 * g + 2)
                    pool.sem_inc(sem("product_ready"), 1)
            if upto >= 5:
                pool.wait_ge(sem("ld_table1"), 32)
                with pool.Fori(0, KT) as i:
                    w = waiter(pool, i)
                    w("kk_raw", 1)
                    pool.tensor_tensor(KS, KK, KK, ALU.mult).then_inc(sem("ksq"), 1)
                    for d in range(2):
                        w("decayed", d + 1)
                        pool.tensor_tensor(SG[d], CS, SG[d], ALU.subtract).then_inc(sem("excl"), 1)
                        w("kk_ready", 1)
                        w("rate_used", d + 1)
                        pool.tensor_tensor(AS[d], KK, AS[d], ALU.mult).then_inc(sem("b_raw"), 1)
                    for d in range(2):
                        if d == 1:
                            w("wu_full", 2)
                            w("wu_ready", 2)
                            w("n_full", 1)
                            w("y_local", 1)
                            w("g_full", 1)
                            settle(pool)
                        else:
                            w("pair_done", 1)
                            settle(pool)
                        for h in range(2):
                            pool.tensor_copy(TM[h], each4(ident))
                            pool.tensor_copy(TT[h], each4(ident)).then_inc(sem("t_reset"), 1)

        @block.vector
        def _(dve):
            link = Chain(dve, sem("dve_chain"))
            link(dve.memset(eps[:, 0:1], LN_EPS))
            link(dve.memset(eps[:, 1:2], RW_GN_EPS))
            link(dve.memset(eps[:, 2:3], 1e-6))
            link(dve.memset(eps[:, 3:4], 0.0))
            dve.wait_ge(sem("rows_turned"), 1)
            for j, n in enumerate(ROW_FILL):
                last = dve.tensor_copy(vec[:, j * P:j * P + n], bank[0][:, j * P:j * P + n])
            last.then_inc(sem("vec_ready"), 1)
            dve.wait_ge(sem("ld_filter"), 16 * 9)
            dve.wait_ge(sem("ld_table"), 16)
            magic = float(1.5 * 2 ** 23)
            for j in range(2):
                dve.wait_ge(sem("sine_in"), j + 1)
                arg, t = hargs[0][0:HY_W, :], hargs[1][0:HY_W, :]
                if j == 1:
                    dve.wait_ge(sem("sine_out"), 1)
                link(dve.tensor_scalar(arg, bank[5 + j][0:HY_W, 0:SEQ], hcol[0:HY_W, j:j + 1],
                                       hcol[0:HY_W, 2 + j:3 + j], ALU.add, ALU.mult))
                link(dve.tensor_scalar(t, arg, 1.0 / (2 * math.pi), magic, ALU.mult, ALU.add))
                link(dve.tensor_scalar(t, t, magic, None, ALU.subtract))
                link(dve.scalar_tensor_tensor(out=arg, in0=t, scalar=-6.28125, in1=arg, op0=ALU.mult, op1=ALU.add))
                link(dve.scalar_tensor_tensor(out=arg, in0=t, scalar=-(2 * math.pi - 6.28125), in1=arg,
                                              op0=ALU.mult, op1=ALU.add))
                dve.tensor_scalar(t, arg, -3.1415925, 3.1415925, ALU.max, ALU.min).then_inc(sem("sine_arg"), 1)
            for n in range(2):
                for q in range(4):
                    g = 4 * n + q
                    half, tt = q // 2, q % 2
                    b = 4 * (g % 2)
                    dve.wait_ge(sem("window"), 2 * g + 2)
                    if g >= 1:
                        dve.wait_ge(sem("taps_ready"), g)
                        dve.wait_ge(sem("pool_taps"), g)
                    link(dve.tensor_tensor(pr[0], bank[b][:, :], win_f[0], ALU.mult))
                    if tt == 0:
                        link(dve.tensor_tensor(pr[0][0:1, :], pr[0][0:1, :],
                                               skip[0:1, n * D + half * 512:n * D + half * 512 + 512], ALU.add))
                        link(dve.scalar_tensor_tensor(out=pr[1], in0=bank[b + 1][:, :], scalar=notfirst,
                                                      in1=win_f[1], op0=ALU.mult, op1=ALU.mult))
                    else:
                        link(dve.tensor_tensor(pr[1], bank[b + 1][:, :], win_f[1], ALU.mult))
                    dve.sem_inc(sem("taps"), 1)
                    dve.sem_inc(sem("filter_taken"), 1)

            def modulation(layer):
                dve.wait_ge(sem("mod_turned"), layer + 1)
                name = f"mod_b{layer}"
                tile, first, n = ROWS[name]
                bias = vec[:, tile * P + first:tile * P + first + n]
                ps = bank[6][:, 0:96].rearrange("p (j s) -> p j s", s=2)
                for s in range(2):
                    link(dve.tensor_tensor(modv[layer][:, :, s], ps[:, :, s], bias, ALU.add))
                for ch in (1, 4):
                    v = modv[layer][:, ch * KT:(ch + 1) * KT, :]
                    link(dve.tensor_scalar(v, v, 1.0, None, ALU.add))
            modulation(0)

            def modulate(layer, first, streams=(0, 1)):
                for k in range(KT):
                    for s in streams:
                        last = dve.tensor_scalar(UT[:, k, seg[s]], XT[:, k, seg[s]], mv(layer, first + 1, k, s),
                                                 mv(layer, first, k, s), ALU.mult, ALU.add)
                last.then_inc(sem("u_ready"), 1)

            def layer_norm(n, layer, j, width=T):
                cols = slice(T - width, T)
                dve.wait_ge(sem("ln_mean"), n)
                for k in range(KT):
                    dve.tensor_tensor(XT[:, k, cols], XT[:, k, cols], bank[0][:, 0:width], ALU.subtract)\
                        .then_inc(sem("ln_centred"), 1)
                dve.wait_ge(sem("ln_std"), n)
                dve.wait_ge(sem("ln_centred"), 8 * n)
                link(dve.reciprocal(rstd[:, 0:width], std[:, 0:width]))
                for k in range(KT):
                    dve.scalar_tensor_tensor(out=XT[:, k, cols], in0=XT[:, k, cols],
                                             scalar=col("ln_g", (2 * layer + j) * KT + k), in1=rstd[:, 0:width],
                                             op0=ALU.mult, op1=ALU.mult).then_inc(sem("ln_scaled"), 1)
                dve.wait_ge(sem("ln_done"), 8 * n)

            def residual(n, layer, gate, bias, b0, streams=(0, 1)):
                for m in range(KT):
                    dve.wait_ge(sem("out_full"), 8 * (n - 1) + m + 1)
                    t = rt[m % 2]
                    for s in streams:
                        g = mv(layer, gate, m, s)
                        ps = bank[b0 + m % 4][:, seg[s]]
                        if bias:
                            link(dve.tensor_scalar(t[:, seg[s]], ps, col(bias, m), g, ALU.add, ALU.mult))
                        else:
                            link(dve.tensor_scalar(t[:, seg[s]], ps, g, None, ALU.mult))
                    c = slice(SEQ * streams[0], T)
                    dve.scalar_tensor_tensor(out=XT[:, m, c], in0=XT[:, m, c], scalar=float(ALPHA), in1=t[:, c],
                                             op0=ALU.mult, op1=ALU.add).then_inc(sem("residual_done"), 1)

            if upto >= 2:
                dve.wait_ge(sem("spectrum_full"), 16)
                modulate(0, 0)
                for p_ in pad:
                    link(dve.memset(p_[:, :, 0:1], 0.0))
                    link(dve.memset(p_[:, :, SEQ + 1:SEQ + 2], 0.0))
                for m in range(24):
                    dve.wait_ge(sem("proj_taken"), m + 1)
                    dst = (cv[m % 2] if m < 8 else X1[:, m - 8, :] if m < 16 else X2[:, m - 16, :])
                    dst = dst.rearrange("p (s t) -> p s t", s=2)
                    pd = pad[m % 2]
                    if 2 <= m < 8:
                        dve.wait_ge(sem("v_turned"), m - 1)
                    link(dve.tensor_scalar(dst, pd[:, :, 1:SEQ + 1], col("hy_conv_w", 24 + m), col("hy_conv_b", m),
                                           ALU.mult, ALU.add))
                    link(dve.scalar_tensor_tensor(out=dst, in0=pd[:, :, 0:SEQ], scalar=col("hy_conv_w", m), in1=dst,
                                                  op0=ALU.mult, op1=ALU.add))
                    dve.scalar_tensor_tensor(out=dst, in0=pd[:, :, 2:SEQ + 2], scalar=col("hy_conv_w", 48 + m), in1=dst,
                                             op0=ALU.mult, op1=ALU.add).then_inc(sem("conv_done"), 1)
                dve.wait_ge(sem("conv_done"), 24)

                def products(n, g):
                    half, s = g // 2, g % 2
                    cs = slice(half * 512, half * 512 + 512)
                    dve.wait_ge(sem("bins_full"), 4 * n + g + 1)
                    for f in range(2):
                        re, im = bank[f][:, :], bank[2 + f][:, :]
                        kr, ki = KSP[:, 4 * n + f, cs], KSP[:, 4 * n + 2 + f, cs]
                        u = 2 * (4 * n + g) + f
                        if u >= 1:
                            dve.wait_ge(sem("pool_re"), u)
                        dve.tensor_tensor(pr[0], re, kr, ALU.mult)
                        link(dve.tensor_tensor(pr[1], im, ki, ALU.mult))
                        dve.sem_inc(sem("bins_mult"), 1)
                        if u >= 1:
                            dve.wait_ge(sem("pool_im"), u)
                        dve.tensor_tensor(pr[2], re, ki, ALU.mult)
                        link(dve.tensor_tensor(pr[3], im, kr, ALU.mult))
                        dve.sem_inc(sem("bins_mult"), 1)
                    dve.sem_inc(sem("bins_taken"), 1)

                def gating(n, g):
                    half, s = g // 2, g % 2
                    X = [X1, X2][n]
                    for ct in range(4):
                        dve.wait_ge(sem("long_full"), 16 * n + 4 * g + ct + 1)
                        x = X[:, 4 * half + ct, seg[s]]
                        dve.tensor_tensor(x, x, bank[4 + ct][:, 0:SEQ], ALU.mult).then_inc(sem("long_taken"), 1)

                for n in range(2):
                    for g in range(5):
                        if g < 4:
                            products(n, g)
                        if g >= 1:
                            gating(n, g - 1)
                residual(1, 0, 2, "hy_b_out", 0)
                layer_norm(1, 0, 0)
            if upto >= 3:
                modulate(0, 3)
                dve.sem_inc(sem("hidden_taken"), 2)
                dve.sem_inc(sem("sil_free"), 2)

                def hid(f, j):
                    dve.wait_ge(sem("sil_ready"), f + 1)
                    dve.tensor_tensor(Hf[:, bass.ds(f * T, T)], sil[j % 2],
                                      bank[2 * ((ffn_start + j) % 2) + 1][:, :], ALU.mult).then_inc(sem("hidden_mult"), 1)
                    dve.wait_ge(sem("hidden_mult"), f + 1)
                    dve.sem_inc(sem("hidden_taken"), 1)
                    dve.sem_inc(sem("sil_free"), 1)
                with_loop(dve, FT, hid)
                residual(2, 0, 5, None, 4)
                modulation(1)
                layer_norm(2, 0, 1)
            if upto >= 4:
                for k in range(KT):
                    for s in range(2):
                        dve.tensor_scalar(UP[:, k, s, 1:SEQ + 1], XT[:, k, seg[s]], mv(1, 1, k, s), mv(1, 0, k, s),
                                          ALU.mult, ALU.add)
                link(dve.memset(UP[:, :, :, 0:1], 0.0))
                link(dve.memset(UP[:, :, :, SEQ + 1:SEQ + 2], 0.0))

                def two(v):
                    return v.rearrange("p (s t) -> p s t", s=2)
                for k in range(KT):
                    dve.tensor_tensor(two(XX[:, k, :]), UP[:, k, :, 0:SEQ], UP[:, k, :, 2:SEQ + 2], ALU.add)
                link(dve.memset(eps[:, 3:4], 0.0))
                for k in range(KT):
                    last = dve.scalar_tensor_tensor(out=two(XX[:, k, :]), in0=two(XX[:, k, :]), scalar=0.5,
                                                    in1=UP[:, k, :, 1:SEQ + 1], op0=ALU.mult, op1=ALU.subtract)
                link(last)

                def mix(dst, j):
                    for k in range(KT):
                        last = dve.scalar_tensor_tensor(out=two(dst[:, k, :]), in0=two(XX[:, k, :]),
                                                        scalar=col("rw_mu", j * KT + k), in1=UP[:, k, :, 1:SEQ + 1],
                                                        op0=ALU.mult, op1=ALU.add)
                    return last

                def mix_x(dst, j):
                    for k in range(KT):
                        last = dve.scalar_tensor_tensor(out=dst[:, k, 0:SEQ], in0=XX[:, k, seg[1]],
                                                        scalar=col("rw_mu", j * KT + k), in1=UP[:, k, 1, 1:SEQ + 1],
                                                        op0=ALU.mult, op1=ALU.add)
                    return last
                mix(XM, 1).then_inc(sem("xm_ready"), 1)
                mix(XK, 2)
                dve.wait_ge(sem("lora_full"), 1)
                mix(XM, 4).then_inc(sem("xm_ready"), 1)
                mix(XV, 3)
                dve.wait_ge(sem("lora_full"), 2)
                mix_x(XM, 5).then_inc(sem("xm_ready"), 1)
                link(mix_x(XR, 0))
                tile, first, n = ROWS["rw_k_a"]
                link(dve.tensor_scalar(one_ka, vec[:, tile * P + first:tile * P + first + n], -1.0, 1.0, ALU.mult, ALU.add))
                dve.wait_ge(sem("lora_full"), 3)
                dve.sem_inc(sem("pair_done"), 1)
            if upto >= 5:
                dve.wait_ge(sem("ld_table1"), 32)
                with dve.Fori(0, KT) as i:
                    w = waiter(dve, i)
                    link.enter(i, DVE_LINKS)
                    w("k_copied", 1)
                    dve.tensor_scalar(KK, Kf, dcol("rw_k_k", i), None, ALU.mult).then_inc(sem("kk_raw"), 1)
                    w("kstd", 1)
                    link(dve.reciprocal(KS, KS))
                    w("kk_raw", 1)
                    dve.tensor_tensor(KK, KK, KS, ALU.mult).then_inc(sem("kk_ready"), 1)
                    w("kk_ready", 1)
                    for d in range(2):
                        w("sg", d + 1)
                        if d == 1:
                            w("e_inv", 1)
                            w("excl", 1)
                        if d == 0:
                            dve.tensor_tensor_scan(CS, reset[0], SG[0], 0.0, ALU.mult, ALU.add).then_inc(sem("decayed"), 1)
                        else:
                            dve.tensor_tensor_scan(CS[:, ::-1], reset[1][:, ::-1], SG[1][:, ::-1], 0.0, ALU.mult,
                                                   ALU.add).then_inc(sem("decayed"), 1)
                        w("rate", d + 1)
                        dve.tensor_scalar(Kt[d], AS[d], dcol("rw_k_a", i), one_ka[:, bass.ds(i, 1)], ALU.mult, ALU.add)\
                            .then_inc(sem("rate_used"), 1)
                        w("rate_used", d + 1)
                        link(dve.tensor_tensor(Kt[d], Kt[d], Kf, ALU.mult))
                        if d == 0:
                            link(dve.tensor_copy(KD, Kt[0][:, seg[1]]))
                        else:
                            link(dve.tensor_tensor(KD, KD, Kt[1][:, seg[1]], ALU.add))
                        w("e_incl", d + 1)
                        w("r_copied", 1)
                        last_col = C - 1 if d == 0 else 0
                        link(dve.tensor_copy(DC[d], EP.rearrange("p (c t) -> p c t", t=C)[:, :, last_col]))
                        dve.tensor_tensor(Rt[d], Rf, EP[:, seg[1]], ALU.mult).then_inc(sem("r_t"), 1)
                        w("e_inv", d + 1)
                        dve.tensor_tensor(Kt[d], Kt[d], EN, ALU.mult).then_inc(sem("k_t"), 1)
                        w("b_raw", d + 1)
                        dve.tensor_tensor(Bt[d], AS[d], EN, ALU.mult).then_inc(sem("b_t"), 1)
                        w("e_excl", d + 1)
                        dve.scalar_tensor_tensor(out=At[d], in0=KK, scalar=-1.0, in1=EX, op0=ALU.mult, op1=ALU.mult)\
                            .then_inc(sem("a_t"), 1)
                        w("b_t", d + 1)
                        w("k_t", d + 1)
                        w("r_t", d + 1)
                        w("a_t", d + 1)
                    link(dve.tensor_tensor(KD, KD, Rf, ALU.mult))
                    dve.tensor_scalar(KD, KD, dcol("rw_r_k", i), None, ALU.mult).then_inc(sem("bonus_in"), 1)
                    for d in range(2):
                        for h in range(2):
                            where = [(0, 1, 5, 6), (2, 3, 4, 0)][h]
                            n = 8 * d + 4 * h
                            w("sc", n + 1)
                            if h == 0:
                                w("t_reset", 2 * d + 2)
                            settle(dve)
                            dve.copy_predicated(TM[h], each4(bits[0][d]), b4(where[0]))
                            dve.tensor_tensor(Aab[h], b4(where[0]), each4(strict[d]), ALU.mult).then_inc(sem("sc_taken"), 1)
                            w("sc", n + 2)
                            settle(dve)
                            dve.copy_predicated(TT[h], each4(bits[0][1 - d]), b4(where[1])).then_inc(sem("sc_taken"), 1)
                            w("sc", n + 3)
                            dve.tensor_tensor(AakT[h], b4(where[2]), each4(strict[1 - d]), ALU.mult)\
                                .then_inc(sem("sc_taken"), 1)
                            w("sc", n + 4)
                            dve.tensor_tensor(ARR[h], b4(where[3]), each4(incl_t[d]), ALU.mult)\
                                .then_inc(sem("sc_taken"), 1)
                        w("sc_taken", 8 * d + 8)
                        for lv in range(1, len(LEVELS)):
                            for h in range(2):
                                n = 10 * d + 2 * (lv - 1) + h + 1
                                w("z_full", n)
                                settle(dve)
                                if lv < len(LEVELS) - 1:
                                    dve.copy_predicated(TM[h], each4(bits[lv][d]), b4(2 + h))
                                dve.copy_predicated(TT[h], each4(bits[lv][1 - d]), b4(4 + h)).then_inc(sem("merged"), 1)
                                w("merged", n)
                        w("m_full", d + 1)
                        for o in range(2):
                            last = dve.tensor_tensor(MO[d][:, o::2, :], c4(4 + o), eye64.unsqueeze(1).to_broadcast([P, 4, C]),
                                                     ALU.add)
                        last.then_inc(sem("mo_ready"), 1)
                        w("n_full", d + 1)
                        for o in range(2):
                            last = dve.tensor_tensor(ND[d][:, o::2, :], c4(o),
                                                     DC[d][:, o::2].unsqueeze(2).to_broadcast([P, 4, C]), ALU.mult)
                        last.then_inc(sem("nd_ready"), 1)
                        w("g_full", d + 1)
                        dve.tensor_tensor(GT[d], bank[6][:, 0:SEQ], Rt[d], ALU.add).then_inc(sem("gt_ready"), 1)
                    w("nd_ready", 2)
                    for d in range(2):
                        dve.tensor_copy(ST[d][:, 1, :], ND[d][:, CHUNKS[d][0], :]).then_inc(sem("st_ready"), 1)
                    for st in range(1, 7):
                        for d in range(2):
                            c = CHUNKS[d][st]
                            w("st_full", 2 * (st - 1) + d + 1)
                            dve.scalar_tensor_tensor(out=ST[d][:, st + 1, :], in0=bank[d][:, 0:C], scalar=DC[d][:, c:c + 1],
                                                     in1=ND[d][:, c, :], op0=ALU.mult, op1=ALU.add)\
                                .then_inc(sem("st_ready"), 1)
                    w("bonus_full", 1)
                    link(dve.tensor_tensor(KD, bank[2][:, 0:SEQ], Vf[:, seg[1]], ALU.mult))
                    w("gn_mean", 1)
                    dve.tensor_tensor(YN, YF, bank[0][:, 0:SEQ], ALU.subtract).then_inc(sem("gn_cent"), 1)
                    w("gn_cent", 1)
                    w("gn_std", 1)
                    link(dve.reciprocal(YS, YS))
                    link(dve.scalar_tensor_tensor(out=YN, in0=YN, scalar=dcol("rw_lnx_g", i), in1=YS, op0=ALU.mult,
                                                  op1=ALU.mult))
                    link(dve.scalar_tensor_tensor(out=YN, in0=YN, scalar=dcol("rw_lnx_b", i), in1=KD, op0=ALU.add,
                                                  op1=ALU.add))
                    dve.tensor_tensor(YT.rearrange("p k t -> p (k t)")[:, bass.ds(i * SEQ, SEQ)], YN, Gf, ALU.mult)\
                        .then_inc(sem("pair_done"), 1)
                    w("pair_done", 2)
                link.leave(KT)
            if upto >= 6:
                residual(3, 1, 2, None, 0, streams=(1,))
                layer_norm(3, 1, 0, SEQ)
            if upto >= 7:
                modulate(1, 3, streams=(1,))
                dve.wait_ge(sem("logits_full"), 1)
                lg = bank[0][:, 0:16].rearrange("p (t e) -> p t e", t=2)
                dve.tensor_copy(logit, lg).then_inc(sem("logits_taken"), 1)
                dve.wait_ge(sem("logits_taken"), 1)
                for tt in range(2):
                    link(dve.max(mx[:, tt, :], logit[:, tt, :]))
                    link(dve.max_index(ix.rearrange("p (t e) -> p t e", t=2)[:, tt, :],
                                       mx[:, tt, :], logit[:, tt, :]))
                link(dve.tensor_copy(ixf.rearrange("p t e -> p (t e)"), ix))
                dve.tensor_tensor(w12[:, :, 0:1], mx[:, :, 1:2], mx[:, :, 0:1], ALU.subtract).then_inc(sem("gap"), 1)
                dve.wait_ge(sem("gap_exp"), 1)
                link(dve.tensor_scalar(w12[:, :, 0:1], w12[:, :, 1:2], 1.0, None, ALU.add))
                link(dve.reciprocal(w12[:, :, 2:3], w12[:, :, 0:1]))
                link(dve.tensor_tensor(w12[:, :, 3:4], w12[:, :, 2:3], w12[:, :, 1:2], ALU.mult))
                for tt in range(2):
                    link(dve.tensor_scalar(comb[:, tt, :], expert_no, ixf[:, tt, 0:1], w12[:, tt, 2:3], ALU.is_equal, ALU.mult))
                    link(dve.tensor_scalar(hot[:, tt, :], expert_no, ixf[:, tt, 1:2], w12[:, tt, 3:4], ALU.is_equal, ALU.mult))
                    link(dve.tensor_tensor(comb[:, tt, :], comb[:, tt, :], hot[:, tt, :], ALU.add))
                for n in range(24):
                    k = n % 8
                    c_ = (mv(1, 5, k, 1), col("ln_g", 24 + k), col("ln_b", 24 + k))[n // 8]
                    if n >= 2:
                        dve.wait_ge(sem("row_full"), n - 1)
                    dve.tensor_scalar(diag[n % 2], ident, c_, None, ALU.mult).then_inc(sem("diag_ready"), 1)
                link(dve.memset(OUT, 0.0))
                dve.sem_inc(sem("h_done"), 4)
                dve.sem_inc(sem("y_taken"), 1)
                with dve.Fori(0, N_EXP) as e:
                    for j in range(EJ):
                        dve.wait_ge(sem("y_done"), 7 * e + j + 1)
                        for f in range(4):
                            n = 4 * j + f
                            dve.wait_ge(sem("sil2_ready"), 28 * e + n + 1)
                            dve.tensor_tensor(HT[j % 2][:, f, :], sil2[n % 2], bank[f][:, seg[1]], ALU.mult)\
                                .then_inc(sem("h_done"), 1)
                    dve.wait_ge(sem("y_done"), 7 * e + 9)
                    for tt in range(2):
                        for half in range(2):
                            o = OUT[:, tt, half * 512:half * 512 + 512]
                            last = dve.scalar_tensor_tensor(out=o, in0=bank[4 + 2 * tt + half][:, :],
                                                            scalar=comb[:, tt, bass.ds(e, 1)], in1=o, op0=ALU.mult, op1=ALU.add)
                    last.then_inc(sem("y_taken"), 1)
                dve.wait_ge(sem("y_taken"), N_EXP + 1)
                for tt in range(2):
                    o = OUT[:, tt, :]
                    link(dve.tensor_tensor(o, o, rowG, ALU.mult))
                    link(dve.scalar_tensor_tensor(out=o, in0=XTOK[:, tt, :], scalar=float(ALPHA), in1=o, op0=ALU.mult,
                                                  op1=ALU.add))
                    link(dve.tensor_reduce(stat[:, tt, 0:1], o, AXX, ALU.add))
                    link(dve.tensor_scalar(stat[:, tt, 0:1], stat[:, tt, 0:1], 1.0 / D, None, ALU.mult))
                    dve.tensor_scalar(o, o, stat[:, tt, 0:1], None, ALU.subtract).then_inc(sem("fin_centred"), 1)
                for tt in range(2):
                    o = OUT[:, tt, :]
                    dve.wait_ge(sem("fin_std"), tt + 1)
                    link(dve.reciprocal(stat[:, tt, 3:4], stat[:, tt, 2:3]))
                    link(dve.scalar_tensor_tensor(out=o, in0=o, scalar=stat[:, tt, 3:4], in1=rowg, op0=ALU.mult, op1=ALU.mult))
                    dve.tensor_tensor(o, o, rowb, ALU.add).then_inc(sem("final"), 1)


_INS = ["x", "c", "ctx", "c_ctx", "mod_w", "mod_b", "ln_g", "ln_b", "hy_w_in", "hy_b_in", "hy_conv_w", "hy_conv_b",
        "hy_f_w1", "hy_f_b1", "hy_f_w2", "hy_f_b2", "hy_f_freq", "hy_f_w3", "hy_decay", "hy_skip", "hy_w_out",
        "hy_b_out", "rw_mu", "rw_w_rkv", "rw_w0", "rw_w1", "rw_w2", "rw_a0", "rw_a1", "rw_a2", "rw_g1", "rw_g2",
        "rw_k_k", "rw_k_a", "rw_r_k", "rw_lnx_g", "rw_lnx_b", "rw_w_out", "ffn_w13", "ffn_w2", "moe_router",
        "moe_w13", "moe_w2"]


def kernel(**inputs):
    import concourse.bacc as _bacc
    from concourse.bass_utils import run_bass_kernel_spmd as _run

    nc = _bacc.Bacc("TRN2", target_bir_lowering=False, num_devices=1)
    arrays, args = {}, {}
    for name in _INS:
        v = np.ascontiguousarray(inputs[name])
        arrays[f"in_{name}_dram"] = v
        args[name] = nc.dram_tensor(f"in_{name}_dram", v.shape, mybir.dt.from_np(v.dtype), kind="ExternalInput").ap()
    consts = []
    for n, v in enumerate(constants()):
        arrays[f"const_{n}_dram"] = v
        consts.append(nc.dram_tensor(f"const_{n}_dram", v.shape, mybir.dt.from_np(v.dtype), kind="ExternalInput").ap())
    out = nc.dram_tensor("out_0_dram", (1, SEQ, D), F32, kind="ExternalOutput").ap()
    build(nc, args, out, consts)
    r = _run(nc, [arrays], core_ids=[0])
    return r.results[0]["out_0_dram"]
```

```python
from contextlib import ExitStack
import math

import numpy as np

import concourse.bass as bass
from concourse import mybir

F32 = mybir.dt.float32
I32 = mybir.dt.int32
U32 = mybir.dt.uint32
ALU = mybir.AluOpType
ACT = mybir.ActivationFunctionType
AXX = mybir.AxisListType.X

P = 128
D = 1024
KT = D // P
SEQ = 256
T = 2 * SEQ
NB = T // P
DEPTH = 2
ALPHA = (2 * DEPTH) ** 0.25
LN_EPS = 1e-5
HY_BANDS = 8
HY_EMB = 1 + 2 * HY_BANDS
HY_W = 64
FFN = 2816
FT = FFN // P
C = 64
HN = 64
RW_GN_EPS = 64e-5
DECAY = math.exp(-0.5)
GATE_LORA = 160
N_EXP = 8
FE = 3584
EJ = FE // 512

QN = 32
LEVELS = (2, 4, 8, 16)

RS = 2048
RN = 6
ERN = 7

ROWS = {}


def _rows():
    at = 0
    for tile, names in enumerate([
        [("mod_b0", 48), ("mod_b1", 48)],
        [("ln_g", 32), ("ln_b", 32), ("hy_b_in", 24), ("hy_conv_b", 24)],
        [("hy_conv_w", 72), ("hy_b_out", 8), ("rw_mu", 48)],
        [("rw_w0", 16), ("rw_a0", 16), ("rw_k_k", 8), ("rw_k_a", 8), ("rw_r_k", 8), ("rw_lnx_g", 8),
         ("rw_lnx_b", 8), ("c", 8), ("c_ctx", 8)],
    ]):
        at = 0
        for name, n in names:
            ROWS[name] = (tile, at, n)
            at += n
    return ROWS


_rows()
ROW_FILL = [96, 112, 128, 88]


def constants():
    f64 = np.float64
    i = np.arange(P)
    ident = np.eye(P)
    mean = np.full((P, P), 1.0 / D)
    same_head = (i[:, None] // HN == i[None, :] // HN).astype(f64)
    common = np.concatenate([ident, mean, same_head, same_head / HN, np.ones((P, P)),
                             np.tile(np.arange(N_EXP), (P, 1)), i[:, None] < i[None, :], np.tile(i, (P, 1))], 1)

    L = SEQ
    t = np.arange(L, dtype=f64)
    w = 2 * np.pi * (np.arange(L) + 0.5) / (2 * L)
    ang = t[:, None] * w[None, :]
    fwd = np.concatenate([np.cos(ang), -np.sin(ang)], 1)
    fwd = fwd.reshape(2, P, 2 * L).transpose(1, 0, 2).reshape(P, -1)
    inv = np.concatenate([np.cos(ang).T, -np.sin(ang).T], 0) / L
    inv = inv.reshape(4, P, L).transpose(1, 0, 2).reshape(P, -1)
    t01 = np.arange(L, dtype=np.float32) / np.float32(max(L - 1, 1))
    bands = np.linspace(1e-4, HY_BANDS - 1, HY_BANDS, dtype=np.float32)
    a32 = (np.float32(2.0 * math.pi / L) * np.arange(L, dtype=np.float32)[:, None] * bands[None, :]).astype(f64)
    feats = np.zeros((P, L))
    feats[:HY_EMB] = np.concatenate([t01[:, None], np.cos(a32), -np.sin(a32)], 1).T
    negt = np.zeros((P, L))
    negt[0] = -t01
    notfirst = (i > 0).astype(f64)[:, None]
    layer0 = np.concatenate([fwd, inv, feats, negt, notfirst], 1)

    row, col = i[:, None], i[None, :]
    block = row // C == col // C
    lower, upper = block & (col < row), block & (col > row)
    strict = [lower, upper]
    incl_t = [block & (row <= col), block & (row >= col)]

    in_row, in_col = i[:, None] % QN, np.arange(QN)[None, :]

    def level(b, after_rows):
        pair = in_row // (2 * b) == in_col // (2 * b)
        r2, c2 = in_row // b % 2, in_col // b % 2
        return pair & (r2 == 1) & (c2 == 0) if after_rows else pair & (r2 == 0) & (c2 == 1)

    pos = np.arange(T) % C
    reset = [np.tile(pos != 0, (P, 1)), np.tile(pos != C - 1, (P, 1))]
    layer1 = np.concatenate([*strict, *incl_t, *reset, row % HN == np.arange(HN)[None, :],
                             in_row == in_col, in_row > in_col, in_row < in_col, level(1, True), level(1, False)], 1)
    bits = np.concatenate([level(b, a) for b in LEVELS for a in (True, False)], 1)
    return (common.astype(np.float32), layer0.astype(np.float32), layer1.astype(np.float32),
            bits.astype(np.int32))


PER = dict(proj=8, k_copied=1, sg=2, rate=2, r_copied=1, v_copied=1, g_copied=1, ksq=1, ksum=1, kstd=1,
           vt_full=1, vt_ready=1, decayed=2, excl=2, e_incl=2, e_inv=2, e_excl=2, kk_ready=1, b_raw=2,
           a_t=2, b_t=2, k_t=2, r_t=2, tr_full=6, q_ready=4, bk_ready=4, sc=12, sc_taken=12, tri_ready=4, off_ready=4,
           y_full=20, y_ready=20, z_full=20, merged=20, z1_full=4, z1_ready=4, wu_full=4, wu_ready=4,
           m_full=2, n_full=2, g_full=2, mo_ready=2, nd_ready=2, gt_ready=2, y_local=2, st_full=12,
           st_ready=14, out_y=1, y_copied=1, gn_mean=1, gn_cent=1, gn_sq=1, gn_var=1, gn_std=1,
           bonus_in=1, bonus_full=1, pair_done=1, kk_raw=1, rate_used=2)


DVE_LINKS = 36


GROUPS = dict(gates=("sg", "rate"), exps=("e_incl", "e_inv", "e_excl"), decayed_all=("r_t", "k_t", "b_t", "a_t"),
              chunk_full=("m_full", "n_full", "g_full", "y_local"), chunk_taken=("mo_ready", "nd_ready", "gt_ready"))
IN_GROUP = {name: (group, n, len(names)) for group, names in GROUPS.items() for n, name in enumerate(names)}


def _expert_steps():
    pe, act, dve = [], [], []
    for j in range(EJ):
        pe += [f"gate{j}"] + [f"turned{j - 1}"] * (j > 0) + ["shares_turned"] * (j == 4) + [f"up{j}"]
        pe += [f"y{j - 1}"] * (j > 0)
        act += [f"silu{j}"] + [f"hidden{j - 1}"] * (j > 0) + ["shareT"] * (j == 4)
        dve += ["share"] * (j == 3) + [f"h{j}"] + ["pick"] * (j == 4)
    last = EJ - 1
    pe += [f"turned{last}", f"y{last}", "gathered"] + [f"spread{o}" for o in range(4)]
    act += [f"hidden{last}", "xg"]
    dve += ["yg0", "yg1"] + [f"added{o}" for o in range(4)]
    return dict(expert_products=pe, expert_copies=act, expert_vectors=dve)


STEPS = _expert_steps()


class Chain:

    def __init__(self, eng, sem):
        self.eng, self.sem, self.n, self.base, self.off = eng, sem, 0, 0, 0

    def __call__(self, ins):
        self.n += 1
        ins.then_inc(self.sem, 1)
        self.eng.wait_ge(self.sem, self.off + self.base + self.n)

    def enter(self, i, per):
        self.base, self.n, self.per, self.off = self.base + self.n, 0, per, i * per

    def leave(self, count):
        assert self.n == self.per, (self.n, self.per)
        self.base, self.n, self.off = self.base + count * self.per, 0, 0


class Ring:

    def __init__(self, eng, loaded):
        self.eng, self.loaded, self.n, self.it16, self.free = eng, loaded, 0, 0, {}

    def slot_to_load(self, done):
        slot, self.n = self.n % RN, self.n + 1
        if slot in self.free:
            self.eng.wait_ge(*self.free[slot])
        self.free[slot] = done
        return slot

    def loaded_slot(self):
        n, self.n = self.n, self.n + 1
        self.eng.wait_ge(self.loaded[n % RN], self.it16 + 16 * (n // RN + 1))
        return n % RN

    def load_loop(self, chunks, done, body):
        rounds = chunks // RN
        start = self.n
        for c in range(RN):
            body(c, self.slot_to_load(done(c)))
        with self.eng.Fori(1, rounds) as i:
            for j in range(RN):
                self.eng.wait_ge(*done((i - 1) * RN + j))
                body(i * RN + j, (start + j) % RN)
        for j in range(RN):
            self.free[(start + j) % RN] = done((rounds - 1) * RN + j)
        self.n = start + rounds * RN
        for c in range(rounds * RN, chunks):
            body(c, self.slot_to_load(done(c)))

    def read_loop(self, chunks, body):
        rounds, start = chunks // RN, self.n
        with self.eng.Fori(0, rounds) as i:
            self.it16 = i * 16
            for j in range(RN):
                body(i * RN + j)
        self.it16, self.n = 0, start + rounds * RN
        for c in range(rounds * RN, chunks):
            body(c)


def with_loop(eng, n, body):
    rounds, rest = divmod(n, RN)
    with eng.Fori(0, rounds) as i:
        for j in range(RN):
            body(i * RN + j, j)
    for j in range(rest):
        body(rounds * RN + j, j)


def build(nc, a, out, consts, upto=99, dump=None):
    ctx = ExitStack()
    with ctx, nc.allow_non_contiguous_dma(reason="a few short columns"):
        sems = {}

        def sem(name):
            name = IN_GROUP.get(name, (name,))[0]
            if name not in sems:
                sems[name] = ctx.enter_context(nc.semaphore(name))
            return sems[name]

        arena = ctx.enter_context(nc.sbuf_tensor("arena", [P, 53000], F32))
        bank = [ctx.enter_context(nc.psum_tensor(f"bank{i}", [P, 512], F32)) for i in range(8)]
        at = [0]

        def mark(n=None):
            if n is not None:
                at[0] = n
            return at[0]

        def sb(*shape):
            n = int(np.prod(shape))
            v = arena[:, at[0]:at[0] + n]
            at[0] += n
            assert at[0] <= 53000, at[0]
            if len(shape) == 2:
                v = v.rearrange("p (a b) -> p a b", b=shape[1])
            if len(shape) == 3:
                v = v.rearrange("p (a b c) -> p a b c", b=shape[1], c=shape[2])
            return v

        common = sb(7 * P + N_EXP)
        expert_no = common[:, 5 * P:5 * P + N_EXP]
        before, slot_no = common[:, 5 * P + N_EXP:6 * P + N_EXP], common[:, 6 * P + N_EXP:]
        ident, meanm, heads1, heads64, ones = (common[:, P * j:P * (j + 1)] for j in range(5))
        vec = sb(4 * P)
        modv = [sb(48, 2), sb(48, 2)]
        silu_c = sb(KT, 2)
        eps = sb(4)
        xt_at = mark()
        XT = sb(KT, T)
        table = mark()
        sb(3400)
        UT = sb(KT, T)
        ring_at = mark()
        ring = [sb(RS) for _ in range(RN)]
        work = mark()

        mark(table)
        fwd, inv = sb(2, T), sb(4, SEQ)
        feats, negt, notfirst = sb(SEQ), sb(SEQ), sb(1)
        hw1, hw2, hcol = sb(HY_W), sb(HY_W), sb(4)
        mark(work)
        X1, X2 = sb(KT, T), sb(KT, T)
        ZT = sb(NB, D)
        KSP = sb(8, D)
        tmp_at = mark()
        pad = [sb(2, SEQ + 2) for _ in range(2)]
        cv = [sb(T) for _ in range(2)]
        pr = [sb(T) for _ in range(4)]
        win = [sb(T) for _ in range(2)]
        gate_t = sb(T)
        cv_spare = sb(T)
        dec = KSP[:, 4:8, :].rearrange("p a b -> p (a b)")
        rows = KSP[:, 0:1, 0:512].rearrange("p a (r c) -> p (a r) c", c=P)
        xin = X2.rearrange("p a b -> p (a b)").rearrange("p (a b) -> p a b", b=D)
        skip = X1.rearrange("p a b -> p (a b)")[:, 0:2 * D]
        hargs = [X1[:, 4 + j, 0:SEQ] for j in range(4)]
        w3 = ZT.rearrange("p a b -> p (a b)")
        kcs = UT.rearrange("p a b -> p (a b)").rearrange("p (s t d) -> p s t d", s=2, t=2)
        Y = UT.rearrange("p a b -> p (a b)").rearrange("p (s f d) -> p s f d", s=2, f=4)
        mod_rows0 = X1.rearrange("p a b -> p (a b)")
        mod_rows0 = arena[:, work:work + 6 * D]
        mark(work)
        Hf = sb(FT * T)
        H = Hf.rearrange("p (f t) -> p f t", t=T)
        SQ = sb(KT, T)
        sil = [sb(T), sb(T)]
        rt = [sb(T), sb(T)]
        std, rstd = sb(T), sb(T)
        mod_rows1 = sb(6 * D)

        mark(table)
        strict, incl_t = [sb(P), sb(P)], [sb(P), sb(P)]
        reset = [sb(T), sb(T)]
        eye64 = sb(HN)
        eye32, strict32, join1 = sb(QN), [sb(QN), sb(QN)], [sb(QN), sb(QN)]
        bits_at = mark()
        bits = [[sb(QN).bitcast(I32) for _ in range(2)] for _ in LEVELS]
        mark(work)
        UP = sb(KT, 2, SEQ + 2)
        XX, XM = sb(KT, T), sb(KT, T)
        pair_end = mark()
        XK, XV, XR = sb(KT, T), sb(KT, T), sb(KT, SEQ)
        HW, HA, G1a, G1b = sb(T), sb(T), sb(SEQ), sb(SEQ)
        YT = sb(KT, SEQ)
        mark(ring_at)
        lw1, la1, lg1 = sb(KT, P), sb(KT, P), sb(KT, GATE_LORA)

        mark(table + 3400)
        wst = sb(3, KT, P)
        w2s, a2s, g2a, g2b = sb(P), sb(P), sb(P), sb(P)
        one_ka = sb(KT)
        mark(ring_at)
        Kf, KK, KS, Vf, Vt, Rf, Gf = sb(T), sb(T), sb(T), sb(T), sb(NB, P), sb(SEQ), sb(SEQ)
        At, Bt, Kt = ([sb(T), sb(T)] for _ in range(3))
        Rt = [sb(SEQ), sb(SEQ)]
        DC, KD = [sb(8), sb(8)], sb(SEQ)
        SG, AS = [sb(T), sb(T)], [sb(T), sb(T)]
        CS, EP, EN, EX = sb(T), sb(T), sb(T), sb(T)
        Btok, Ktok = sb(NB, P), sb(NB, P)
        App, Aoff, TMp, TTp, Yp = ([sb(NB, QN) for _ in range(2)] for _ in range(5))
        AakT = [sb(NB, P) for _ in range(2)]
        ARR = [sb(NB, P) for _ in range(2)]
        TT = [[sb(NB, P) for _ in range(2)] for _ in range(2)]
        Q = [sb(NB, P) for _ in range(2)]
        WU = [[t[d].rearrange("p (b c) -> p b c", c=P) for t in (At, Kt)] for d in range(2)]
        MO, ND = [sb(8, C) for _ in range(2)], [sb(8, C) for _ in range(2)]
        GT = [sb(SEQ) for _ in range(2)]
        ST = [sb(8, C) for _ in range(2)]
        YF, YS, YN = sb(SEQ), sb(SEQ), sb(SEQ)
        assert mark() <= pair_end, (mark(), pair_end)

        mark(table)
        XTOK = sb(2, D)
        rt_w, logit, mx, ixf, comb = sb(KT, N_EXP), sb(2, 8), sb(2, 8), sb(2, 8), sb(2, 8)
        ix = sb(16).bitcast(U32)
        hot, chosen, place = sb(2, 8), sb(2, 8), sb(2, 8)
        slots, shares = sb(2, 2 * N_EXP + 1), sb(2, 2 * N_EXP + 1)
        most = sb(1)
        passes = sb(1).bitcast(I32)
        w12 = sb(2, 4)
        stat = sb(2, 4)
        diag = [sb(P), sb(P)]
        assert mark() <= table + 3400
        mark(xt_at)
        UTOK = sb(2, D)
        HTOK = [sb(512), sb(512)]
        sil2 = [sb(512), sb(512)]
        assert mark() <= table
        mark(ring_at)
        ering = [sb(KT, 512) for _ in range(ERN)]
        OUT = sb(2, D)
        XG = sb(KT, P)
        HT = [sb(4, P), sb(4, P)]
        YG = sb(D)
        pick, share = sb(2, P), sb(2, P)
        shareT = sb(2, P)
        rowG, rowg, rowb = sb(D), sb(D), sb(D)
        assert mark() <= 53000

        def col(name, j):
            tile, first, n = ROWS[name]
            assert j < n
            return vec[:, tile * P + first + j:tile * P + first + j + 1]

        def mv(layer, chunk, k, s):
            return modv[layer][:, chunk * KT + k, 1 - s:2 - s]

        ring_start = [0, 24 + 16 + FT + 16]
        ffn_start = 24 + 16
        win_f = [gate_t, cv_spare]

        seg = [slice(0, SEQ), slice(SEQ, T)]

        def dcol(name, i):
            tile, first, n = ROWS[name]
            return vec[:, bass.ds(tile * P + first + i, 1)]

        def each4(m):
            return m.unsqueeze(1).to_broadcast([P, 4, P])

        def b4(b):
            return bank[b][:, :].rearrange("p (b c) -> p b c", b=4)

        def each4q(m):
            return m.unsqueeze(1).to_broadcast([m.shape[0], NB, QN])

        def quarter(q):
            return slice(QN * q, QN * q + QN)

        def packed(b):
            return bank[b][:, 0:P].rearrange("p (b c) -> p b c", b=NB)

        JOINED = (4, 6)

        def c4(b):
            return bank[b][:, 0:4 * C].rearrange("p (b c) -> p b c", b=4)

        def hd(h):
            return slice(HN * h, HN * h + HN)

        def waiter(eng, i):
            def w(name, c):
                if name in IN_GROUP:
                    _, n, size = IN_GROUP[name]
                    eng.wait_ge(sem(name), i * 2 * size + (c - 1) * size + n + 1)
                else:
                    eng.wait_ge(sem(name), i * PER[name] + c)
            return w

        def settle(eng):
            eng.sem_inc(sem("settled"), 1)

        def step(eng, steps, name, item):
            eng.wait_ge(sem(steps), (item + 1) * len(STEPS[steps]) + STEPS[steps].index(name) + 1)

        CHUNKS = [[0, 1, 2, 3, 4, 5, 6, 7], [3, 2, 1, 0, 7, 6, 5, 4]]

        block = ctx.enter_context(nc.Block())
        w_loaded = [sem(f"w_loaded{i}") for i in range(RN)]
        up_loaded = [sem(f"up_loaded{i}") for i in range(RN)]

        @block.sync
        def _(sp):
            ld = Ring(sp, w_loaded)

            def load(name, dst, src, n=16):
                sp.dma_start(dst, src).then_inc(sem(name), 16)

            load("ld_common", common, consts[0])
            for name in ROWS:
                tile, first, n = ROWS[name]
                src = {"mod_b0": a["mod_b"][0:1], "mod_b1": a["mod_b"][1:2], "c_ctx": a["c_ctx"],
                       "c": a["c"]}.get(name, a.get(name))
                flat = src
                if len(src.shape) == 2:
                    flat = src.rearrange("a b -> (a b)")
                if len(src.shape) == 3:
                    flat = src.rearrange("a b c -> (a b c)")
                load("ld_rows", rows[first:first + n, tile, :], flat.rearrange("(r p) -> r p", p=P))
            load("ld_x", xin[:, 0:2, :], a["ctx"][0].rearrange("(t p) d -> p t d", p=P))
            load("ld_x", xin[:, 2:4, :], a["x"][0].rearrange("(t p) d -> p t d", p=P))
            load("ld_table", arena[:, table:table + 2 * T + 4 * SEQ + 2 * SEQ + 1], consts[1])
            load("ld_filter", hw1[0:HY_EMB, :], a["hy_f_w1"])
            load("ld_filter", hw2[0:HY_W, :], a["hy_f_w2"])
            for j, s in enumerate([a["hy_f_b1"], a["hy_f_b2"], a["hy_f_freq"][0], a["hy_f_freq"][1]]):
                load("ld_filter", hcol[0:HY_W, j:j + 1], s.rearrange("(p o) -> p o", o=1))
            load("ld_filter", w3[0:HY_W, :], a["hy_f_w3"])
            load("ld_filter", dec[0:1, :], a["hy_decay"].rearrange("a (o b) -> o (a b)", o=1))
            load("ld_filter", skip[0:1, :], a["hy_skip"].rearrange("a (o b) -> o (a b)", o=1))

            def load_mod(layer):
                w = a["mod_w"][layer].rearrange("(k p) n -> p k n", p=P)
                ld.load_loop(24, lambda c: (sem("mod_full"), c + 1 + 24 * layer),
                             lambda c, s: sp.dma_start(ring[s].rearrange("p (k n) -> p k n", n=256),
                                                       w[:, :, bass.ds(c * 256, 256)]).then_inc(w_loaded[s], 16))

            def load_cols(w, n, name, first=0):
                w = w.rearrange("(k p) n -> p k n", p=P)
                for c in range(n):
                    s = ld.slot_to_load((sem(name), first + 2 * c + 2))
                    sp.dma_start(ring[s].rearrange("p (k n) -> p k n", n=256), w[:, :, c * 256:(c + 1) * 256])\
                        .then_inc(w_loaded[s], 16)

            load_mod(0)
            if upto >= 2:
                load_cols(a["hy_w_in"], 12, "proj_full")
                load_cols(a["hy_w_out"], 4, "out_full")
            if upto >= 3:
                w13 = a["ffn_w13"][0].rearrange("(k p) (h n) -> p k h n", p=P, h=2)

                def load13(f, s):
                    dst = ring[s].rearrange("p (h k n) -> p h k n", h=2, n=P)
                    sp.dma_start(dst[:, 0], w13[:, :, 0, bass.ds(f * P, P)]).then_inc(w_loaded[s], 16)
                    sp.dma_start(dst[:, 1], w13[:, :, 1, bass.ds(f * P, P)]).then_inc(up_loaded[s], 16)
                ld.load_loop(FT, lambda f: (sem("hidden_full"), f + 1), load13)
                w2 = a["ffn_w2"][0].rearrange("(g k p) n -> p g k n", p=P, g=2)
                for m in range(KT):
                    for g in range(2):
                        s = ld.slot_to_load((sem("out_full"), 8 + m + 1))
                        sp.dma_start(ring[s][:, 0:11 * P].rearrange("p (k n) -> p k n", n=P),
                                     w2[:, g, :, m * P:(m + 1) * P]).then_inc(w_loaded[s], 16)
                load_mod(1)
            if upto >= 4:
                sp.wait_ge(sem("long_taken"), 32)
                load("ld_table1", arena[:, table:bits_at], consts[2])
                load("ld_table1", arena[:, bits_at:bits_at + len(LEVELS) * 2 * QN].bitcast(I32), consts[3])
                sp.wait_ge(sem("mod_full"), 48)
                for d in range(2):
                    load("ld_lora", lw1[:, :, d * HN:(d + 1) * HN], a["rw_w1"][d].rearrange("(k p) n -> p k n", p=P))
                    load("ld_lora", la1[:, :, d * HN:(d + 1) * HN], a["rw_a1"][d].rearrange("(k p) n -> p k n", p=P))
                load("ld_lora", lg1, a["rw_g1"].rearrange("(k p) n -> p k n", p=P))
            if upto >= 5:
                wr = a["rw_w_rkv"].rearrange("j (k p) n -> p (j k) n", p=P)
                w2d = a["rw_w2"].rearrange("d r n -> (d r) n")
                a2d = a["rw_a2"].rearrange("d r n -> (d r) n")
                sp.wait_ge(sem("hidden_full"), FT)
                with sp.Fori(0, KT) as i:
                    sp.wait_ge(sem("stage_free"), i + 1)
                    cols = bass.ds(i * P, P)
                    sp.dma_start(wst.rearrange("p j k n -> p (j k) n"), wr[:, :, cols]).then_inc(sem("ld_pair"), 16)
                    sp.dma_start(w2s, w2d[:, cols]).then_inc(sem("ld_pair"), 16)
                    sp.dma_start(a2s, a2d[:, cols]).then_inc(sem("ld_pair"), 16)
                    sp.dma_start(g2a, a["rw_g2"][0:P, cols]).then_inc(sem("ld_pair"), 16)
                    sp.dma_start(g2b[0:GATE_LORA - P, :], a["rw_g2"][P:GATE_LORA, cols]).then_inc(sem("ld_pair"), 16)
            if upto >= 6:
                sp.wait_ge(sem("pair_done"), KT + 1)
                ld.free = {}
                load_cols(a["rw_w_out"], 4, "out_full", 16)
            if upto >= 7:
                load("ld_router", rt_w, a["moe_router"][0].rearrange("(k p) e -> p k e", p=P))
                w13 = a["moe_w13"][0].rearrange("e (k p) n -> p (e k) n", p=P)
                w2 = a["moe_w2"][0].rearrange("e (k p) n -> p (e k) n", p=P)
                n_passes = sp.alloc_register("n_passes")
                with sp.Fori(0, n_passes) as p:
                    with sp.Fori(0, N_EXP) as e:
                        for q in range(3 * EJ):
                            (j, r), (jb, rb) = divmod(q, 3), divmod((q - ERN) % (3 * EJ), 3)
                            step(sp, "expert_products", ("gate", "up", "y")[rb] + str(jb),
                                 p * N_EXP + e - (1 if q < ERN else 0))
                            if q == 2:
                                sp.wait_ge(sem("ln_done"), 24)
                                sp.wait_ge(sem("u_ready"), 3)
                            s = (q + 3) % ERN
                            if r < 2:
                                src = w13[:, bass.ds(e * KT, KT), r * FE + j * 512:r * FE + j * 512 + 512]
                                dst = ering[s]
                            else:
                                src = w2[:, bass.ds(e * (FE // P) + 4 * j, 4), :]
                                dst = ering[s].rearrange("p a b -> p (a b)").rearrange("p (a b) -> p a b", b=D)
                            sp.dma_start(dst, src).then_inc(sem(f"ew_loaded{s}"), 16)
                    sp.wait_ge(sem("passes_ready"), 1)
                    sp.reg_load(n_passes, passes[0:1, 0:1])
                for tt in range(2):
                    sp.wait_ge(sem("final"), tt + 1)
                    sp.dma_start(out[0, tt * P:(tt + 1) * P, :], OUT[:, tt, :]).then_inc(sem("stored"), 16)
                sp.wait_ge(sem("stored"), 32)
        @block.tensor
        def _(pe):
            rg = Ring(pe, w_loaded)
            pe.wait_ge(sem("ld_common"), 16)
            pe.wait_ge(sem("ld_rows"), 16 * len(ROWS))
            for j, n in enumerate(ROW_FILL):
                last = pe.transpose(bank[0][:, j * P:j * P + n], rows[0:n, j, :], ident[0:n, 0:n])
            last.then_inc(sem("rows_turned"), 1)
            pe.wait_ge(sem("ld_x"), 32)
            for k in range(KT):
                if k >= 4:
                    pe.wait_ge(sem("x_taken"), k - 3)
                for t in range(NB):
                    last = pe.transpose(bank[1 + k % 4][:, t * P:(t + 1) * P], xin[:, t, k * P:(k + 1) * P], ident)
                last.then_inc(sem("x_turned"), 1)

            pe.wait_ge(sem("ld_table"), 16)
            pe.wait_ge(sem("ld_filter"), 16 * 9)
            pe.matmul(bank[5][0:HY_W, 0:SEQ], hw1[0:HY_EMB, :], feats[0:HY_EMB, :], start=True, stop=True)\
                .then_inc(sem("sine_in"), 1)
            pe.wait_ge(sem("sine_out"), 1)
            pe.matmul(bank[6][0:HY_W, 0:SEQ], hw2[0:HY_W, :], hargs[2][0:HY_W, :], start=True, stop=True)\
                .then_inc(sem("sine_in"), 1)
            pe.wait_ge(sem("sine_out"), 2)
            pe.wait_ge(sem("decay_abs"), 1)
            pe.wait_ge(sem("x_taken"), 8)
            pe.wait_ge(sem("vec_ready"), 1)
            for n in range(2):
                for q in range(4):
                    g = 4 * n + q
                    half, tt = q // 2, q % 2
                    b = 4 * (g % 2)
                    if g >= 2:
                        pe.wait_ge(sem("filter_taken"), g - 1)
                    if g == 4:
                        pe.wait_ge(sem("spectrum_taken"), 8)
                    for j in range(2):
                        cs = slice((2 * n + j) * D + half * 512, (2 * n + j) * D + half * 512 + 512)
                        pe.matmul(bank[b + j][:, :], hargs[3][0:HY_W, tt * P:(tt + 1) * P], w3[0:HY_W, cs],
                                  start=True, stop=True)
                        last = pe.matmul(bank[b + 2 + j][:, :], negt[0:1, tt * P:(tt + 1) * P], dec[0:1, cs],
                                         start=True, stop=True)
                    last.then_inc(sem("filter_full"), 1)
                pe.wait_ge(sem("pool_taps"), 4 * (n + 1))
                pe.wait_ge(sem("taps_ready"), 4 * (n + 1))
                for o in range(8):
                    c, f, half = o // 4, o // 2 % 2, o % 2
                    for tt in range(2):
                        last = pe.matmul(bank[o][:, :], fwd[:, tt, c * SEQ + f * P:c * SEQ + (f + 1) * P],
                                         kcs[:, c, tt, half * 512:half * 512 + 512], start=(tt == 0), stop=(tt == 1))
                    last.then_inc(sem("spectrum_full"), 1)

            def modulation(layer):
                dst = [mod_rows0, mod_rows1][layer]
                pe.wait_ge(sem("silu_ready"), 1)
                if layer == 0:
                    pe.wait_ge(sem("spectrum_taken"), 16)
                base = 25 * layer

                def body(c):
                    s = rg.loaded_slot()
                    pe.wait_ge(sem("mod_taken"), c + 1 + 30 * layer)
                    w = ring[s].rearrange("p (k n) -> p k n", n=256)
                    for k in range(KT):
                        last = pe.matmul(bank[s][0:2, 0:256], silu_c[:, k, :], w[:, k, :], start=(k == 0),
                                         stop=(k == KT - 1))
                    last.then_inc(sem("mod_full"), 1)
                rg.read_loop(24, body)
                pe.wait_ge(sem("mod_taken"), 30 * (layer + 1))
                for j in range(48):
                    last = pe.transpose(bank[6][:, 2 * j:2 * j + 2], dst[0:2, j * P:(j + 1) * P], ident[0:2, 0:2])
                last.then_inc(sem("mod_turned"), 1)

            modulation(0)

            def layer_norm(n, width=T):
                cols = slice(T - width, T)
                pe.wait_ge(sem("residual_done"), 8 * n)
                for k in range(KT):
                    last = pe.matmul(bank[0][:, 0:width], meanm, XT[:, k, cols], start=(k == 0), stop=(k == KT - 1))
                last.then_inc(sem("ln_mean"), 1)
                for k in range(KT):
                    pe.wait_ge(sem("ln_square"), 8 * (n - 1) + k + 1)
                    last = pe.matmul(bank[1][:, 0:width], meanm, SQ[:, k, 0:width], start=(k == 0), stop=(k == KT - 1))
                last.then_inc(sem("ln_var"), 1)

            if upto >= 2:
                pe.wait_ge(sem("u_ready"), 1)

                def turn_v(m):
                    pe.wait_ge(sem("conv_done"), m + 1)
                    if m >= 2:
                        pe.wait_ge(sem("v_taken"), m - 1)
                    for t in range(NB):
                        last = pe.transpose(bank[4 + m % 2][:, t * P:(t + 1) * P], cv[m % 2][:, t * P:(t + 1) * P], ident)
                    last.then_inc(sem("v_turned"), 1)

                for m in range(24):
                    if m % 2 == 0:
                        s = rg.loaded_slot()
                    if m >= 4:
                        pe.wait_ge(sem("proj_taken"), m - 3)
                    w = ring[s].rearrange("p (k n) -> p k n", n=256)[:, :, (m % 2) * P:(m % 2 + 1) * P]
                    for k in range(KT):
                        last = pe.matmul(bank[m % 4][:, :], w[:, k, :], UT[:, k, :], start=(k == 0), stop=(k == KT - 1))
                    last.then_inc(sem("proj_full"), 1)
                    if 1 <= m <= KT:
                        turn_v(m - 1)
                for n in range(2):
                    X = [X1, X2][n]
                    if n == 0:
                        pe.wait_ge(sem("v_taken"), 8)
                        pe.wait_ge(sem("conv_done"), 24)
                    else:
                        for k in range(KT):
                            if k >= 4:
                                pe.wait_ge(sem("z_taken"), k - 3)
                            for t in range(NB):
                                last = pe.transpose(bank[k % 4][:, t * P:(t + 1) * P], X1[:, k, t * P:(t + 1) * P], ident)
                            last.then_inc(sem("z_turned"), 1)
                        pe.wait_ge(sem("z_taken"), 8)
                    def forward(g):
                        half, s = g // 2, g % 2
                        if g + 4 * n >= 1:
                            pe.wait_ge(sem("bins_taken"), g + 4 * n)
                        for f in range(4):
                            for tt in range(2):
                                last = pe.matmul(bank[f][:, :], fwd[:, tt, f * P:(f + 1) * P],
                                                 ZT[:, 2 * s + tt, half * 512:half * 512 + 512],
                                                 start=(tt == 0), stop=(tt == 1))
                        last.then_inc(sem("bins_full"), 1)

                    def inverse(g):
                        half, s = g // 2, g % 2
                        pe.wait_ge(sem("product_ready"), 4 * n + g + 1)
                        for ct in range(4):
                            if 16 * n + 4 * g + ct >= 4:
                                pe.wait_ge(sem("long_taken"), 16 * n + 4 * g + ct - 3)
                            for f in range(4):
                                last = pe.matmul(bank[4 + ct][:, 0:SEQ], Y[:, g % 2, f, ct * P:(ct + 1) * P],
                                                 inv[:, f, :], start=(f == 0), stop=(f == 3))
                            last.then_inc(sem("long_full"), 1)

                    for g in range(5):
                        if g < 4:
                            forward(g)
                        if g >= 1:
                            inverse(g - 1)
                    pe.wait_ge(sem("long_taken"), 16 * (n + 1))
                for m in range(KT):
                    if m % 2 == 0:
                        s = rg.loaded_slot()
                    if m >= 4:
                        pe.wait_ge(sem("residual_done"), m - 3)
                    w = ring[s].rearrange("p (k n) -> p k n", n=256)[:, :, (m % 2) * P:(m % 2 + 1) * P]
                    for k in range(KT):
                        last = pe.matmul(bank[m % 4][:, :], w[:, k, :], X2[:, k, :], start=(k == 0), stop=(k == KT - 1))
                    last.then_inc(sem("out_full"), 1)
                layer_norm(1)
            if upto >= 3:
                pe.wait_ge(sem("u_ready"), 2)

                def hidden(f):
                    s = rg.loaded_slot()
                    b = 2 * (s % 2)
                    pe.wait_ge(up_loaded[s], rg.it16 + 16 * ((rg.n - 1 - ffn_start) // RN + 1))
                    pe.wait_ge(sem("hidden_taken"), f + 1)
                    w = ring[s].rearrange("p (h k n) -> p h k n", h=2, n=P)
                    for h in range(2):
                        for k in range(KT):
                            last = pe.matmul(bank[b + h][:, :], w[:, h, k, :], UT[:, k, :], start=(k == 0),
                                             stop=(k == KT - 1))
                    last.then_inc(sem("hidden_full"), 1)
                rg.read_loop(FT, hidden)
                pe.wait_ge(sem("hidden_taken"), FT + 2)
                for m in range(KT):
                    if m >= 4:
                        pe.wait_ge(sem("residual_done"), 8 + m - 3)
                    for g in range(2):
                        s = rg.loaded_slot()
                        w = ring[s][:, 0:11 * P].rearrange("p (k n) -> p k n", n=P)
                        for k in range(11):
                            last = pe.matmul(bank[4 + m % 4][:, :], w[:, k, :], H[:, 11 * g + k, :],
                                             start=(g + k == 0), stop=(g == 1 and k == 10))
                    last.then_inc(sem("out_full"), 1)
                pe.wait_ge(sem("residual_done"), 16)
                modulation(1)
                layer_norm(2)
            if upto >= 4:
                pe.wait_ge(sem("ld_lora"), 16 * 5)
                pe.wait_ge(sem("xm_ready"), 1)
                for k in range(KT):
                    last = pe.matmul(bank[0][:, :], lw1[:, k, :], XM[:, k, :], start=(k == 0), stop=(k == KT - 1))
                last.then_inc(sem("lora_full"), 1)
                pe.wait_ge(sem("xm_ready"), 2)
                for k in range(KT):
                    last = pe.matmul(bank[1][:, :], la1[:, k, :], XM[:, k, :], start=(k == 0), stop=(k == KT - 1))
                last.then_inc(sem("lora_full"), 1)
                pe.wait_ge(sem("xm_ready"), 3)
                for r0, r1 in ((0, P), (P, GATE_LORA)):
                    b = bank[2 + r0 // P]
                    for k in range(KT):
                        last = pe.matmul(b[0:r1 - r0, 0:SEQ], lg1[:, k, r0:r1], XM[:, k, 0:SEQ], start=(k == 0),
                                         stop=(k == KT - 1))
                last.then_inc(sem("lora_full"), 1)
            if upto >= 5:
                pe.sem_inc(sem("stage_free"), 1)
                pe.wait_ge(sem("lora_taken"), 4)
                pe.wait_ge(sem("ld_table1"), 32)
                with pe.Fori(0, KT) as i:
                    w = waiter(pe, i)
                    mm = pe.matmul
                    pe.wait_ge(sem("ld_pair"), i * 80 + 80)
                    w("pair_done", 1)
                    for k in range(KT):
                        last = mm(bank[0][:, :], wst[:, 1, k, :], XK[:, k, :], start=(k == 0), stop=(k == KT - 1))
                    last.then_inc(sem("proj"), 1)
                    for d in range(2):
                        r = hd(d)
                        mm(bank[3 + d][:, :], w2s[r, :], HW[r, :], start=True, stop=True).then_inc(sem("proj"), 1)
                        mm(bank[5 + d][:, :], a2s[r, :], HA[r, :], start=True, stop=True).then_inc(sem("proj"), 1)
                    for k in range(KT):
                        last = mm(bank[2][:, 0:SEQ], wst[:, 0, k, :], XR[:, k, :], start=(k == 0), stop=(k == KT - 1))
                    last.then_inc(sem("proj"), 1)
                    w("k_copied", 1)
                    w("ksq", 1)
                    mm(bank[0][:, :], heads1, KS, start=True, stop=True).then_inc(sem("ksum"), 1)
                    for k in range(KT):
                        last = mm(bank[1][:, :], wst[:, 2, k, :], XV[:, k, :], start=(k == 0), stop=(k == KT - 1))
                    last.then_inc(sem("proj"), 1)
                    mm(bank[7][:, 0:SEQ], g2a, G1a, start=True, stop=False)
                    mm(bank[7][:, 0:SEQ], g2b[0:32, :], G1b[0:32, :], start=False, stop=True).then_inc(sem("proj"), 1)
                    w("v_copied", 1)
                    for b in range(NB):
                        last = pe.transpose(bank[1][:, b * P:(b + 1) * P], Vf[:, b * P:(b + 1) * P], ident)
                    last.then_inc(sem("vt_full"), 1)
                    pe.wait_ge(sem("proj"), i * 8 + 8)
                    pe.sem_inc(sem("stage_free"), 1)
                    w("sg", 2)
                    w("rate", 2)
                    w("r_copied", 1)
                    w("g_copied", 1)
                    w("vt_ready", 1)
                    w("kstd", 1)
                    for d in range(2):
                        for j, (src, name) in enumerate(((At, "a_t"), (Bt, "b_t"), (Kt, "k_t"))):
                            w(name, d + 1)
                            if d == 1:
                                (w("z1_ready", 2), w("wu_ready", 2), w("mo_ready", 1), w("nd_ready", 1), w("gt_ready", 1))
                            for b in range(NB):
                                last = pe.transpose(bank[2 + j][:, b * P:(b + 1) * P], src[d][:, b * P:(b + 1) * P], ident)
                            last.then_inc(sem("tr_full"), 1)
                        w("r_t", d + 1)
                        for kind in range(3):
                            for h in range(2):
                                r = hd(h)
                                if kind == 2 and h == 0:
                                    w("q_ready", 2 * d + 2)
                                    w("bk_ready", 2 * d + 2)
                                ps = bank[(0, 5, 2)[kind] + h]
                                for b in range(NB):
                                    cs = slice(b * P, b * P + P)
                                    rs = slice((b % 2) * P, (b % 2) * P + P)
                                    if kind == 0:
                                        lhs, rhs = At[d][r, cs], Bt[d][r, cs]
                                    elif kind == 1:
                                        lhs, rhs = Kt[d][r, cs], At[d][r, cs]
                                    else:
                                        src = (Bt, Kt)[b // 2][d]
                                        lhs, rhs = src[r, SEQ + rs.start:SEQ + rs.stop], Rt[d][r, rs]
                                    last = mm(ps[:, cs], lhs, rhs, start=True, stop=True)
                                last.then_inc(sem("sc"), 1)
                        for lv in range(len(LEVELS)):
                            n0 = 10 * d + 2 * lv
                            for h in range(2):
                                if lv == 0:
                                    w("tri_ready", 2 * d + h + 1)
                                    w("off_ready", 2 * d + h + 1)
                                else:
                                    w("merged", n0 + h - 1)
                                settle(pe)
                                for b in range(NB):
                                    for q in range(4):
                                        last = mm(bank[h][quarter(q), b * QN:b * QN + QN], App[h][quarter(q), b, :],
                                                  TTp[h][quarter(q), b, :], start=True, stop=True)
                                last.then_inc(sem("y_full"), 1)
                            if lv == 0:
                                w("sc_taken", 6 * d + 4)
                                for h in range(2):
                                    for b in range(NB):
                                        last = mm(bank[5][:, (NB * h + b) * C:(NB * h + b + 1) * C], AakT[h][:, b, :],
                                                  Vt[:, b, hd(h)], start=True, stop=True)
                                    last.then_inc(sem("z1_full"), 1)
                            for h in range(2):
                                w("y_ready", n0 + h + 1)
                                settle(pe)
                                for b in range(NB):
                                    for q in range(4):
                                        last = mm(bank[JOINED[h]][quarter(q), b * QN:b * QN + QN], Yp[h][quarter(q), b, :],
                                                  TMp[h][quarter(q), b, :], start=True, stop=True)
                                last.then_inc(sem("z_full"), 1)
                        for h in range(2):
                            w("merged", 10 * d + 7 + h)
                            settle(pe)
                            for b in range(NB):
                                for s_ in range(2):
                                    late, early = quarter(2 * s_ + 1 - d), quarter(2 * s_ + d)
                                    last = mm(bank[h][early, b * QN:b * QN + QN], Aoff[h][late, b, :], TTp[h][late, b, :],
                                              start=True, stop=True)
                            last.then_inc(sem("y_full"), 1)
                        for h in range(2):
                            w("y_ready", 10 * d + 9 + h)
                            settle(pe)
                            for b in range(NB):
                                for s_ in range(2):
                                    early = quarter(2 * s_ + d)
                                    last = mm(bank[JOINED[h]][early, b * QN:b * QN + QN], TMp[h][early, b, :],
                                              Yp[h][early, b, :], start=True, stop=True)
                            last.then_inc(sem("z_full"), 1)
                        w("z1_ready", 2 * d + 2)
                        w("sc_taken", 6 * d + 6)
                        for h in range(2):
                            w("merged", 10 * d + 9 + h)
                            for b in range(NB):
                                last = mm(bank[2 + h][:, b * P:b * P + P], TT[d][h][:, b, :], Q[h][:, b, :],
                                          start=True, stop=True)
                            last.then_inc(sem("wu_full"), 1)
                        w("wu_ready", 2 * d + 2)
                        settle(pe)
                        for h in range(2):
                            for c in range(8):
                                b, r = c // 2, hd(c % 2)
                                last = mm(bank[4 + c % 2][hd(h), b * C:b * C + C], WU[d][h][r, b, 0:C], Btok[r, b, hd(h)],
                                          start=True, stop=True)
                        last.then_inc(sem("m_full"), 1)
                        for h in range(2):
                            for c in range(8):
                                b, r = c // 2, hd(c % 2)
                                mm(bank[c % 2][hd(h), b * C:b * C + C], Ktok[r, b, hd(h)], Vt[r, b, hd(h)],
                                   start=True, stop=False, skip_group_check=True)
                                last = mm(bank[c % 2][hd(h), b * C:b * C + C], Btok[r, b, hd(h)], WU[d][h][r, b, C:P],
                                          start=False, stop=True, skip_group_check=True)
                        last.then_inc(sem("n_full"), 1)
                        for h in range(2):
                            for b in range(2):
                                last = mm(bank[6][hd(h), b * P:b * P + P], WU[d][h][:, 2 + b, 0:C], ARR[h][:, b, :],
                                          start=True, stop=True)
                        last.then_inc(sem("g_full"), 1)
                        for h in range(2):
                            for b in range(2):
                                mm(bank[7][hd(h), b * P:b * P + P], Vt[:, 2 + b, hd(h)], ARR[h][:, 2 + b, :],
                                   start=(d == 0 and b == 0), stop=False, skip_group_check=True)
                                last = mm(bank[7][hd(h), b * P:b * P + P], WU[d][h][:, 2 + b, C:P], ARR[h][:, b, :],
                                          start=False, stop=False, skip_group_check=True)
                        last.then_inc(sem("y_local"), 1)
                    w("mo_ready", 2)
                    for st in range(1, 8):
                        for d in range(2):
                            c = CHUNKS[d][st]
                            w("st_ready", 2 * (st - 1) + d + 1)
                            settle(pe)
                            if st < 7:
                                for h in range(2):
                                    last = mm(bank[d][hd(h), 0:C], MO[d][hd(h), c, :], ST[d][hd(h), st, :],
                                              start=True, stop=True)
                                last.then_inc(sem("st_full"), 1)
                            if st >= 4:
                                if st == 4 and d == 0:
                                    w("gt_ready", 2)
                                    settle(pe)
                                x = (c - 4) * C
                                for h in range(2):
                                    last = mm(bank[7][hd(h), x:x + C], ST[d][hd(h), st, :], GT[d][hd(h), x:x + C],
                                              start=False, stop=(st == 7 and d == 1), skip_group_check=True)
                    last.then_inc(sem("out_y"), 1)
                    w("bonus_in", 1)
                    mm(bank[2][:, 0:SEQ], heads1, KD, start=True, stop=True).then_inc(sem("bonus_full"), 1)
                    w("y_copied", 1)
                    mm(bank[0][:, 0:SEQ], heads64, YF, start=True, stop=True).then_inc(sem("gn_mean"), 1)
                    w("gn_sq", 1)
                    mm(bank[1][:, 0:SEQ], heads64, YS, start=True, stop=True).then_inc(sem("gn_var"), 1)
                pe.wait_ge(sem("pair_done"), KT + 1)
            if upto >= 6:
                for m in range(KT):
                    if m % 2 == 0:
                        s = rg.loaded_slot()
                    if m >= 4:
                        pe.wait_ge(sem("residual_done"), 16 + m - 3)
                    w_ = ring[s].rearrange("p (k n) -> p k n", n=256)[:, :, (m % 2) * P:(m % 2 + 1) * P]
                    for k in range(KT):
                        last = pe.matmul(bank[m % 4][:, seg[1]], w_[:, k, :], YT[:, k, :], start=(k == 0), stop=(k == KT - 1))
                    last.then_inc(sem("out_full"), 1)
                layer_norm(3, SEQ)
            if upto >= 7:
                pe.wait_ge(sem("ld_router"), 16)
                pe.wait_ge(sem("u_ready"), 3)
                for tt in range(2):
                    cs = slice(SEQ + tt * P, SEQ + tt * P + P)
                    for k in range(KT):
                        last = pe.matmul(bank[0][:, tt * 8:tt * 8 + 8], UT[:, k, cs], rt_w[:, k, :],
                                         start=(k == 0), stop=(k == KT - 1))
                last.then_inc(sem("logits_full"), 1)
                for tt in range(2):
                    for k in range(KT):
                        last = pe.transpose(bank[1 + 2 * tt + k // 4][:, (k % 4) * P:(k % 4) * P + P],
                                            XT[:, k, SEQ + tt * P:SEQ + tt * P + P], ident)
                last.then_inc(sem("tok_full"), 1)
                for tt in range(2):
                    for k in range(KT):
                        b = (5, 6, 7, 1)[2 * tt + k // 4]
                        if b == 1 and k == 4:
                            last.then_inc(sem("tok_full"), 1)
                            pe.wait_ge(sem("tok_taken"), 1)
                        last = pe.transpose(bank[b][:, (k % 4) * P:(k % 4) * P + P],
                                            UT[:, k, SEQ + tt * P:SEQ + tt * P + P], ident)
                last.then_inc(sem("tok_full"), 1)
                pe.wait_ge(sem("chosen_ready"), 1)
                places = bank[0][:, 16:40]
                pe.matmul(places[:, 0:8], before, chosen[:, 0, :], start=True, stop=True)
                pe.matmul(places[:, 8:16], ones, chosen[:, 0, :], start=True, stop=False)
                pe.matmul(places[:, 8:16], before, chosen[:, 1, :], start=False, stop=True)
                pe.matmul(places[:, 16:24], ones, chosen[:, 0, :], start=True, stop=False)
                pe.matmul(places[:, 16:24], ones, chosen[:, 1, :], start=False, stop=True).then_inc(sem("places_full"), 1)
                for n in range(24):
                    pe.wait_ge(sem("diag_ready"), n + 1)
                    if n == 0:
                        pe.wait_ge(sem("tok_taken"), 8)
                    pe.matmul(bank[2 + n // 4][:, (n % 4) * P:(n % 4) * P + P], ones, diag[n % 2],
                              start=True, stop=True).then_inc(sem("row_full"), 1)
                pe.wait_ge(sem("row_taken"), 6)

                def gather(item):
                    step(pe, "expert_vectors", "pick", item - 1)
                    for k in range(KT):
                        for tt in range(2):
                            last = pe.matmul(bank[6 + k // 4][:, (k % 4) * P:(k % 4) * P + P],
                                             UTOK[:, tt, k * P:(k + 1) * P], pick[:, tt, :], start=(tt == 0), stop=(tt == 1))
                    last.then_inc(sem("expert_products"), 1)

                def loaded(q, item):
                    s = (q + 3) % ERN
                    before_ = sum((c + 3) % ERN == s for c in range(q))
                    pe.wait_ge(sem(f"ew_loaded{s}"), 48 * item + 16 * (before_ + 1))
                    return ering[s]

                def hidden_products(j, r, item):
                    w_ = loaded(3 * j + r, item)
                    b = 2 * (j % 2) + r
                    if j == 0 and r == 0:
                        step(pe, "expert_copies", "xg", item - 1)
                    if j < 2:
                        step(pe, "expert_vectors", f"added{b}", item - 1)
                    else:
                        step(pe, "expert_vectors", f"h{j - 2}", item)
                    for k in range(KT):
                        last = pe.matmul(bank[b][:, :], XG[:, k, :], w_[:, k, :], start=(k == 0), stop=(k == KT - 1))
                    last.then_inc(sem("expert_products"), 1)

                def turn_hidden(j, item):
                    step(pe, "expert_vectors", f"h{j}", item)
                    if j:
                        step(pe, "expert_copies", f"hidden{j - 1}", item)
                    for f in range(4):
                        last = pe.transpose(bank[6][:, f * P:f * P + P], HTOK[j % 2][:, f * P:f * P + P], ident)
                    last.then_inc(sem("expert_products"), 1)

                def down_products(j, item):
                    w_ = loaded(3 * j + 2, item).rearrange("p a b -> p (a b)").rearrange("p (a b) -> p a b", b=D)
                    step(pe, "expert_copies", f"hidden{j}", item)
                    for f in range(4):
                        for half in range(2):
                            last = pe.matmul(bank[4 + half][:, :], HT[j % 2][:, f, :], w_[:, f, half * 512:half * 512 + 512],
                                             start=(j == 0 and f == 0), stop=(j == EJ - 1 and f == 3))
                    last.then_inc(sem("expert_products"), 1)

                first = STEPS["expert_products"].index("gathered")
                pe.sem_inc(sem("expert_products"), first)
                gather(0)
                step(pe, "expert_copies", "xg", -1)
                pe.sem_inc(sem("expert_products"), len(STEPS["expert_products"]) - first - 1)
                pe.wait_ge(sem("passes_ready"), 1)
                n_passes = pe.value_load(passes[0:1, 0:1], min_val=1, max_val=2)
                with pe.Fori(0, n_passes) as p:
                    with pe.Fori(0, N_EXP) as e:
                        item = p * N_EXP + e
                        for j in range(EJ):
                            hidden_products(j, 0, item)
                            if j:
                                turn_hidden(j - 1, item)
                            if j == 4:
                                step(pe, "expert_vectors", "share", item)
                                for tt in range(2):
                                    last = pe.transpose(bank[7][:, tt * P:tt * P + P], share[:, tt, :], ident)
                                last.then_inc(sem("expert_products"), 1)
                            hidden_products(j, 1, item)
                            if j:
                                down_products(j - 1, item)
                        turn_hidden(EJ - 1, item)
                        down_products(EJ - 1, item)
                        gather(item + 1)
                        for o in range(4):
                            tt, half = divmod(o, 2)
                            if o < 2:
                                step(pe, "expert_vectors", f"yg{half}", item)
                            pe.matmul(bank[o][:, :], shareT[:, tt, :], YG[:, half * 512:half * 512 + 512],
                                      start=True, stop=True).then_inc(sem("expert_products"), 1)

        @block.scalar
        def _(act):
            link = Chain(act, sem("act_chain"))
            pe_x = sem("x_turned")
            act.wait_ge(sem("vec_ready"), 1)
            link(act.activation(silu_c[:, :, 0], vec[:, 3 * P + 72:3 * P + 80], ACT.Silu))
            act.activation(silu_c[:, :, 1], vec[:, 3 * P + 80:3 * P + 88], ACT.Silu).then_inc(sem("silu_ready"), 1)
            for k in range(KT):
                act.wait_ge(pe_x, k + 1)
                act.copy(XT[:, k, :], bank[1 + k % 4][:, :]).then_inc(sem("x_taken"), 1)
            act.wait_ge(sem("ld_filter"), 16 * 9)
            act.activation(dec[0:1, :], dec[0:1, :], ACT.Abs).then_inc(sem("decay_abs"), 1)
            for j in range(2):
                act.wait_ge(sem("sine_arg"), j + 1)
                act.activation(hargs[2 + j][0:HY_W, :], hargs[1][0:HY_W, :], ACT.Sin).then_inc(sem("sine_out"), 1)
            for n in range(2):
                for q in range(4):
                    g = 4 * n + q
                    act.wait_ge(sem("filter_full"), g + 1)
                    if g >= 1:
                        act.wait_ge(sem("filter_taken"), g)
                    for j in range(2):
                        act.activation(win_f[j], bank[4 * (g % 2) + 2 + j][:, :], ACT.Exp).then_inc(sem("window"), 1)
                for o in range(8):
                    act.wait_ge(sem("spectrum_full"), 8 * n + o + 1)
                    c, f, half = o // 4, o // 2 % 2, o % 2
                    act.copy(KSP[:, 4 * n + 2 * c + f, half * 512:half * 512 + 512], bank[o][:, :])\
                        .then_inc(sem("spectrum_taken"), 1)

            def modulation(layer):
                dst = [mod_rows0, mod_rows1][layer]
                act.sem_inc(sem("mod_taken"), 6)

                def round_(c0, j):
                    act.wait_ge(sem("mod_full"), c0 + j + 1 + 24 * layer)
                    b = (ring_start[layer] + j) % RN
                    act.copy(dst[0:2, bass.ds((c0 + j) * 256, 256)], bank[b][0:2, 0:256]).then_inc(sem("mod_taken"), 1)
                with act.Fori(0, 4) as i:
                    for j in range(RN):
                        round_(i * RN, j)
            modulation(0)

            def layer_norm(n, layer, j, width=T):
                cols = slice(T - width, T)
                for k in range(KT):
                    act.wait_ge(sem("ln_centred"), 8 * (n - 1) + k + 1)
                    act.activation(SQ[:, k, 0:width], XT[:, k, cols], ACT.Square).then_inc(sem("ln_square"), 1)
                act.wait_ge(sem("ln_var"), n)
                act.activation(std[:, 0:width], bank[1][:, 0:width], ACT.Sqrt, bias=eps[:, 0:1]).then_inc(sem("ln_std"), 1)
                for k in range(KT):
                    act.wait_ge(sem("ln_scaled"), 8 * (n - 1) + k + 1)
                    act.activation(XT[:, k, cols], XT[:, k, cols], ACT.Identity,
                                   bias=col("ln_b", (2 * layer + j) * KT + k)).then_inc(sem("ln_done"), 1)

            if upto >= 2:
                for m in range(24):
                    act.wait_ge(sem("proj_full"), m + 1)
                    if m >= 2:
                        act.wait_ge(sem("conv_done"), m - 1)
                    act.activation(pad[m % 2][:, :, 1:SEQ + 1], bank[m % 4][:, :].rearrange("p (s t) -> p s t", s=2),
                                   ACT.Identity, bias=col("hy_b_in", m)).then_inc(sem("proj_taken"), 1)
                    if 1 <= m <= KT:
                        act.wait_ge(sem("v_turned"), m)
                        act.copy(ZT[:, :, (m - 1) * P:m * P], bank[4 + (m - 1) % 2][:, :].rearrange("p (t c) -> p t c", t=NB))\
                            .then_inc(sem("v_taken"), 1)
                for k in range(KT):
                    act.wait_ge(sem("z_turned"), k + 1)
                    act.copy(ZT[:, :, k * P:(k + 1) * P], bank[k % 4][:, :].rearrange("p (t c) -> p t c", t=NB))\
                        .then_inc(sem("z_taken"), 1)
                layer_norm(1, 0, 0)
            if upto >= 3:
                with_loop(act, FT, lambda f, j: (
                    act.wait_ge(sem("hidden_full"), f + 1),
                    act.wait_ge(sem("sil_free"), f + 1),
                    act.activation(sil[j % 2], bank[2 * ((ffn_start + j) % 2)][:, :], ACT.Silu)
                    .then_inc(sem("sil_ready"), 1)))
                modulation(1)
                layer_norm(2, 0, 1)
            if upto >= 4:
                act.wait_ge(sem("lora_full"), 1)
                act.activation(HW, bank[0][:, :], ACT.Tanh).then_inc(sem("lora_taken"), 1)
                act.wait_ge(sem("lora_full"), 2)
                act.copy(HA, bank[1][:, :]).then_inc(sem("lora_taken"), 1)
                act.wait_ge(sem("lora_full"), 3)
                act.activation(G1a, bank[2][:, 0:SEQ], ACT.Sigmoid).then_inc(sem("lora_taken"), 1)
                act.activation(G1b[0:32, :], bank[3][0:32, 0:SEQ], ACT.Sigmoid).then_inc(sem("lora_taken"), 1)
            if upto >= 5:
                with act.Fori(0, KT) as i:
                    w = waiter(act, i)
                    w("proj", 1)
                    w("pair_done", 1)
                    act.copy(Kf, bank[0][:, :]).then_inc(sem("k_copied"), 1)
                    for d in range(2):
                        w("proj", 2 * d + 2)
                        act.activation(SG[d], bank[3 + d][:, :], ACT.Sigmoid, bias=dcol("rw_w0", i + 8 * d))\
                            .then_inc(sem("sg"), 1)
                        w("proj", 2 * d + 3)
                        act.activation(AS[d], bank[5 + d][:, :], ACT.Sigmoid, bias=dcol("rw_a0", i + 8 * d))\
                            .then_inc(sem("rate"), 1)
                    for d in range(2):
                        if d == 1:
                            w("proj", 6)
                            act.copy(Rf, bank[2][:, 0:SEQ]).then_inc(sem("r_copied"), 1)
                            w("ksum", 1)
                            act.activation(KS, bank[0][:, :], ACT.Sqrt, bias=eps[:, 2:3]).then_inc(sem("kstd"), 1)
                            w("proj", 7)
                            act.copy(Vf, bank[1][:, :]).then_inc(sem("v_copied"), 1)
                            w("proj", 8)
                            act.copy(Gf, bank[7][:, 0:SEQ]).then_inc(sem("g_copied"), 1)
                            w("vt_full", 1)
                            act.copy(Vt, b4(1)).then_inc(sem("vt_ready"), 1)
                        w("decayed", d + 1)
                        if d == 1:
                            w("k_t", 1)
                            w("r_t", 1)
                        act.activation(EP, CS, ACT.Exp, scale=-DECAY).then_inc(sem("e_incl"), 1)
                        act.activation(EN, CS, ACT.Exp, scale=DECAY).then_inc(sem("e_inv"), 1)
                        w("excl", d + 1)
                        act.activation(EX, SG[d], ACT.Exp, scale=-DECAY).then_inc(sem("e_excl"), 1)
                    for d in range(2):
                        w("tr_full", 3 * d + 1)
                        for h in range(2):
                            if d == 1:
                                w("wu_full", h + 1)
                            act.copy(Q[h][:, :, 0:C], b4(2)[:, :, hd(h)]).then_inc(sem("q_ready"), 1)
                        w("tr_full", 3 * d + 2)
                        if d == 1:
                            w("n_full", 1)
                        act.copy(Btok, b4(3)).then_inc(sem("bk_ready"), 1)
                        w("tr_full", 3 * d + 3)
                        act.copy(Ktok, b4(4)).then_inc(sem("bk_ready"), 1)
                        for h in range(2):
                            w("sc_taken", 6 * d + h + 1)
                            for s_ in range(2):
                                late, early = quarter(2 * s_ + 1 - d), quarter(2 * s_ + d)
                                last = act.copy(Aoff[h][late, :, :], b4(h)[late, :, early])
                            last.then_inc(sem("off_ready"), 1)
                        for n in range(10 * d + 1, 10 * d + 11):
                            h = (n - 1) % 2
                            w("y_full", n)
                            if n > 2:
                                w("z_full", n - 2)
                            act.copy(Yp[h], packed(h)).then_inc(sem("y_ready"), 1)
                            if n == 10 * d + 2:
                                w("z1_full", 2 * d + 2)
                                for g in range(2):
                                    act.copy(Q[g][:, :, C:P], bank[5][:, g * NB * C:(g + 1) * NB * C]
                                             .rearrange("p (b c) -> p b c", b=NB)).then_inc(sem("z1_ready"), 1)
                        for h in range(2):
                            w("wu_full", 2 * d + h + 1)
                            act.copy(WU[d][h], b4(2 + h)).then_inc(sem("wu_ready"), 1)
                    w("out_y", 1)
                    act.copy(YF, bank[7][:, 0:SEQ]).then_inc(sem("y_copied"), 1)
                    w("gn_cent", 1)
                    act.activation(YS, YN, ACT.Square).then_inc(sem("gn_sq"), 1)
                    w("gn_var", 1)
                    act.activation(YS, bank[1][:, 0:SEQ], ACT.Sqrt, bias=eps[:, 1:2]).then_inc(sem("gn_std"), 1)
            if upto >= 6:
                layer_norm(3, 1, 0, SEQ)
            if upto >= 7:
                act.wait_ge(sem("tok_full"), 1)
                for tt in range(2):
                    for h in range(2):
                        act.copy(XTOK[:, tt, h * 512:h * 512 + 512], bank[1 + 2 * tt + h][:, :]).then_inc(sem("tok_taken"), 1)
                act.wait_ge(sem("gap"), 1)
                act.activation(w12[:, :, 1:2], w12[:, :, 0:1], ACT.Exp).then_inc(sem("gap_exp"), 1)
                for tt in range(2):
                    for h in range(2):
                        act.wait_ge(sem("tok_full"), 2 if 2 * tt + h < 3 else 3)
                        act.copy(UTOK[:, tt, h * 512:h * 512 + 512], bank[(5, 6, 7, 1)[2 * tt + h]][:, :])\
                            .then_inc(sem("tok_taken"), 1)
                for n in range(6):
                    act.wait_ge(sem("row_full"), 4 * n + 4)
                    row = (rowG, rowg, rowb)[n // 2]
                    act.copy(row[:, (n % 2) * 512:(n % 2) * 512 + 512], bank[2 + n][:, :]).then_inc(sem("row_taken"), 1)

                def copy_gathered(item):
                    step(act, "expert_products", "gathered", item - 1)
                    for g in range(2):
                        last = act.copy(XG[:, 4 * g:4 * g + 4, :].rearrange("p a b -> p (a b)"), bank[6 + g][:, :])
                    last.then_inc(sem("expert_copies"), 1)

                def copy_hidden(j, item):
                    step(act, "expert_products", f"turned{j}", item)
                    act.copy(HT[j % 2].rearrange("p a b -> p (a b)"), bank[6][:, :]).then_inc(sem("expert_copies"), 1)

                act.sem_inc(sem("expert_copies"), len(STEPS["expert_copies"]) - 1)
                copy_gathered(0)
                act.wait_ge(sem("passes_ready"), 1)
                n_passes = act.value_load(passes[0:1, 0:1], min_val=1, max_val=2)
                with act.Fori(0, n_passes) as p:
                    with act.Fori(0, N_EXP) as e:
                        item = p * N_EXP + e
                        for j in range(EJ):
                            step(act, "expert_products", f"gate{j}", item)
                            step(act, "expert_vectors", f"h{(j - 2) % EJ}", item - (1 if j < 2 else 0))
                            act.activation(sil2[j % 2], bank[2 * (j % 2)][:, :], ACT.Silu).then_inc(sem("expert_copies"), 1)
                            if j:
                                copy_hidden(j - 1, item)
                            if j == 4:
                                step(act, "expert_products", "shares_turned", item)
                                act.copy(shareT.rearrange("p a b -> p (a b)"), bank[7][:, 0:2 * P])\
                                    .then_inc(sem("expert_copies"), 1)
                        copy_hidden(EJ - 1, item)
                        copy_gathered(item + 1)
                for tt in range(2):
                    act.wait_ge(sem("fin_centred"), tt + 1)
                    act.activation(XTOK[:, tt, :], OUT[:, tt, :], ACT.Square, accum_out=stat[:, tt, 1:2])\
                        .then_inc(sem("fin_square"), 1)
                    act.wait_ge(sem("fin_square"), tt + 1)
                    act.activation(stat[:, tt, 2:3], stat[:, tt, 1:2], ACT.Sqrt, bias=eps[:, 0:1], scale=1.0 / D)\
                        .then_inc(sem("fin_std"), 1)

        @block.gpsimd
        def _(pool):
            for n in range(2):
                for q in range(4):
                    g = 4 * n + q
                    half, tt = q // 2, q % 2
                    pool.wait_ge(sem("taps"), g + 1)
                    if q == 0 and n == 1:
                        pool.wait_ge(sem("spectrum_full"), 8)
                    cs = slice(half * 512, half * 512 + 512)
                    pool.tensor_tensor(kcs[:, 0, tt, cs], pr[0], pr[1], ALU.add).then_inc(sem("pool_taps"), 1)
                    pool.tensor_tensor(kcs[:, 1, tt, cs], pr[0], pr[1], ALU.subtract).then_inc(sem("taps_ready"), 1)
            if upto >= 2:
                for g in range(8):
                    for f in range(2):
                        pool.wait_ge(sem("bins_mult"), 4 * g + 2 * f + 1)
                        if f == 0 and g >= 2:
                            pool.wait_ge(sem("long_full"), 4 * (g - 1))
                        pool.tensor_tensor(Y[:, g % 2, f, :], pr[0], pr[1], ALU.subtract).then_inc(sem("pool_re"), 1)
                        pool.wait_ge(sem("bins_mult"), 4 * g + 2 * f + 2)
                        pool.tensor_tensor(Y[:, g % 2, 2 + f, :], pr[2], pr[3], ALU.add)\
                            .then_inc(sem("pool_im"), 1)
                    pool.wait_ge(sem("pool_re"), 2 * g + 2)
                    pool.wait_ge(sem("pool_im"), 2 * g + 2)
                    pool.sem_inc(sem("product_ready"), 1)
            if upto >= 5:
                pool.wait_ge(sem("ld_table1"), 32)
                with pool.Fori(0, KT) as i:
                    w = waiter(pool, i)
                    w("kk_raw", 1)
                    pool.tensor_tensor(KS, KK, KK, ALU.mult).then_inc(sem("ksq"), 1)
                    for d in range(2):
                        w("decayed", d + 1)
                        pool.tensor_tensor(SG[d], CS, SG[d], ALU.subtract).then_inc(sem("excl"), 1)
                        w("kk_ready", 1)
                        w("rate_used", d + 1)
                        pool.tensor_tensor(AS[d], KK, AS[d], ALU.mult).then_inc(sem("b_raw"), 1)

        @block.vector
        def _(dve):
            link = Chain(dve, sem("dve_chain"))
            link(dve.memset(eps[:, 0:1], LN_EPS))
            link(dve.memset(eps[:, 1:2], RW_GN_EPS))
            link(dve.memset(eps[:, 2:3], 1e-6))
            link(dve.memset(eps[:, 3:4], 0.0))
            dve.wait_ge(sem("rows_turned"), 1)
            for j, n in enumerate(ROW_FILL):
                last = dve.tensor_copy(vec[:, j * P:j * P + n], bank[0][:, j * P:j * P + n])
            last.then_inc(sem("vec_ready"), 1)
            dve.wait_ge(sem("ld_filter"), 16 * 9)
            dve.wait_ge(sem("ld_table"), 16)
            magic = float(1.5 * 2 ** 23)
            for j in range(2):
                dve.wait_ge(sem("sine_in"), j + 1)
                arg, t = hargs[0][0:HY_W, :], hargs[1][0:HY_W, :]
                if j == 1:
                    dve.wait_ge(sem("sine_out"), 1)
                link(dve.tensor_scalar(arg, bank[5 + j][0:HY_W, 0:SEQ], hcol[0:HY_W, j:j + 1],
                                       hcol[0:HY_W, 2 + j:3 + j], ALU.add, ALU.mult))
                link(dve.tensor_scalar(t, arg, 1.0 / (2 * math.pi), magic, ALU.mult, ALU.add))
                link(dve.tensor_scalar(t, t, magic, None, ALU.subtract))
                link(dve.scalar_tensor_tensor(out=arg, in0=t, scalar=-6.28125, in1=arg, op0=ALU.mult, op1=ALU.add))
                link(dve.scalar_tensor_tensor(out=arg, in0=t, scalar=-(2 * math.pi - 6.28125), in1=arg,
                                              op0=ALU.mult, op1=ALU.add))
                dve.tensor_scalar(t, arg, -3.1415925, 3.1415925, ALU.max, ALU.min).then_inc(sem("sine_arg"), 1)
            for n in range(2):
                for q in range(4):
                    g = 4 * n + q
                    half, tt = q // 2, q % 2
                    b = 4 * (g % 2)
                    dve.wait_ge(sem("window"), 2 * g + 2)
                    if g >= 1:
                        dve.wait_ge(sem("taps_ready"), g)
                        dve.wait_ge(sem("pool_taps"), g)
                    link(dve.tensor_tensor(pr[0], bank[b][:, :], win_f[0], ALU.mult))
                    if tt == 0:
                        link(dve.tensor_tensor(pr[0][0:1, :], pr[0][0:1, :],
                                               skip[0:1, n * D + half * 512:n * D + half * 512 + 512], ALU.add))
                        link(dve.scalar_tensor_tensor(out=pr[1], in0=bank[b + 1][:, :], scalar=notfirst,
                                                      in1=win_f[1], op0=ALU.mult, op1=ALU.mult))
                    else:
                        link(dve.tensor_tensor(pr[1], bank[b + 1][:, :], win_f[1], ALU.mult))
                    dve.sem_inc(sem("taps"), 1)
                    dve.sem_inc(sem("filter_taken"), 1)

            def modulation(layer):
                dve.wait_ge(sem("mod_turned"), layer + 1)
                name = f"mod_b{layer}"
                tile, first, n = ROWS[name]
                bias = vec[:, tile * P + first:tile * P + first + n]
                ps = bank[6][:, 0:96].rearrange("p (j s) -> p j s", s=2)
                for s in range(2):
                    link(dve.tensor_tensor(modv[layer][:, :, s], ps[:, :, s], bias, ALU.add))
                for ch in (1, 4):
                    v = modv[layer][:, ch * KT:(ch + 1) * KT, :]
                    link(dve.tensor_scalar(v, v, 1.0, None, ALU.add))
            modulation(0)

            def modulate(layer, first, streams=(0, 1)):
                for k in range(KT):
                    for s in streams:
                        last = dve.tensor_scalar(UT[:, k, seg[s]], XT[:, k, seg[s]], mv(layer, first + 1, k, s),
                                                 mv(layer, first, k, s), ALU.mult, ALU.add)
                last.then_inc(sem("u_ready"), 1)

            def layer_norm(n, layer, j, width=T):
                cols = slice(T - width, T)
                dve.wait_ge(sem("ln_mean"), n)
                for k in range(KT):
                    dve.tensor_tensor(XT[:, k, cols], XT[:, k, cols], bank[0][:, 0:width], ALU.subtract)\
                        .then_inc(sem("ln_centred"), 1)
                dve.wait_ge(sem("ln_std"), n)
                dve.wait_ge(sem("ln_centred"), 8 * n)
                link(dve.reciprocal(rstd[:, 0:width], std[:, 0:width]))
                for k in range(KT):
                    dve.scalar_tensor_tensor(out=XT[:, k, cols], in0=XT[:, k, cols],
                                             scalar=col("ln_g", (2 * layer + j) * KT + k), in1=rstd[:, 0:width],
                                             op0=ALU.mult, op1=ALU.mult).then_inc(sem("ln_scaled"), 1)
                dve.wait_ge(sem("ln_done"), 8 * n)

            def residual(n, layer, gate, bias, b0, streams=(0, 1)):
                for m in range(KT):
                    dve.wait_ge(sem("out_full"), 8 * (n - 1) + m + 1)
                    t = rt[m % 2]
                    for s in streams:
                        g = mv(layer, gate, m, s)
                        ps = bank[b0 + m % 4][:, seg[s]]
                        if bias:
                            link(dve.tensor_scalar(t[:, seg[s]], ps, col(bias, m), g, ALU.add, ALU.mult))
                        else:
                            link(dve.tensor_scalar(t[:, seg[s]], ps, g, None, ALU.mult))
                    c = slice(SEQ * streams[0], T)
                    dve.scalar_tensor_tensor(out=XT[:, m, c], in0=XT[:, m, c], scalar=float(ALPHA), in1=t[:, c],
                                             op0=ALU.mult, op1=ALU.add).then_inc(sem("residual_done"), 1)

            if upto >= 2:
                dve.wait_ge(sem("spectrum_full"), 16)
                modulate(0, 0)
                for p_ in pad:
                    link(dve.memset(p_[:, :, 0:1], 0.0))
                    link(dve.memset(p_[:, :, SEQ + 1:SEQ + 2], 0.0))
                for m in range(24):
                    dve.wait_ge(sem("proj_taken"), m + 1)
                    dst = (cv[m % 2] if m < 8 else X1[:, m - 8, :] if m < 16 else X2[:, m - 16, :])
                    dst = dst.rearrange("p (s t) -> p s t", s=2)
                    pd = pad[m % 2]
                    if 2 <= m < 8:
                        dve.wait_ge(sem("v_turned"), m - 1)
                    link(dve.tensor_scalar(dst, pd[:, :, 1:SEQ + 1], col("hy_conv_w", 24 + m), col("hy_conv_b", m),
                                           ALU.mult, ALU.add))
                    link(dve.scalar_tensor_tensor(out=dst, in0=pd[:, :, 0:SEQ], scalar=col("hy_conv_w", m), in1=dst,
                                                  op0=ALU.mult, op1=ALU.add))
                    dve.scalar_tensor_tensor(out=dst, in0=pd[:, :, 2:SEQ + 2], scalar=col("hy_conv_w", 48 + m), in1=dst,
                                             op0=ALU.mult, op1=ALU.add).then_inc(sem("conv_done"), 1)
                dve.wait_ge(sem("conv_done"), 24)

                def products(n, g):
                    half, s = g // 2, g % 2
                    cs = slice(half * 512, half * 512 + 512)
                    dve.wait_ge(sem("bins_full"), 4 * n + g + 1)
                    for f in range(2):
                        re, im = bank[f][:, :], bank[2 + f][:, :]
                        kr, ki = KSP[:, 4 * n + f, cs], KSP[:, 4 * n + 2 + f, cs]
                        u = 2 * (4 * n + g) + f
                        if u >= 1:
                            dve.wait_ge(sem("pool_re"), u)
                        dve.tensor_tensor(pr[0], re, kr, ALU.mult)
                        link(dve.tensor_tensor(pr[1], im, ki, ALU.mult))
                        dve.sem_inc(sem("bins_mult"), 1)
                        if u >= 1:
                            dve.wait_ge(sem("pool_im"), u)
                        dve.tensor_tensor(pr[2], re, ki, ALU.mult)
                        link(dve.tensor_tensor(pr[3], im, kr, ALU.mult))
                        dve.sem_inc(sem("bins_mult"), 1)
                    dve.sem_inc(sem("bins_taken"), 1)

                def gating(n, g):
                    half, s = g // 2, g % 2
                    X = [X1, X2][n]
                    for ct in range(4):
                        dve.wait_ge(sem("long_full"), 16 * n + 4 * g + ct + 1)
                        x = X[:, 4 * half + ct, seg[s]]
                        dve.tensor_tensor(x, x, bank[4 + ct][:, 0:SEQ], ALU.mult).then_inc(sem("long_taken"), 1)

                for n in range(2):
                    for g in range(5):
                        if g < 4:
                            products(n, g)
                        if g >= 1:
                            gating(n, g - 1)
                residual(1, 0, 2, "hy_b_out", 0)
                layer_norm(1, 0, 0)
            if upto >= 3:
                modulate(0, 3)
                dve.sem_inc(sem("hidden_taken"), 2)
                dve.sem_inc(sem("sil_free"), 2)

                def hid(f, j):
                    dve.wait_ge(sem("sil_ready"), f + 1)
                    dve.tensor_tensor(Hf[:, bass.ds(f * T, T)], sil[j % 2],
                                      bank[2 * ((ffn_start + j) % 2) + 1][:, :], ALU.mult).then_inc(sem("hidden_mult"), 1)
                    dve.wait_ge(sem("hidden_mult"), f + 1)
                    dve.sem_inc(sem("hidden_taken"), 1)
                    dve.sem_inc(sem("sil_free"), 1)
                with_loop(dve, FT, hid)
                residual(2, 0, 5, None, 4)
                modulation(1)
                layer_norm(2, 0, 1)
            if upto >= 4:
                for k in range(KT):
                    for s in range(2):
                        dve.tensor_scalar(UP[:, k, s, 1:SEQ + 1], XT[:, k, seg[s]], mv(1, 1, k, s), mv(1, 0, k, s),
                                          ALU.mult, ALU.add)
                link(dve.memset(UP[:, :, :, 0:1], 0.0))
                link(dve.memset(UP[:, :, :, SEQ + 1:SEQ + 2], 0.0))

                def two(v):
                    return v.rearrange("p (s t) -> p s t", s=2)
                for k in range(KT):
                    dve.tensor_tensor(two(XX[:, k, :]), UP[:, k, :, 0:SEQ], UP[:, k, :, 2:SEQ + 2], ALU.add)
                link(dve.memset(eps[:, 3:4], 0.0))
                for k in range(KT):
                    last = dve.scalar_tensor_tensor(out=two(XX[:, k, :]), in0=two(XX[:, k, :]), scalar=0.5,
                                                    in1=UP[:, k, :, 1:SEQ + 1], op0=ALU.mult, op1=ALU.subtract)
                link(last)

                def mix(dst, j):
                    for k in range(KT):
                        last = dve.scalar_tensor_tensor(out=two(dst[:, k, :]), in0=two(XX[:, k, :]),
                                                        scalar=col("rw_mu", j * KT + k), in1=UP[:, k, :, 1:SEQ + 1],
                                                        op0=ALU.mult, op1=ALU.add)
                    return last

                def mix_x(dst, j):
                    for k in range(KT):
                        last = dve.scalar_tensor_tensor(out=dst[:, k, 0:SEQ], in0=XX[:, k, seg[1]],
                                                        scalar=col("rw_mu", j * KT + k), in1=UP[:, k, 1, 1:SEQ + 1],
                                                        op0=ALU.mult, op1=ALU.add)
                    return last
                mix(XM, 1).then_inc(sem("xm_ready"), 1)
                mix(XK, 2)
                dve.wait_ge(sem("lora_full"), 1)
                mix(XM, 4).then_inc(sem("xm_ready"), 1)
                mix(XV, 3)
                dve.wait_ge(sem("lora_full"), 2)
                mix_x(XM, 5).then_inc(sem("xm_ready"), 1)
                link(mix_x(XR, 0))
                tile, first, n = ROWS["rw_k_a"]
                link(dve.tensor_scalar(one_ka, vec[:, tile * P + first:tile * P + first + n], -1.0, 1.0, ALU.mult, ALU.add))
                dve.wait_ge(sem("lora_full"), 3)
                for d in range(2):
                    for h in range(2):
                        last = dve.memset(TT[d][h], 0.0)
                link(last)
                dve.sem_inc(sem("pair_done"), 1)
            if upto >= 5:
                dve.wait_ge(sem("ld_table1"), 32)
                with dve.Fori(0, KT) as i:
                    w = waiter(dve, i)
                    link.enter(i, DVE_LINKS)
                    w("k_copied", 1)
                    dve.tensor_scalar(KK, Kf, dcol("rw_k_k", i), None, ALU.mult).then_inc(sem("kk_raw"), 1)
                    for d in range(2):
                        w("sg", d + 1)
                        if d == 1:
                            w("e_inv", 1)
                            w("excl", 1)
                        if d == 0:
                            dve.tensor_tensor_scan(CS, reset[0], SG[0], 0.0, ALU.mult, ALU.add).then_inc(sem("decayed"), 1)
                        else:
                            dve.tensor_tensor_scan(CS[:, ::-1], reset[1][:, ::-1], SG[1][:, ::-1], 0.0, ALU.mult,
                                                   ALU.add).then_inc(sem("decayed"), 1)
                        w("rate", d + 1)
                        dve.tensor_scalar(Kt[d], AS[d], dcol("rw_k_a", i), one_ka[:, bass.ds(i, 1)], ALU.mult, ALU.add)\
                            .then_inc(sem("rate_used"), 1)
                        w("rate_used", d + 1)
                        link(dve.tensor_tensor(Kt[d], Kt[d], Kf, ALU.mult))
                        if d == 0:
                            link(dve.tensor_copy(KD, Kt[0][:, seg[1]]))
                        else:
                            link(dve.tensor_tensor(KD, KD, Kt[1][:, seg[1]], ALU.add))
                        if d == 0:
                            w("kstd", 1)
                            link(dve.reciprocal(KS, KS))
                            w("kk_raw", 1)
                            dve.tensor_tensor(KK, KK, KS, ALU.mult).then_inc(sem("kk_ready"), 1)
                            w("kk_ready", 1)
                        w("e_incl", d + 1)
                        w("r_copied", 1)
                        last_col = C - 1 if d == 0 else 0
                        link(dve.tensor_copy(DC[d], EP.rearrange("p (c t) -> p c t", t=C)[:, :, last_col]))
                        dve.tensor_tensor(Rt[d], Rf, EP[:, seg[1]], ALU.mult).then_inc(sem("r_t"), 1)
                        w("e_inv", d + 1)
                        dve.tensor_tensor(Kt[d], Kt[d], EN, ALU.mult).then_inc(sem("k_t"), 1)
                        w("b_raw", d + 1)
                        dve.tensor_tensor(Bt[d], AS[d], EN, ALU.mult).then_inc(sem("b_t"), 1)
                        w("e_excl", d + 1)
                        dve.scalar_tensor_tensor(out=At[d], in0=KK, scalar=-1.0, in1=EX, op0=ALU.mult, op1=ALU.mult)\
                            .then_inc(sem("a_t"), 1)
                        w("b_t", d + 1)
                        w("k_t", d + 1)
                        w("r_t", d + 1)
                        w("a_t", d + 1)
                    link(dve.tensor_tensor(KD, KD, Rf, ALU.mult))
                    dve.tensor_scalar(KD, KD, dcol("rw_r_k", i), None, ALU.mult).then_inc(sem("bonus_in"), 1)
                    for d in range(2):
                        for h in range(2):
                            w("sc", 6 * d + h + 1)
                            for q in range(4):
                                r = quarter(q)
                                last = dve.tensor_tensor(App[h][r, :, :], b4(h)[r, :, r], each4q(strict32[d][r, :]), ALU.mult)
                            last.then_inc(sem("sc_taken"), 1)
                            w("sc_taken", 6 * d + h + 1)
                            link(dve.tensor_tensor(TMp[h], App[h], each4q(join1[d]), ALU.mult))
                            link(dve.tensor_tensor(TMp[h], TMp[h], each4q(eye32), ALU.add))
                            dve.transpose(TTp[h].rearrange("p b c -> p (b c)"), TMp[h].rearrange("p b c -> p (b c)"))\
                                .then_inc(sem("tri_ready"), 1)
                        for h in range(2):
                            w("sc", 6 * d + 3 + h)
                            dve.tensor_tensor(AakT[h], b4(5 + h), each4(strict[1 - d]), ALU.mult)\
                                .then_inc(sem("sc_taken"), 1)
                        for h in range(2):
                            w("sc", 6 * d + 5 + h)
                            dve.tensor_tensor(ARR[h], b4(2 + h), each4(incl_t[d]), ALU.mult)\
                                .then_inc(sem("sc_taken"), 1)
                        for lv in range(len(LEVELS)):
                            for h in range(2):
                                n = 10 * d + 2 * lv + h + 1
                                w("z_full", n)
                                settle(dve)
                                link(dve.copy_predicated(TMp[h], each4q(bits[lv][d]), packed(JOINED[h])))
                                dve.transpose(TTp[h].rearrange("p b c -> p (b c)"), TMp[h].rearrange("p b c -> p (b c)"))\
                                    .then_inc(sem("merged"), 1)
                        for h in range(2):
                            w("merged", 10 * d + 7 + h)
                            for q in range(4):
                                r = quarter(q)
                                dve.tensor_copy(TT[d][h][r, :, r], TTp[h][r, :, :])
                        for h in range(2):
                            w("z_full", 10 * d + 9 + h)
                            for s_ in range(2):
                                late, early = quarter(2 * s_ + 1 - d), quarter(2 * s_ + d)
                                last = dve.tensor_copy(TT[d][h][early, :, late], packed(JOINED[h])[early, :, :])
                            last.then_inc(sem("merged"), 1)
                        w("m_full", d + 1)
                        for o in range(2):
                            last = dve.tensor_tensor(MO[d][:, o::2, :], c4(4 + o), eye64.unsqueeze(1).to_broadcast([P, 4, C]),
                                                     ALU.add)
                        last.then_inc(sem("mo_ready"), 1)
                        w("n_full", d + 1)
                        for o in range(2):
                            last = dve.tensor_tensor(ND[d][:, o::2, :], c4(o),
                                                     DC[d][:, o::2].unsqueeze(2).to_broadcast([P, 4, C]), ALU.mult)
                        last.then_inc(sem("nd_ready"), 1)
                        w("g_full", d + 1)
                        dve.tensor_tensor(GT[d], bank[6][:, 0:SEQ], Rt[d], ALU.add).then_inc(sem("gt_ready"), 1)
                    w("nd_ready", 2)
                    for d in range(2):
                        dve.tensor_copy(ST[d][:, 1, :], ND[d][:, CHUNKS[d][0], :]).then_inc(sem("st_ready"), 1)
                    for st in range(1, 7):
                        for d in range(2):
                            c = CHUNKS[d][st]
                            w("st_full", 2 * (st - 1) + d + 1)
                            dve.scalar_tensor_tensor(out=ST[d][:, st + 1, :], in0=bank[d][:, 0:C], scalar=DC[d][:, c:c + 1],
                                                     in1=ND[d][:, c, :], op0=ALU.mult, op1=ALU.add)\
                                .then_inc(sem("st_ready"), 1)
                    w("bonus_full", 1)
                    link(dve.tensor_tensor(KD, bank[2][:, 0:SEQ], Vf[:, seg[1]], ALU.mult))
                    w("gn_mean", 1)
                    dve.tensor_tensor(YN, YF, bank[0][:, 0:SEQ], ALU.subtract).then_inc(sem("gn_cent"), 1)
                    w("gn_cent", 1)
                    w("gn_std", 1)
                    link(dve.reciprocal(YS, YS))
                    link(dve.scalar_tensor_tensor(out=YN, in0=YN, scalar=dcol("rw_lnx_g", i), in1=YS, op0=ALU.mult,
                                                  op1=ALU.mult))
                    link(dve.scalar_tensor_tensor(out=YN, in0=YN, scalar=dcol("rw_lnx_b", i), in1=KD, op0=ALU.add,
                                                  op1=ALU.add))
                    dve.tensor_tensor(YT.rearrange("p k t -> p (k t)")[:, bass.ds(i * SEQ, SEQ)], YN, Gf, ALU.mult)\
                        .then_inc(sem("pair_done"), 1)
                    w("pair_done", 2)
                link.leave(KT)
            if upto >= 6:
                residual(3, 1, 2, None, 0, streams=(1,))
                layer_norm(3, 1, 0, SEQ)
            if upto >= 7:
                modulate(1, 3, streams=(1,))
                dve.wait_ge(sem("logits_full"), 1)
                lg = bank[0][:, 0:16].rearrange("p (t e) -> p t e", t=2)
                dve.tensor_copy(logit, lg).then_inc(sem("logits_taken"), 1)
                dve.wait_ge(sem("logits_taken"), 1)
                for tt in range(2):
                    link(dve.max(mx[:, tt, :], logit[:, tt, :]))
                    link(dve.max_index(ix.rearrange("p (t e) -> p t e", t=2)[:, tt, :],
                                       mx[:, tt, :], logit[:, tt, :]))
                link(dve.tensor_copy(ixf.rearrange("p t e -> p (t e)"), ix))
                dve.tensor_tensor(w12[:, :, 0:1], mx[:, :, 1:2], mx[:, :, 0:1], ALU.subtract).then_inc(sem("gap"), 1)
                dve.wait_ge(sem("gap_exp"), 1)
                link(dve.tensor_scalar(w12[:, :, 0:1], w12[:, :, 1:2], 1.0, None, ALU.add))
                link(dve.reciprocal(w12[:, :, 2:3], w12[:, :, 0:1]))
                link(dve.tensor_tensor(w12[:, :, 3:4], w12[:, :, 2:3], w12[:, :, 1:2], ALU.mult))
                for tt in range(2):
                    link(dve.tensor_scalar(comb[:, tt, :], expert_no, ixf[:, tt, 0:1], w12[:, tt, 2:3], ALU.is_equal, ALU.mult))
                    link(dve.tensor_scalar(hot[:, tt, :], expert_no, ixf[:, tt, 1:2], w12[:, tt, 3:4], ALU.is_equal, ALU.mult))
                    link(dve.tensor_tensor(comb[:, tt, :], comb[:, tt, :], hot[:, tt, :], ALU.add))
                    link(dve.tensor_scalar(hot[:, tt, :], expert_no, ixf[:, tt, 0:1], None, ALU.is_equal))
                    link(dve.scalar_tensor_tensor(out=chosen[:, tt, :], in0=expert_no, scalar=ixf[:, tt, 1:2],
                                                  in1=hot[:, tt, :], op0=ALU.is_equal, op1=ALU.add))
                dve.sem_inc(sem("chosen_ready"), 1)
                dve.memset(slots, -1.0)
                dve.memset(shares, 0.0)
                dve.wait_ge(sem("places_full"), 1)
                link(dve.scalar_tensor_tensor(out=place, in0=bank[0][:, 16:32].rearrange("p (t e) -> p t e", t=2), scalar=1.0,
                                              in1=chosen, op0=ALU.add, op1=ALU.mult))
                for q in range(2):
                    dve.tensor_copy(shares[:, :, q * N_EXP:(q + 1) * N_EXP], comb)
                    last = dve.tensor_scalar(slots[:, :, q * N_EXP:(q + 1) * N_EXP], place, 1.0 + q * P, None, ALU.subtract)
                link(last)
                link(dve.tensor_reduce(most, bank[0][:, 32:40], AXX, ALU.max))
                dve.tensor_scalar(passes, most, float(P), 1.0, ALU.is_gt, ALU.add).then_inc(sem("passes_ready"), 1)

                def choose(item):
                    for tt in range(2):
                        last = dve.tensor_scalar(pick[:, tt, :], slot_no, slots[:, tt, bass.ds(item, 1)], None, ALU.is_equal)
                    last.then_inc(sem("expert_vectors"), 1)
                first = STEPS["expert_vectors"].index("pick")
                dve.sem_inc(sem("expert_vectors"), first)
                choose(0)
                for n in range(24):
                    k = n % 8
                    c_ = (mv(1, 5, k, 1), col("ln_g", 24 + k), col("ln_b", 24 + k))[n // 8]
                    if n >= 2:
                        dve.wait_ge(sem("row_full"), n - 1)
                    dve.tensor_scalar(diag[n % 2], ident, c_, None, ALU.mult).then_inc(sem("diag_ready"), 1)
                link(dve.memset(OUT, 0.0))
                dve.sem_inc(sem("expert_vectors"), len(STEPS["expert_vectors"]) - first - 1)
                dve.wait_ge(sem("passes_ready"), 1)
                n_passes = dve.value_load(passes[0:1, 0:1], min_val=1, max_val=2)
                with dve.Fori(0, n_passes) as p:
                    with dve.Fori(0, N_EXP) as e:
                        item = p * N_EXP + e
                        for j in range(EJ):
                            if j == 3:
                                for tt in range(2):
                                    last = dve.tensor_scalar(share[:, tt, :], slot_no, slots[:, tt, bass.ds(item, 1)],
                                                             shares[:, tt, bass.ds(item, 1)], ALU.is_equal, ALU.mult)
                                last.then_inc(sem("expert_vectors"), 1)
                            step(dve, "expert_products", f"up{j}", item)
                            step(dve, "expert_copies", f"silu{j}", item)
                            dve.tensor_tensor(HTOK[j % 2], sil2[j % 2], bank[2 * (j % 2) + 1][:, :], ALU.mult)\
                                .then_inc(sem("expert_vectors"), 1)
                            if j == 4:
                                choose(item + 1)
                        step(dve, "expert_products", f"y{EJ - 1}", item)
                        for half in range(2):
                            dve.tensor_copy(YG[:, half * 512:half * 512 + 512], bank[4 + half][:, :])\
                                .then_inc(sem("expert_vectors"), 1)
                        step(dve, "expert_vectors", "added3", item - 1)
                        for o in range(4):
                            tt, half = divmod(o, 2)
                            step(dve, "expert_products", f"spread{o}", item)
                            sums = OUT[:, tt, half * 512:half * 512 + 512]
                            dve.tensor_tensor(sums, sums, bank[o][:, :], ALU.add).then_inc(sem("expert_vectors"), 1)
                step(dve, "expert_vectors", "added3", n_passes * N_EXP - 1)
                for tt in range(2):
                    o = OUT[:, tt, :]
                    link(dve.tensor_tensor(o, o, rowG, ALU.mult))
                    link(dve.scalar_tensor_tensor(out=o, in0=XTOK[:, tt, :], scalar=float(ALPHA), in1=o, op0=ALU.mult,
                                                  op1=ALU.add))
                    link(dve.tensor_reduce(stat[:, tt, 0:1], o, AXX, ALU.add))
                    link(dve.tensor_scalar(stat[:, tt, 0:1], stat[:, tt, 0:1], 1.0 / D, None, ALU.mult))
                    dve.tensor_scalar(o, o, stat[:, tt, 0:1], None, ALU.subtract).then_inc(sem("fin_centred"), 1)
                for tt in range(2):
                    o = OUT[:, tt, :]
                    dve.wait_ge(sem("fin_std"), tt + 1)
                    link(dve.reciprocal(stat[:, tt, 3:4], stat[:, tt, 2:3]))
                    link(dve.scalar_tensor_tensor(out=o, in0=o, scalar=stat[:, tt, 3:4], in1=rowg, op0=ALU.mult, op1=ALU.mult))
                    dve.tensor_tensor(o, o, rowb, ALU.add).then_inc(sem("final"), 1)


_INS = ["x", "c", "ctx", "c_ctx", "mod_w", "mod_b", "ln_g", "ln_b", "hy_w_in", "hy_b_in", "hy_conv_w", "hy_conv_b",
        "hy_f_w1", "hy_f_b1", "hy_f_w2", "hy_f_b2", "hy_f_freq", "hy_f_w3", "hy_decay", "hy_skip", "hy_w_out",
        "hy_b_out", "rw_mu", "rw_w_rkv", "rw_w0", "rw_w1", "rw_w2", "rw_a0", "rw_a1", "rw_a2", "rw_g1", "rw_g2",
        "rw_k_k", "rw_k_a", "rw_r_k", "rw_lnx_g", "rw_lnx_b", "rw_w_out", "ffn_w13", "ffn_w2", "moe_router",
        "moe_w13", "moe_w2"]


def kernel(**inputs):
    import concourse.bacc as _bacc
    from concourse.bass_utils import run_bass_kernel_spmd as _run

    nc = _bacc.Bacc("TRN2", target_bir_lowering=False, num_devices=1)
    arrays, args = {}, {}
    for name in _INS:
        v = np.ascontiguousarray(inputs[name])
        arrays[f"in_{name}_dram"] = v
        args[name] = nc.dram_tensor(f"in_{name}_dram", v.shape, mybir.dt.from_np(v.dtype), kind="ExternalInput").ap()
    consts = []
    for n, v in enumerate(constants()):
        arrays[f"const_{n}_dram"] = v
        consts.append(nc.dram_tensor(f"const_{n}_dram", v.shape, mybir.dt.from_np(v.dtype), kind="ExternalInput").ap())
    out = nc.dram_tensor("out_0_dram", (1, SEQ, D), F32, kind="ExternalOutput").ap()
    build(nc, args, out, consts)
    r = _run(nc, [arrays], core_ids=[0])
    return r.results[0]["out_0_dram"]
```

```python
from contextlib import ExitStack
import math

import numpy as np

import concourse.bass as bass
from concourse import mybir

F32 = mybir.dt.float32
F32R = mybir.dt.float32r
I32 = mybir.dt.int32
U32 = mybir.dt.uint32
ALU = mybir.AluOpType
ACT = mybir.ActivationFunctionType
AXX = mybir.AxisListType.X

P = 128
D = 1024
KT = D // P
SEQ = 256
T = 2 * SEQ
NB = T // P
DEPTH = 2
ALPHA = (2 * DEPTH) ** 0.25
LN_EPS = 1e-5
HY_BANDS = 8
HY_EMB = 1 + 2 * HY_BANDS
HY_W = 64
FFN = 2816
FT = FFN // P
C = 64
HN = 64
RW_GN_EPS = 64e-5
DECAY = math.exp(-0.5)
GATE_LORA = 160
N_EXP = 8
FE = 3584
EJ = FE // 512

QN = 32
LEVELS = (2, 4, 8, 16)

ARENA = 53000
RS = 2048
RN = 6
PIECES = 4
ERN = 7

ROWS = {}


def _rows():
    for tile, names in enumerate([
        [("mod_b0", 48), ("mod_b1", 48)],
        [("ln_g", 32), ("ln_b", 32), ("hy_b_in", 24), ("hy_conv_b", 24)],
        [("hy_conv_w", 72), ("hy_b_out", 8), ("rw_mu", 48)],
        [("rw_w0", 16), ("rw_a0", 16), ("rw_k_k", 8), ("rw_k_a", 8), ("rw_r_k", 8), ("rw_lnx_g", 8),
         ("rw_lnx_b", 8), ("c", 8), ("c_ctx", 8)],
    ]):
        at = 0
        for name, n in names:
            ROWS[name] = (tile, at, n)
            at += n
    return ROWS


_rows()
ROW_FILL = [96, 112, 128, 88]


def constants():
    f64 = np.float64
    i = np.arange(P)
    ident = np.eye(P)
    mean = np.full((P, P), 1.0 / D)
    same_head = (i[:, None] // HN == i[None, :] // HN).astype(f64)
    common = np.concatenate([ident, mean, same_head, same_head / HN, np.ones((P, P)),
                             np.tile(np.arange(N_EXP), (P, 1)), i[:, None] < i[None, :], np.tile(i, (P, 1))], 1)

    L = SEQ
    t = np.arange(L, dtype=f64)
    w = 2 * np.pi * (np.arange(L) + 0.5) / (2 * L)
    ang = t[:, None] * w[None, :]
    fwd = np.concatenate([np.cos(ang), -np.sin(ang)], 1)
    fwd = fwd.reshape(2, P, 2 * L).transpose(1, 0, 2).reshape(P, -1)
    inv = np.concatenate([np.cos(ang).T, -np.sin(ang).T], 0) / L
    inv = inv.reshape(4, P, L).transpose(1, 0, 2).reshape(P, -1)
    t01 = np.arange(L, dtype=np.float32) / np.float32(max(L - 1, 1))
    bands = np.linspace(1e-4, HY_BANDS - 1, HY_BANDS, dtype=np.float32)
    a32 = (np.float32(2.0 * math.pi / L) * np.arange(L, dtype=np.float32)[:, None] * bands[None, :]).astype(f64)
    feats = np.zeros((P, L))
    feats[:HY_EMB] = np.concatenate([t01[:, None], np.cos(a32), -np.sin(a32)], 1).T
    negt = np.zeros((P, L))
    negt[0] = -t01
    notfirst = (i > 0).astype(f64)[:, None]
    layer0 = np.concatenate([fwd, inv, feats, negt, notfirst], 1)

    row, col = i[:, None], i[None, :]
    block = row // C == col // C
    lower, upper = block & (col < row), block & (col > row)
    strict = [lower, upper]
    incl_t = [block & (row <= col), block & (row >= col)]

    in_row, in_col = i[:, None] % QN, np.arange(QN)[None, :]

    def level(b, after_rows):
        pair = in_row // (2 * b) == in_col // (2 * b)
        r2, c2 = in_row // b % 2, in_col // b % 2
        return pair & (r2 == 1) & (c2 == 0) if after_rows else pair & (r2 == 0) & (c2 == 1)

    pos = np.arange(T) % C
    reset = [np.tile(pos != 0, (P, 1)), np.tile(pos != C - 1, (P, 1))]
    layer1 = np.concatenate([*strict, *incl_t, *reset, row % HN == np.arange(HN)[None, :],
                             in_row == in_col, in_row > in_col, in_row < in_col, level(1, True), level(1, False)], 1)
    bits = np.concatenate([level(b, a) for b in LEVELS for a in (True, False)], 1)
    return (common.astype(np.float32), layer0.astype(np.float32), layer1.astype(np.float32),
            bits.astype(np.int32))


PER = dict(proj=8, k_copied=1, sg=2, rate=2, r_copied=1, v_copied=1, g_copied=1, ksq=1, ksum=1, kstd=1,
           vt_full=1, vt_ready=1, decayed=2, excl=2, e_incl=2, e_inv=2, e_excl=2, kk_ready=1, b_raw=2,
           a_t=2, b_t=2, k_t=2, r_t=2, tr_full=6, q_ready=4, bk_ready=4, sc=12, sc_taken=12, tri_ready=4, off_ready=4,
           y_full=20, y_ready=20, z_full=20, merged=20, z1_full=4, z1_ready=4, wu_full=4, wu_ready=4,
           m_full=2, n_full=2, g_full=2, mo_ready=2, nd_ready=2, gt_ready=2, y_local=2, st_full=12,
           st_ready=14, out_y=1, y_copied=1, gn_mean=1, gn_cent=1, gn_sq=1, gn_var=1, gn_std=1, logs=2,
           bonus_in=1, bonus_full=1, pair_done=1, kk_raw=1, rate_used=2)


DVE_LINKS = 34


GROUPS = dict(gates=("sg", "rate"), exps=("e_incl", "e_inv", "e_excl"), decayed_all=("r_t", "k_t", "b_t", "a_t"),
              chunk_full=("m_full", "n_full", "g_full", "y_local"), chunk_taken=("mo_ready", "nd_ready", "gt_ready"))
IN_GROUP = {name: (group, n, len(names)) for group, names in GROUPS.items() for n, name in enumerate(names)}


def _expert_steps():
    pe, act, dve = [], [], []

    def pieces(name):
        return [f"{name}_{i}" for i in range(PIECES)]
    act += pieces("high_gate0")
    dve += pieces("low_gate0")
    last = EJ - 1
    for j in range(EJ):
        pe += pieces(f"gate{j}") + [f"turned{j - 1}"] * (j > 0) + ["shares_turned"] * (j == 4) + pieces(f"up{j}")
        pe += [f"y{j - 1}"] * (j > 0)
        act += pieces(f"high_up{j}") + [f"silu{j}"] + [f"hidden{j - 1}"] * (j > 0) + ["shareT"] * (j == 4)
        act += pieces(f"high_gate{j + 1}") * (j < last)
        dve += pieces(f"low_up{j}") + ["share"] * (j == 3) + [f"h{j}"] + ["pick"] * (j == 4)
        dve += pieces(f"low_gate{j + 1}") * (j < last)
    pe += [f"turned{last}", f"y{last}", "gathered"] + [f"spread{o}" for o in range(4)]
    act += [f"hidden{last}", "xg_high"]
    dve += ["yg0", "yg1", "xg_low"] + [f"added{o}" for o in range(4)]
    return dict(expert_products=pe, expert_copies=act, expert_vectors=dve)


STEPS = _expert_steps()


class Chain:

    def __init__(self, eng, sem):
        self.eng, self.sem, self.n, self.base, self.off = eng, sem, 0, 0, 0

    def __call__(self, ins):
        self.n += 1
        ins.then_inc(self.sem, 1)
        self.eng.wait_ge(self.sem, self.off + self.base + self.n)

    def enter(self, i, per):
        self.base, self.n, self.per, self.off = self.base + self.n, 0, per, i * per

    def leave(self, count):
        assert self.n == self.per, (self.n, self.per)
        self.base, self.n, self.off = self.base + count * self.per, 0, 0


class Ring:

    def __init__(self, eng, loaded):
        self.eng, self.loaded, self.n, self.it16, self.free = eng, loaded, 0, 0, {}

    def slot_to_load(self, done):
        slot, self.n = self.n % RN, self.n + 1
        if slot in self.free:
            self.eng.wait_ge(*self.free[slot])
        self.free[slot] = done
        return slot

    def loaded_slot(self):
        n, self.n = self.n, self.n + 1
        self.eng.wait_ge(self.loaded[n % RN], self.it16 + 16 * (n // RN + 1))
        return n % RN

    def load_loop(self, chunks, done, body):
        rounds = chunks // RN
        start = self.n
        for c in range(RN):
            body(c, self.slot_to_load(done(c)))
        with self.eng.Fori(1, rounds) as i:
            for j in range(RN):
                self.eng.wait_ge(*done((i - 1) * RN + j))
                body(i * RN + j, (start + j) % RN)
        for j in range(RN):
            self.free[(start + j) % RN] = done((rounds - 1) * RN + j)
        self.n = start + rounds * RN
        for c in range(rounds * RN, chunks):
            body(c, self.slot_to_load(done(c)))

    def read_loop(self, chunks, body, first=0):
        rounds, start = chunks // RN, self.n
        with self.eng.Fori(first, rounds) as i:
            self.it16 = (i - first) * 16
            for j in range(RN):
                body(i * RN + j)
        self.it16, self.n = 0, start + (rounds - first) * RN
        for c in range(rounds * RN, chunks):
            body(c)


def with_loop(eng, n, body):
    rounds, rest = divmod(n, RN)
    with eng.Fori(0, rounds) as i:
        for j in range(RN):
            body(i * RN + j, j)
    for j in range(rest):
        body(rounds * RN + j, j)


def build(nc, a, out, consts):
    ctx = ExitStack()
    with ctx, nc.allow_non_contiguous_dma(reason="a few short columns"):
        sems = {}

        def sem(name):
            name = IN_GROUP.get(name, (name,))[0]
            if name not in sems:
                sems[name] = ctx.enter_context(nc.semaphore(name))
            return sems[name]

        arena = ctx.enter_context(nc.sbuf_tensor("arena", [P, ARENA], F32))
        bank = [ctx.enter_context(nc.psum_tensor(f"bank{i}", [P, 512], F32)) for i in range(8)]
        at = [0]

        arena_at = nc.sbuf_base - 4 * ARENA

        def split(name, first, *shape, dtype=F32R):
            v = nc.alloc_sbuf_tensor_at(name, [P, int(np.prod(shape))], dtype, offset=arena_at + 4 * first)
            return v[:, :].rearrange("p (a b) -> p a b", b=shape[-1])

        def mark(n=None):
            if n is not None:
                at[0] = n
            return at[0]

        def sb(*shape):
            n = int(np.prod(shape))
            v = arena[:, at[0]:at[0] + n]
            at[0] += n
            assert at[0] <= ARENA, at[0]
            if len(shape) == 2:
                v = v.rearrange("p (a b) -> p a b", b=shape[1])
            if len(shape) == 3:
                v = v.rearrange("p (a b c) -> p a b c", b=shape[1], c=shape[2])
            return v

        common = sb(7 * P + N_EXP)
        expert_no = common[:, 5 * P:5 * P + N_EXP]
        before, slot_no = common[:, 5 * P + N_EXP:6 * P + N_EXP], common[:, 6 * P + N_EXP:]
        ident, meanm, heads1, heads64, ones = (common[:, P * j:P * (j + 1)] for j in range(5))
        vec = sb(4 * P)
        modv = [sb(48, 2), sb(48, 2)]
        silu_c = sb(KT, 2)
        eps = sb(4)
        xt_at = mark()
        XT = sb(KT, T)
        table = mark((mark() + 7) // 8 * 8)
        sb(3400)
        ut_at = mark((mark() + 7) // 8 * 8)
        UT = sb(KT, T)
        ring_at = mark()
        ring = [sb(RS) for _ in range(RN)]
        work = mark()

        mark(table)
        fwd, inv = sb(2, T), sb(4, SEQ)
        feats, negt, notfirst = sb(SEQ), sb(SEQ), sb(1)
        hw1, hw2, hcol = sb(HY_W), sb(HY_W), sb(4)
        mark(work)
        X1, X2 = sb(KT, T), sb(KT, T)
        ZT = sb(NB, D)
        KSP = sb(8, D)
        tmp_at = mark()
        pad = [sb(2, SEQ + 2) for _ in range(2)]
        cv = [sb(T) for _ in range(2)]
        pr = [sb(T) for _ in range(4)]
        win = [sb(T) for _ in range(2)]
        gate_t = sb(T)
        cv_spare = sb(T)
        dec = KSP[:, 4:8, :].rearrange("p a b -> p (a b)")
        rows = KSP[:, 0:1, 0:512].rearrange("p a (r c) -> p (a r) c", c=P)
        xin = X2.rearrange("p a b -> p (a b)").rearrange("p (a b) -> p a b", b=D)
        skip = X1.rearrange("p a b -> p (a b)")[:, 0:2 * D]
        hargs = [X1[:, 4 + j, 0:SEQ] for j in range(4)]
        w3 = ZT.rearrange("p a b -> p (a b)")
        kcs = UT.rearrange("p a b -> p (a b)").rearrange("p (s t d) -> p s t d", s=2, t=2)
        Y = UT.rearrange("p a b -> p (a b)").rearrange("p (s f d) -> p s f d", s=2, f=4)
        mod_rows0 = arena[:, work:work + 6 * D]
        work8 = mark((work + 7) // 8 * 8)
        Hf = sb(FT * T)
        H = Hf.rearrange("p (f t) -> p f t", t=T)
        sq_at = mark()
        SQ = sb(KT, T)
        sil = [sb(T), sb(T)]
        rt = [sb(T), sb(T)]
        std, rstd = sb(T), sb(T)
        u_at = mark((mark() + 7) // 8 * 8)
        mod_rows1 = sb(6 * D)
        UH = [split(f"u_high{g}", u_at + 4 * T * g, 4, T) for g in range(2)]
        UL = [split(f"u_low{g}", ut_at + 4 * T * g, 4, T) for g in range(2)]
        WH = [split("ring_high0", table, 2 * KT, P), split("ring_high1", mark(), 2 * KT, P)]
        WL = [split(f"ring_low{s}", ring_at + RS * s, 2 * KT, P) for s in range(RN)]
        assert mark() + RS <= ARENA
        HH = [split(f"hidden_high{g}", sq_at + 2 * T * g, 2, T) for g in range(2)]
        HL = [split(f"hidden_low{c}", work8 + 2 * T * c, 2, T) for c in range(FT // 2)]

        mark(table)
        strict, incl_t = [sb(P), sb(P)], [sb(P), sb(P)]
        reset = [sb(T), sb(T)]
        eye64 = sb(HN)
        eye32, strict32, join1 = sb(QN), [sb(QN), sb(QN)], [sb(QN), sb(QN)]
        bits_at = mark()
        bits = [[sb(QN).bitcast(I32) for _ in range(2)] for _ in LEVELS]
        mark(work)
        UP = sb(KT, 2, SEQ + 2)
        XX, XM = sb(KT, T), sb(KT, T)
        pair_end = mark()
        x_at = mark()
        XK, XV, XR = sb(KT, T), sb(KT, T), sb(KT, SEQ)
        HW, HA, G1a, G1b = sb(T), sb(T), sb(SEQ), sb(SEQ)
        low_k = 3
        wo_at = max(x_at + low_k * D, work + FT * T + (KT + 4) * T + T)
        assert wo_at + (KT - low_k) * D <= mark()
        WO = [arena[:, (x_at if k < low_k else wo_at - low_k * D) + k * D:][:, :D] for k in range(KT)]
        YT = sb(KT, SEQ)
        mark(ring_at)
        lw1, la1, lg1 = sb(KT, P), sb(KT, P), sb(KT, GATE_LORA)

        mark(ut_at)
        wst = sb(3, KT, P)
        w2s, a2s, g2a, g2b = sb(P), sb(P), sb(P), sb(P)
        one_ka = sb(KT)
        mark(ring_at)
        Kf, KK, KS, Vf, Vt, Rf, Gf = sb(T), sb(T), sb(T), sb(T), sb(NB, P), sb(SEQ), sb(SEQ)
        At, Bt, Kt = ([sb(T), sb(T)] for _ in range(3))
        Rt = [sb(SEQ), sb(SEQ)]
        DC, KD = [sb(8), sb(8)], sb(SEQ)
        SG, AS = [sb(T), sb(T)], [sb(T), sb(T)]
        CS, EP, EN, EX = sb(T), sb(T), sb(T), sb(T)
        Btok, Ktok = sb(NB, P), sb(NB, P)
        App, Aoff, TMp, TTp, Yp = ([sb(NB, QN) for _ in range(2)] for _ in range(5))
        AakT = [sb(NB, P) for _ in range(2)]
        ARR = [sb(NB, P) for _ in range(2)]
        TT = [[sb(NB, P) for _ in range(2)] for _ in range(2)]
        Q = [sb(NB, P) for _ in range(2)]
        WU = [[t[d].rearrange("p (b c) -> p b c", c=P) for t in (At, Kt)] for d in range(2)]
        MO, ND = [sb(8, C) for _ in range(2)], [sb(8, C) for _ in range(2)]
        GT = [sb(SEQ) for _ in range(2)]
        ST = [sb(8, C) for _ in range(2)]
        YF, YS, YN = sb(SEQ), sb(SEQ), sb(SEQ)
        assert mark() <= pair_end, (mark(), pair_end)

        mark(table)
        XTOK = sb(2, D)
        rt_w, logit, mx, ixf, comb = sb(KT, N_EXP), sb(2, 8), sb(2, 8), sb(2, 8), sb(2, 8)
        ix = sb(16).bitcast(U32)
        hot, chosen, place = sb(2, 8), sb(2, 8), sb(2, 8)
        slots, shares = sb(2, 2 * N_EXP + 1), sb(2, 2 * N_EXP + 1)
        most = sb(1)
        passes = sb(1).bitcast(I32)
        w12 = sb(2, 4)
        stat = sb(2, 4)
        diag = [sb(P), sb(P)]
        assert mark() <= table + 3400
        mark(xt_at)
        UTOK = sb(2, D)
        HTOK = [sb(512), sb(512)]
        sil2 = [sb(512), sb(512)]
        assert mark() <= table
        mark(ring_at)
        ering = [split(f"expert_w{s}", mark() + KT * 512 * s, KT, 512, dtype=F32) for s in range(ERN)]
        mark(mark() + ERN * KT * 512)
        OUT = sb(2, D)
        high = [split(f"w_high{i}", ut_at + 1024 * i, 2, 512) for i in range(PIECES)]
        low = [split(f"w_low{s}", ring_at + KT * 512 * s, KT, 512) for s in range(ERN)]
        mark((mark() + 7) // 8 * 8)
        XGH = split("xg_high", mark(), KT, P)
        XGL = split("xg_low", mark() + KT * P, KT, P)
        mark(mark() + 2 * KT * P)
        HT = [sb(4, P), sb(4, P)]
        YG = sb(D)
        pick, share = sb(2, P), sb(2, P)
        shareT = sb(2, P)
        rowG, rowg, rowb = sb(D), sb(D), sb(D)
        assert mark() <= ARENA

        def col(name, j):
            tile, first, n = ROWS[name]
            assert j < n
            return vec[:, tile * P + first + j:tile * P + first + j + 1]

        def mv(layer, chunk, k, s):
            return modv[layer][:, chunk * KT + k, 1 - s:2 - s]

        ring_start = [0, 24 + 16 + FT + FT // 2]
        ffn_start = 24 + 16
        win_f = [gate_t, cv_spare]

        seg = [slice(0, SEQ), slice(SEQ, T)]

        def dcol(name, i):
            tile, first, n = ROWS[name]
            return vec[:, bass.ds(tile * P + first + i, 1)]

        def each4(m):
            return m.unsqueeze(1).to_broadcast([P, 4, P])

        def b4(b):
            return bank[b][:, :].rearrange("p (b c) -> p b c", b=4)

        def each4q(m):
            return m.unsqueeze(1).to_broadcast([m.shape[0], NB, QN])

        def quarter(q):
            return slice(QN * q, QN * q + QN)

        def packed(b):
            return bank[b][:, 0:P].rearrange("p (b c) -> p b c", b=NB)

        ROW_BANKS = (2, 3, 4, 5, 6, 7)
        JOINED = (4, 6)

        def c4(b):
            return bank[b][:, 0:4 * C].rearrange("p (b c) -> p b c", b=4)

        def hd(h):
            return slice(HN * h, HN * h + HN)

        def waiter(eng, i):
            def w(name, c):
                if name in IN_GROUP:
                    _, n, size = IN_GROUP[name]
                    eng.wait_ge(sem(name), i * 2 * size + (c - 1) * size + n + 1)
                else:
                    eng.wait_ge(sem(name), i * PER[name] + c)
            return w

        def settle(eng):
            eng.sem_inc(sem("settled"), 1)

        def ln_banks(n):
            return (7, 6) if n == 2 else (0, 1)

        def slot_of(q):
            return q % ERN

        def step(eng, steps, name, item):
            eng.wait_ge(sem(steps), (item + 1) * len(STEPS[steps]) + STEPS[steps].index(name) + 1)

        CHUNKS = [[0, 1, 2, 3, 4, 5, 6, 7], [3, 2, 1, 0, 7, 6, 5, 4]]

        block = ctx.enter_context(nc.Block())
        w_loaded = [sem(f"w_loaded{i}") for i in range(RN)]
        up_loaded = [sem(f"up_loaded{i}") for i in range(RN)]

        @block.sync
        def _(sp):
            ld = Ring(sp, w_loaded)

            def load(name, dst, src, n=16):
                sp.dma_start(dst, src).then_inc(sem(name), 16)

            load("ld_common", common, consts[0])
            for name in ROWS:
                tile, first, n = ROWS[name]
                src = {"mod_b0": a["mod_b"][0:1], "mod_b1": a["mod_b"][1:2], "c_ctx": a["c_ctx"],
                       "c": a["c"]}.get(name, a.get(name))
                flat = src
                if len(src.shape) == 2:
                    flat = src.rearrange("a b -> (a b)")
                if len(src.shape) == 3:
                    flat = src.rearrange("a b c -> (a b c)")
                load("ld_rows", rows[first:first + n, tile, :], flat.rearrange("(r p) -> r p", p=P))

            def load_mod(layer):
                w = a["mod_w"][layer].rearrange("(k p) n -> p k n", p=P)
                ld.load_loop(24, lambda c: (sem("mod_full"), c + 1 + 24 * layer),
                             lambda c, s: sp.dma_start(ring[s].rearrange("p (k n) -> p k n", n=256),
                                                       w[:, :, bass.ds(c * 256, 256)]).then_inc(w_loaded[s], 16))

            def load_cols(w, n, name, first=0):
                w = w.rearrange("(k p) n -> p k n", p=P)
                for c in range(n):
                    s = ld.slot_to_load((sem(name), first + 2 * c + 2))
                    sp.dma_start(ring[s].rearrange("p (k n) -> p k n", n=256), w[:, :, c * 256:(c + 1) * 256])\
                        .then_inc(w_loaded[s], 16)

            load_mod(0)
            load_cols(a["hy_w_in"], 12, "proj_full")
            load_cols(a["hy_w_out"], 4, "out_full")
            w13 = a["ffn_w13"][0].rearrange("(k p) (h n) -> p k h n", p=P, h=2)

            def load13(f, s):
                dst = ring[s].rearrange("p (h k n) -> p h k n", h=2, n=P)
                sp.dma_start(dst[:, 0], w13[:, :, 0, bass.ds(f * P, P)]).then_inc(w_loaded[s], 16)
                sp.dma_start(dst[:, 1], w13[:, :, 1, bass.ds(f * P, P)]).then_inc(up_loaded[s], 16)
            ld.load_loop(FT, lambda f: (sem("hidden_full"), f + 1), load13)
            w2 = a["ffn_w2"][0].rearrange("(c p) n -> p c n", p=P)
            for c in range(FT // 2):
                s = ld.slot_to_load((sem("hidden_full"), FT + c + 1) if c < FT // 2 - 1 else (sem("out_full"), 16))
                sp.dma_start(ring[s].rearrange("p (c n) -> p c n", n=D), w2[:, 2 * c:2 * c + 2, :])\
                    .then_inc(w_loaded[s], 16)
            load_mod(1)
            sp.wait_ge(sem("hidden_full"), FT)
            load("ld_table1", arena[:, table:bits_at], consts[2])
            load("ld_table1", arena[:, bits_at:bits_at + len(LEVELS) * 2 * QN].bitcast(I32), consts[3])
            sp.wait_ge(sem("mod_full"), 48)
            for d in range(2):
                load("ld_lora", lw1[:, :, d * HN:(d + 1) * HN], a["rw_w1"][d].rearrange("(k p) n -> p k n", p=P))
                load("ld_lora", la1[:, :, d * HN:(d + 1) * HN], a["rw_a1"][d].rearrange("(k p) n -> p k n", p=P))
            load("ld_lora", lg1, a["rw_g1"].rearrange("(k p) n -> p k n", p=P))
            wr = a["rw_w_rkv"].rearrange("j (k p) n -> p (j k) n", p=P)
            w2d = a["rw_w2"].rearrange("d r n -> (d r) n")
            a2d = a["rw_a2"].rearrange("d r n -> (d r) n")
            sp.wait_ge(sem("hidden_full"), FT)
            with sp.Fori(0, KT) as i:
                sp.wait_ge(sem("stage_free"), i + 1)
                cols = bass.ds(i * P, P)
                sp.dma_start(wst.rearrange("p j k n -> p (j k) n"), wr[:, :, cols]).then_inc(sem("ld_pair"), 16)
                sp.dma_start(w2s, w2d[:, cols]).then_inc(sem("ld_pair"), 16)
                sp.dma_start(a2s, a2d[:, cols]).then_inc(sem("ld_pair"), 16)
                sp.dma_start(g2a, a["rw_g2"][0:P, cols]).then_inc(sem("ld_pair"), 16)
                sp.dma_start(g2b[0:GATE_LORA - P, :], a["rw_g2"][P:GATE_LORA, cols]).then_inc(sem("ld_pair"), 16)
            sp.wait_ge(sem("stage_free"), KT + 1)
            wo = a["rw_w_out"].rearrange("(k p) n -> p k n", p=P)
            load("ld_out", arena[:, x_at:x_at + low_k * D].rearrange("p (k n) -> p k n", n=D), wo[:, 0:low_k, :])
            load("ld_out", arena[:, wo_at:wo_at + (KT - low_k) * D].rearrange("p (k n) -> p k n", n=D), wo[:, low_k:, :])
            sp.wait_ge(sem("pair_done"), KT + 1)
            load("ld_router", rt_w, a["moe_router"][0].rearrange("(k p) e -> p k e", p=P))
            w13 = a["moe_w13"][0].rearrange("e (k p) n -> p (e k) n", p=P)
            w2 = a["moe_w2"][0].rearrange("e (k p) n -> p (e k) n", p=P)
            n_passes = sp.alloc_register("n_passes")
            with sp.Fori(0, n_passes) as p:
                with sp.Fori(0, N_EXP) as e:
                    for q in range(3 * EJ):
                        (j, r), (jb, rb) = divmod(q, 3), divmod((q - ERN) % (3 * EJ), 3)
                        last = f"y{jb}" if rb == 2 else f"{('gate', 'up')[rb]}{jb}_{PIECES - 1}"
                        step(sp, "expert_products", last,
                             p * N_EXP + e - (1 if q < ERN else 0))
                        if q == 5:
                            sp.wait_ge(sem("ln_done"), 24)
                            sp.wait_ge(sem("u_ready"), 6)
                        s = slot_of(q)
                        if r < 2:
                            src = w13[:, bass.ds(e * KT, KT), r * FE + j * 512:r * FE + j * 512 + 512]
                            dst = ering[s]
                        else:
                            src = w2[:, bass.ds(e * (FE // P) + 4 * j, 4), :]
                            dst = ering[s].rearrange("p a b -> p (a b)").rearrange("p (a b) -> p a b", b=D)
                        sp.dma_start(dst, src).then_inc(sem(f"ew_loaded{s}"), 16)
                sp.wait_ge(sem("routed"), 2)
                sp.reg_load(n_passes, passes[0:1, 0:1])
            for tt in range(2):
                sp.wait_ge(sem("final"), tt + 1)
                sp.dma_start(out[0, tt * P:(tt + 1) * P, :], OUT[:, tt, :]).then_inc(sem("stored"), 16)
            sp.wait_ge(sem("stored"), 32)
        @block.tensor
        def _(pe):
            rg = Ring(pe, w_loaded)
            pe.wait_ge(sem("ld_common"), 16)
            pe.wait_ge(sem("ld_rows"), 16 * len(ROWS))
            for j, n in enumerate(ROW_FILL):
                last = pe.transpose(bank[0][:, j * P:j * P + n], rows[0:n, j, :], ident[0:n, 0:n])
            last.then_inc(sem("rows_turned"), 1)
            pe.wait_ge(sem("ld_x"), 32)
            for k in range(KT):
                if k >= 4:
                    pe.wait_ge(sem("x_taken"), k - 3)
                for t in range(NB):
                    last = pe.transpose(bank[1 + k % 4][:, t * P:(t + 1) * P], xin[:, t, k * P:(k + 1) * P], ident)
                last.then_inc(sem("x_turned"), 1)

            pe.wait_ge(sem("ld_table"), 16)
            pe.wait_ge(sem("ld_filter"), 16 * 9)
            pe.matmul(bank[5][0:HY_W, 0:SEQ], hw1[0:HY_EMB, :], feats[0:HY_EMB, :], start=True, stop=True)\
                .then_inc(sem("sine_in"), 1)
            pe.wait_ge(sem("sine_out"), 1)
            pe.matmul(bank[6][0:HY_W, 0:SEQ], hw2[0:HY_W, :], hargs[2][0:HY_W, :], start=True, stop=True)\
                .then_inc(sem("sine_in"), 1)
            pe.wait_ge(sem("sine_out"), 2)
            pe.wait_ge(sem("decay_abs"), 1)
            pe.wait_ge(sem("x_taken"), 8)
            pe.wait_ge(sem("vec_ready"), 1)
            for n in range(2):
                for q in range(4):
                    g = 4 * n + q
                    half, tt = q // 2, q % 2
                    b = 4 * (g % 2)
                    if g >= 2:
                        pe.wait_ge(sem("filter_taken"), g - 1)
                    if g == 4:
                        pe.wait_ge(sem("spectrum_taken"), 8)
                    for j in range(2):
                        cs = slice((2 * n + j) * D + half * 512, (2 * n + j) * D + half * 512 + 512)
                        pe.matmul(bank[b + j][:, :], hargs[3][0:HY_W, tt * P:(tt + 1) * P], w3[0:HY_W, cs],
                                  start=True, stop=True)
                        last = pe.matmul(bank[b + 2 + j][:, :], negt[0:1, tt * P:(tt + 1) * P], dec[0:1, cs],
                                         start=True, stop=True)
                    last.then_inc(sem("filter_full"), 1)
                pe.wait_ge(sem("pool_taps"), 4 * (n + 1))
                pe.wait_ge(sem("taps_ready"), 4 * (n + 1))
                for o in range(8):
                    c, f, half = o // 4, o // 2 % 2, o % 2
                    for tt in range(2):
                        last = pe.matmul(bank[o][:, :], fwd[:, tt, c * SEQ + f * P:c * SEQ + (f + 1) * P],
                                         kcs[:, c, tt, half * 512:half * 512 + 512], start=(tt == 0), stop=(tt == 1))
                    last.then_inc(sem("spectrum_full"), 1)

            def modulation(layer):
                dst = [mod_rows0, mod_rows1][layer]
                pe.wait_ge(sem("silu_ready"), 1)
                if layer == 0:
                    pe.wait_ge(sem("spectrum_taken"), 16)

                def body(c):
                    s = rg.loaded_slot()
                    pe.wait_ge(sem("mod_taken"), c + 1 + 30 * layer)
                    w = ring[s].rearrange("p (k n) -> p k n", n=256)
                    for k in range(KT):
                        last = pe.matmul(bank[s][0:2, 0:256], silu_c[:, k, :], w[:, k, :], start=(k == 0),
                                         stop=(k == KT - 1))
                    last.then_inc(sem("mod_full"), 1)
                if layer == 0:
                    rg.read_loop(24, body)
                else:
                    for c in range(RN):
                        body(c)
                    ln_mean(2)
                    for c in range(RN, 2 * RN):
                        body(c)
                    ln_var(2)
                    rg.read_loop(24, body, first=2)
                pe.wait_ge(sem("mod_taken"), 30 * (layer + 1))
                for j in range(48):
                    last = pe.transpose(bank[6][:, 2 * j:2 * j + 2], dst[0:2, j * P:(j + 1) * P], ident[0:2, 0:2])
                last.then_inc(sem("mod_turned"), 1)

            modulation(0)

            def ln_mean(n, width=T):
                cols = slice(T - width, T)
                pe.wait_ge(sem("residual_done"), 8 * n)
                for k in range(KT):
                    last = pe.matmul(bank[ln_banks(n)[0]][:, 0:width], meanm, XT[:, k, cols], start=(k == 0), stop=(k == KT - 1))
                last.then_inc(sem("ln_mean"), 1)

            def ln_var(n, width=T):
                for k in range(KT):
                    pe.wait_ge(sem("ln_square"), 8 * (n - 1) + k + 1)
                    last = pe.matmul(bank[ln_banks(n)[1]][:, 0:width], meanm, SQ[:, k, 0:width], start=(k == 0), stop=(k == KT - 1))
                last.then_inc(sem("ln_var"), 1)

            def layer_norm(n, width=T):
                ln_mean(n, width)
                ln_var(n, width)

            pe.wait_ge(sem("u_ready"), 2)

            def turn_v(m):
                pe.wait_ge(sem("conv_done"), m + 1)
                if m >= 2:
                    pe.wait_ge(sem("v_taken"), m - 1)
                for t in range(NB):
                    last = pe.transpose(bank[4 + m % 2][:, t * P:(t + 1) * P], cv[m % 2][:, t * P:(t + 1) * P], ident)
                last.then_inc(sem("v_turned"), 1)

            for m in range(24):
                if m % 2 == 0:
                    s = rg.loaded_slot()
                if m >= 4:
                    pe.wait_ge(sem("proj_taken"), m - 3)
                w = ring[s].rearrange("p (k n) -> p k n", n=256)[:, :, (m % 2) * P:(m % 2 + 1) * P]
                for k in range(KT):
                    last = pe.matmul(bank[m % 4][:, :], w[:, k, :], UT[:, k, :], start=(k == 0), stop=(k == KT - 1))
                last.then_inc(sem("proj_full"), 1)
                if 1 <= m <= KT:
                    turn_v(m - 1)
            for n in range(2):
                X = [X1, X2][n]
                if n == 0:
                    pe.wait_ge(sem("v_taken"), 8)
                    pe.wait_ge(sem("conv_done"), 24)
                else:
                    for k in range(KT):
                        if k >= 4:
                            pe.wait_ge(sem("z_taken"), k - 3)
                        for t in range(NB):
                            last = pe.transpose(bank[k % 4][:, t * P:(t + 1) * P], X1[:, k, t * P:(t + 1) * P], ident)
                        last.then_inc(sem("z_turned"), 1)
                    pe.wait_ge(sem("z_taken"), 8)
                def forward(g):
                    half, s = g // 2, g % 2
                    if g + 4 * n >= 1:
                        pe.wait_ge(sem("bins_taken"), g + 4 * n)
                    for f in range(4):
                        for tt in range(2):
                            last = pe.matmul(bank[f][:, :], fwd[:, tt, f * P:(f + 1) * P],
                                             ZT[:, 2 * s + tt, half * 512:half * 512 + 512],
                                             start=(tt == 0), stop=(tt == 1))
                    last.then_inc(sem("bins_full"), 1)

                def inverse(g):
                    half, s = g // 2, g % 2
                    pe.wait_ge(sem("product_ready"), 4 * n + g + 1)
                    for ct in range(4):
                        if 16 * n + 4 * g + ct >= 4:
                            pe.wait_ge(sem("long_taken"), 16 * n + 4 * g + ct - 3)
                        for f in range(4):
                            last = pe.matmul(bank[4 + ct][:, 0:SEQ], Y[:, g % 2, f, ct * P:(ct + 1) * P],
                                             inv[:, f, :], start=(f == 0), stop=(f == 3))
                        last.then_inc(sem("long_full"), 1)

                for g in range(5):
                    if g < 4:
                        forward(g)
                    if g >= 1:
                        inverse(g - 1)
                pe.wait_ge(sem("long_taken"), 16 * (n + 1))
            for m in range(KT):
                if m % 2 == 0:
                    s = rg.loaded_slot()
                if m >= 4:
                    pe.wait_ge(sem("residual_done"), m - 3)
                w = ring[s].rearrange("p (k n) -> p k n", n=256)[:, :, (m % 2) * P:(m % 2 + 1) * P]
                for k in range(KT):
                    last = pe.matmul(bank[m % 4][:, :], w[:, k, :], X2[:, k, :], start=(k == 0), stop=(k == KT - 1))
                last.then_inc(sem("out_full"), 1)
            layer_norm(1)
            pe.wait_ge(sem("u_ready"), 4)

            def hidden(f):
                s = rg.loaded_slot()
                b = 2 * (s % 2)
                pe.wait_ge(up_loaded[s], rg.it16 + 16 * ((rg.n - 1 - ffn_start) // RN + 1))
                pe.wait_ge(sem("hidden_taken"), f + 1)
                pe.wait_ge(sem("ffn_low"), f + 3)
                wh, wl = WH[s % 2], WL[s]
                for h in range(2):
                    for k in range(KT):
                        c, uh, ul = h * KT + k, UH[k // 4][:, k % 4, :], UL[k // 4][:, k % 4, :]
                        pe.matmul(bank[b + h][:, :], wh[:, c, :], uh, start=(k == 0), stop=False)
                        pe.matmul(bank[b + h][:, :], wh[:, c, :], ul, start=False, stop=False)
                        last = pe.matmul(bank[b + h][:, :], wl[:, c, :], uh, start=False, stop=(k == KT - 1))
                last.then_inc(sem("hidden_full"), 1)
            rg.read_loop(FT, hidden)
            pe.wait_ge(sem("hidden_taken"), FT + 2)
            for c in range(FT // 2):
                s = rg.loaded_slot()
                pe.wait_ge(sem("ffn_low"), 2 + FT + 2 * c + 2)
                wh, wl = WH[s % 2], WL[s]
                for g in range(2):
                    for m in range(KT):
                        first, final = c + g == 0, c == FT // 2 - 1 and g == 1
                        o, hh, hl = g * KT + m, HH[c % 2][:, g, :], HL[c][:, g, :]
                        pe.matmul(bank[m][:, :], wh[:, o, :], hh, start=first, stop=False)
                        pe.matmul(bank[m][:, :], wh[:, o, :], hl, start=False, stop=False)
                        last = pe.matmul(bank[m][:, :], wl[:, o, :], hh, start=False, stop=final)
                        if final:
                            last.then_inc(sem("out_full"), 1)
                if c < FT // 2 - 1:
                    last.then_inc(sem("hidden_full"), 1)
            pe.wait_ge(sem("residual_done"), 8 + RN)
            modulation(1)
            pe.wait_ge(sem("ld_lora"), 16 * 5)
            for k in range(KT):
                pe.wait_ge(sem("xm_ready"), k + 1)
                last = pe.matmul(bank[0][:, :], lw1[:, k, :], XM[:, k, :], start=(k == 0), stop=(k == KT - 1))
            last.then_inc(sem("lora_full"), 1)
            for k in range(KT):
                pe.wait_ge(sem("xm_ready"), KT + k + 1)
                last = pe.matmul(bank[1][:, :], la1[:, k, :], XV[:, k, :], start=(k == 0), stop=(k == KT - 1))
            last.then_inc(sem("lora_full"), 1)
            pe.wait_ge(sem("xm_ready"), 2 * KT + 1)
            for r0, r1 in ((0, P), (P, GATE_LORA)):
                b = bank[2 + r0 // P]
                for k in range(KT):
                    last = pe.matmul(b[0:r1 - r0, 0:SEQ], lg1[:, k, r0:r1], XM[:, k, 0:SEQ], start=(k == 0),
                                     stop=(k == KT - 1))
            last.then_inc(sem("lora_full"), 1)
            pe.sem_inc(sem("stage_free"), 1)
            pe.wait_ge(sem("lora_taken"), 4)
            pe.wait_ge(sem("ld_table1"), 32)
            mm = pe.matmul

            def project_keys(i, tiles):
                if tiles[0] == 0:
                    pe.wait_ge(sem("ld_pair"), i * 80 + 80)
                for k in tiles:
                    last = mm(bank[0][:, :], wst[:, 1, k, :], XK[:, k, :], start=(k == 0), stop=(k == KT - 1))
                if tiles[-1] == KT - 1:
                    last.then_inc(sem("proj"), 1)

            def pair(i, more):
                w = waiter(pe, i)
                for d in range(2):
                    r = hd(d)
                    mm(bank[3 + d][:, :], w2s[r, :], HW[r, :], start=True, stop=True).then_inc(sem("proj"), 1)
                    mm(bank[5 + d][:, :], a2s[r, :], HA[r, :], start=True, stop=True).then_inc(sem("proj"), 1)
                for k in range(KT):
                    last = mm(bank[2][:, 0:SEQ], wst[:, 0, k, :], XR[:, k, :], start=(k == 0), stop=(k == KT - 1))
                last.then_inc(sem("proj"), 1)
                w("k_copied", 1)
                w("ksq", 1)
                mm(bank[0][:, :], heads1, KS, start=True, stop=True).then_inc(sem("ksum"), 1)
                w("pair_done", 1)
                for k in range(KT):
                    last = mm(bank[1][:, :], wst[:, 2, k, :], XV[:, k, :], start=(k == 0), stop=(k == KT - 1))
                last.then_inc(sem("proj"), 1)
                mm(bank[7][:, 0:SEQ], g2a, G1a, start=True, stop=False)
                mm(bank[7][:, 0:SEQ], g2b[0:32, :], G1b[0:32, :], start=False, stop=True).then_inc(sem("proj"), 1)
                w("v_copied", 1)
                for b in range(NB):
                    last = pe.transpose(bank[1][:, b * P:(b + 1) * P], Vf[:, b * P:(b + 1) * P], ident)
                last.then_inc(sem("vt_full"), 1)
                pe.wait_ge(sem("proj"), i * 8 + 8)
                pe.sem_inc(sem("stage_free"), 1)
                w("sg", 2)
                w("rate", 2)
                w("r_copied", 1)
                w("g_copied", 1)
                w("vt_ready", 1)
                w("kstd", 1)
                for d in range(2):
                    for j, (src, name) in enumerate(((At, "a_t"), (Bt, "b_t"), (Kt, "k_t"))):
                        w(name, d + 1)
                        if d == 1:
                            (w("z1_ready", 2), w("wu_ready", 2), w("mo_ready", 1), w("nd_ready", 1), w("gt_ready", 1))
                        for b in range(NB):
                            last = pe.transpose(bank[2 + j][:, b * P:(b + 1) * P], src[d][:, b * P:(b + 1) * P], ident)
                        last.then_inc(sem("tr_full"), 1)
                    w("r_t", d + 1)
                    for kind in range(3):
                        for h in range(2):
                            r = hd(h)
                            if kind == 2 and h == 0:
                                w("q_ready", 2 * d + 2)
                                w("bk_ready", 2 * d + 2)
                            ps = bank[(0, 5, 2)[kind] + h]
                            for b in range(NB):
                                cs = slice(b * P, b * P + P)
                                rs = slice((b % 2) * P, (b % 2) * P + P)
                                if kind == 0:
                                    lhs, rhs = At[d][r, cs], Bt[d][r, cs]
                                elif kind == 1:
                                    lhs, rhs = Kt[d][r, cs], At[d][r, cs]
                                else:
                                    src = (Bt, Kt)[b // 2][d]
                                    lhs, rhs = src[r, SEQ + rs.start:SEQ + rs.stop], Rt[d][r, rs]
                                last = mm(ps[:, cs], lhs, rhs, start=True, stop=True)
                            last.then_inc(sem("sc"), 1)
                    for lv in range(len(LEVELS)):
                        n0 = 10 * d + 2 * lv
                        for h in range(2):
                            if lv == 0:
                                w("tri_ready", 2 * d + h + 1)
                                w("off_ready", 2 * d + h + 1)
                            else:
                                w("merged", n0 + h - 1)
                            settle(pe)
                            for b in range(NB):
                                for q in range(4):
                                    last = mm(bank[h][quarter(q), b * QN:b * QN + QN], App[h][quarter(q), b, :],
                                              TTp[h][quarter(q), b, :], start=True, stop=True)
                            last.then_inc(sem("y_full"), 1)
                        if lv == 0:
                            w("sc_taken", 6 * d + 4)
                            for h in range(2):
                                for b in range(NB):
                                    last = mm(bank[5][:, (NB * h + b) * C:(NB * h + b + 1) * C], AakT[h][:, b, :],
                                              Vt[:, b, hd(h)], start=True, stop=True)
                                last.then_inc(sem("z1_full"), 1)
                        for h in range(2):
                            w("y_ready", n0 + h + 1)
                            settle(pe)
                            for b in range(NB):
                                for q in range(4):
                                    last = mm(bank[JOINED[h]][quarter(q), b * QN:b * QN + QN], Yp[h][quarter(q), b, :],
                                              TMp[h][quarter(q), b, :], start=True, stop=True)
                            last.then_inc(sem("z_full"), 1)
                    for h in range(2):
                        w("merged", 10 * d + 7 + h)
                        settle(pe)
                        for b in range(NB):
                            for s_ in range(2):
                                late, early = quarter(2 * s_ + 1 - d), quarter(2 * s_ + d)
                                last = mm(bank[h][early, b * QN:b * QN + QN], Aoff[h][late, b, :], TTp[h][late, b, :],
                                          start=True, stop=True)
                        last.then_inc(sem("y_full"), 1)
                    for h in range(2):
                        w("y_ready", 10 * d + 9 + h)
                        settle(pe)
                        for b in range(NB):
                            for s_ in range(2):
                                early = quarter(2 * s_ + d)
                                last = mm(bank[JOINED[h]][early, b * QN:b * QN + QN], TMp[h][early, b, :],
                                          Yp[h][early, b, :], start=True, stop=True)
                        last.then_inc(sem("z_full"), 1)
                    w("z1_ready", 2 * d + 2)
                    w("sc_taken", 6 * d + 6)
                    for h in range(2):
                        w("merged", 10 * d + 9 + h)
                        for b in range(NB):
                            last = mm(bank[2 + h][:, b * P:b * P + P], TT[d][h][:, b, :], Q[h][:, b, :],
                                      start=True, stop=True)
                        last.then_inc(sem("wu_full"), 1)
                    w("wu_ready", 2 * d + 2)
                    settle(pe)
                    for h in range(2):
                        for c in range(8):
                            b, r = c // 2, hd(c % 2)
                            last = mm(bank[4 + c % 2][hd(h), b * C:b * C + C], WU[d][h][r, b, 0:C], Btok[r, b, hd(h)],
                                      start=True, stop=True)
                    last.then_inc(sem("m_full"), 1)
                    for h in range(2):
                        for c in range(8):
                            b, r = c // 2, hd(c % 2)
                            mm(bank[c % 2][hd(h), b * C:b * C + C], Ktok[r, b, hd(h)], Vt[r, b, hd(h)],
                               start=True, stop=False, skip_group_check=True)
                            last = mm(bank[c % 2][hd(h), b * C:b * C + C], Btok[r, b, hd(h)], WU[d][h][r, b, C:P],
                                      start=False, stop=True, skip_group_check=True)
                    last.then_inc(sem("n_full"), 1)
                    for h in range(2):
                        for b in range(2):
                            last = mm(bank[6][hd(h), b * P:b * P + P], WU[d][h][:, 2 + b, 0:C], ARR[h][:, b, :],
                                      start=True, stop=True)
                    last.then_inc(sem("g_full"), 1)
                    for h in range(2):
                        for b in range(2):
                            mm(bank[7][hd(h), b * P:b * P + P], Vt[:, 2 + b, hd(h)], ARR[h][:, 2 + b, :],
                               start=(d == 0 and b == 0), stop=False, skip_group_check=True)
                            last = mm(bank[7][hd(h), b * P:b * P + P], WU[d][h][:, 2 + b, C:P], ARR[h][:, b, :],
                                      start=False, stop=False, skip_group_check=True)
                    last.then_inc(sem("y_local"), 1)
                w("mo_ready", 2)
                for st in range(1, 8):
                    for d in range(2):
                        c = CHUNKS[d][st]
                        w("st_ready", 2 * (st - 1) + d + 1)
                        settle(pe)
                        if st < 7:
                            for h in range(2):
                                last = mm(bank[d][hd(h), 0:C], MO[d][hd(h), c, :], ST[d][hd(h), st, :],
                                          start=True, stop=True)
                            last.then_inc(sem("st_full"), 1)
                        if st >= 4:
                            if st == 4 and d == 0:
                                w("gt_ready", 2)
                                settle(pe)
                            x = (c - 4) * C
                            for h in range(2):
                                last = mm(bank[7][hd(h), x:x + C], ST[d][hd(h), st, :], GT[d][hd(h), x:x + C],
                                          start=False, stop=(st == 7 and d == 1), skip_group_check=True)
                last.then_inc(sem("out_y"), 1)
                w("bonus_in", 1)
                mm(bank[2][:, 0:SEQ], heads1, KD, start=True, stop=True).then_inc(sem("bonus_full"), 1)
                if more:
                    project_keys(i + 1, range(0, 3))
                w("y_copied", 1)
                mm(bank[3][:, 0:SEQ], heads64, YF, start=True, stop=True).then_inc(sem("gn_mean"), 1)
                if more:
                    project_keys(i + 1, range(3, KT))
                w("gn_sq", 1)
                mm(bank[1][:, 0:SEQ], heads64, YS, start=True, stop=True).then_inc(sem("gn_var"), 1)

            pe.wait_ge(sem("pair_done"), 1)
            project_keys(0, range(KT))
            with pe.Fori(0, KT - 1) as i:
                pair(i, True)
            pair(KT - 1, False)
            pe.wait_ge(sem("pair_done"), KT + 1)
            first = STEPS["expert_products"].index("gathered")
            pe.sem_inc(sem("expert_products"), first)
            for m in range(KT):
                if m == 0:
                    pe.wait_ge(sem("ld_out"), 32)
                if m >= 4:
                    pe.wait_ge(sem("residual_done"), 16 + m - 3)
                for k in range(KT):
                    last = pe.matmul(bank[m % 4][:, seg[1]], WO[k][:, m * P:(m + 1) * P], YT[:, k, :],
                                     start=(k == 0), stop=(k == KT - 1))
                last.then_inc(sem("out_full"), 1)
            layer_norm(3, SEQ)
            for n in range(24):
                pe.wait_ge(sem("diag_ready"), n + 1)
                pe.matmul(bank[ROW_BANKS[n // 4]][:, (n % 4) * P:(n % 4) * P + P], ones, diag[n % 2],
                          start=True, stop=True).then_inc(sem("row_full"), 1)
            pe.wait_ge(sem("ld_router"), 16)
            pe.wait_ge(sem("u_ready"), 6)
            for tt in range(2):
                cs = slice(SEQ + tt * P, SEQ + tt * P + P)
                for k in range(KT):
                    last = pe.matmul(bank[0][:, tt * 8:tt * 8 + 8], UT[:, k, cs], rt_w[:, k, :],
                                     start=(k == 0), stop=(k == KT - 1))
            last.then_inc(sem("logits_full"), 1)
            pe.wait_ge(sem("row_taken"), 6)
            for tt in range(2):
                for k in range(KT):
                    last = pe.transpose(bank[1 + 2 * tt + k // 4][:, (k % 4) * P:(k % 4) * P + P],
                                        XT[:, k, SEQ + tt * P:SEQ + tt * P + P], ident)
            last.then_inc(sem("tok_full"), 1)
            for tt in range(2):
                for k in range(KT):
                    b = (5, 6, 7, 1)[2 * tt + k // 4]
                    if b == 1 and k == 4:
                        last.then_inc(sem("tok_full"), 1)
                        pe.wait_ge(sem("tok_taken"), 1)
                    last = pe.transpose(bank[b][:, (k % 4) * P:(k % 4) * P + P],
                                        UT[:, k, SEQ + tt * P:SEQ + tt * P + P], ident)
            last.then_inc(sem("tok_full"), 1)
            pe.wait_ge(sem("routed"), 1)
            places = bank[0][:, 16:40]
            pe.matmul(places[:, 0:8], before, chosen[:, 0, :], start=True, stop=True)
            pe.matmul(places[:, 8:16], ones, chosen[:, 0, :], start=True, stop=False)
            pe.matmul(places[:, 8:16], before, chosen[:, 1, :], start=False, stop=True)
            pe.matmul(places[:, 16:24], ones, chosen[:, 0, :], start=True, stop=False)
            pe.matmul(places[:, 16:24], ones, chosen[:, 1, :], start=False, stop=True).then_inc(sem("places_full"), 1)
            def gather(item):
                step(pe, "expert_vectors", "pick", item - 1)
                for k in range(KT):
                    for tt in range(2):
                        last = pe.matmul(bank[6 + k // 4][:, (k % 4) * P:(k % 4) * P + P],
                                         UTOK[:, tt, k * P:(k + 1) * P], pick[:, tt, :], start=(tt == 0), stop=(tt == 1))
                last.then_inc(sem("expert_products"), 1)

            def loaded(q, item):
                s = slot_of(q)
                pe.wait_ge(sem(f"ew_loaded{s}"), 48 * item + 16 * (q // ERN + 1))
                return ering[s]

            def hidden_products(j, r, item):
                s_, b, name = slot_of(3 * j + r), 2 * (j % 2) + r, ("gate", "up")[r]
                if j == 0 and r == 0:
                    step(pe, "expert_vectors", "xg_low", item - 1)
                if j < 2:
                    step(pe, "expert_vectors", f"added{b}", item - 1)
                else:
                    step(pe, "expert_vectors", f"h{j - 2}", item)
                for i_ in range(PIECES):
                    step(pe, "expert_vectors", f"low_{name}{j}_{i_}", item)
                    for k in (2 * i_, 2 * i_ + 1):
                        wh, wl = high[i_][:, k % 2, :], low[s_][:, k, :]
                        pe.matmul(bank[b][:, :], XGH[:, k, :], wh, start=(k == 0), stop=False)
                        pe.matmul(bank[b][:, :], XGH[:, k, :], wl, start=False, stop=False)
                        last = pe.matmul(bank[b][:, :], XGL[:, k, :], wh, start=False, stop=(k == KT - 1))
                    last.then_inc(sem("expert_products"), 1)

            def turn_hidden(j, item):
                step(pe, "expert_vectors", f"h{j}", item)
                if j:
                    step(pe, "expert_copies", f"hidden{j - 1}", item)
                for f in range(4):
                    last = pe.transpose(bank[6][:, f * P:f * P + P], HTOK[j % 2][:, f * P:f * P + P], ident)
                last.then_inc(sem("expert_products"), 1)

            def down_products(j, item):
                w_ = loaded(3 * j + 2, item).rearrange("p a b -> p (a b)").rearrange("p (a b) -> p a b", b=D)
                step(pe, "expert_copies", f"hidden{j}", item)
                for f in range(4):
                    for half in range(2):
                        last = pe.matmul(bank[4 + half][:, :], HT[j % 2][:, f, :], w_[:, f, half * 512:half * 512 + 512],
                                         start=(j == 0 and f == 0), stop=(j == EJ - 1 and f == 3))
                last.then_inc(sem("expert_products"), 1)

            pe.wait_ge(sem("tok_taken"), 8)
            gather(0)
            step(pe, "expert_copies", "xg_high", -1)
            pe.sem_inc(sem("expert_products"), len(STEPS["expert_products"]) - first - 1)
            pe.wait_ge(sem("routed"), 2)
            n_passes = pe.value_load(passes[0:1, 0:1], min_val=1, max_val=2)
            with pe.Fori(0, n_passes) as p:
                with pe.Fori(0, N_EXP) as e:
                    item = p * N_EXP + e
                    for j in range(EJ):
                        hidden_products(j, 0, item)
                        if j:
                            turn_hidden(j - 1, item)
                        if j == 4:
                            step(pe, "expert_vectors", "share", item)
                            for tt in range(2):
                                last = pe.transpose(bank[7][:, tt * P:tt * P + P], share[:, tt, :], ident)
                            last.then_inc(sem("expert_products"), 1)
                        hidden_products(j, 1, item)
                        if j:
                            down_products(j - 1, item)
                    turn_hidden(EJ - 1, item)
                    down_products(EJ - 1, item)
                    gather(item + 1)
                    for o in range(4):
                        tt, half = divmod(o, 2)
                        if o < 2:
                            step(pe, "expert_vectors", f"yg{half}", item)
                        pe.matmul(bank[o][:, :], shareT[:, tt, :], YG[:, half * 512:half * 512 + 512],
                                  start=True, stop=True).then_inc(sem("expert_products"), 1)

        @block.scalar
        def _(act):
            def load(name, dst, src):
                act.dma_start(dst, src).then_inc(sem(name), 16)

            load("ld_filter", hw1[0:HY_EMB, :], a["hy_f_w1"])
            load("ld_filter", hw2[0:HY_W, :], a["hy_f_w2"])
            for j, s in enumerate([a["hy_f_b1"], a["hy_f_b2"], a["hy_f_freq"][0], a["hy_f_freq"][1]]):
                load("ld_filter", hcol[0:HY_W, j:j + 1], s.rearrange("(p o) -> p o", o=1))
            load("ld_filter", w3[0:HY_W, :], a["hy_f_w3"])
            load("ld_filter", dec[0:1, :], a["hy_decay"].rearrange("a (o b) -> o (a b)", o=1))
            load("ld_filter", skip[0:1, :], a["hy_skip"].rearrange("a (o b) -> o (a b)", o=1))
            load("ld_x", xin[:, 0:2, :], a["ctx"][0].rearrange("(t p) d -> p t d", p=P))
            load("ld_x", xin[:, 2:4, :], a["x"][0].rearrange("(t p) d -> p t d", p=P))
            load("ld_table", arena[:, table:table + 2 * T + 4 * SEQ + 2 * SEQ + 1], consts[1])

            link = Chain(act, sem("act_chain"))
            pe_x = sem("x_turned")
            act.wait_ge(sem("vec_ready"), 1)
            link(act.activation(silu_c[:, :, 0], vec[:, 3 * P + 72:3 * P + 80], ACT.Silu))
            act.activation(silu_c[:, :, 1], vec[:, 3 * P + 80:3 * P + 88], ACT.Silu).then_inc(sem("silu_ready"), 1)
            for k in range(KT):
                act.wait_ge(pe_x, k + 1)
                act.copy(XT[:, k, :], bank[1 + k % 4][:, :]).then_inc(sem("x_taken"), 1)
            act.wait_ge(sem("ld_filter"), 16 * 9)
            act.activation(dec[0:1, :], dec[0:1, :], ACT.Abs).then_inc(sem("decay_abs"), 1)
            for j in range(2):
                act.wait_ge(sem("sine_arg"), j + 1)
                act.activation(hargs[2 + j][0:HY_W, :], hargs[1][0:HY_W, :], ACT.Sin).then_inc(sem("sine_out"), 1)
            for n in range(2):
                for q in range(4):
                    g = 4 * n + q
                    act.wait_ge(sem("filter_full"), g + 1)
                    if g >= 1:
                        act.wait_ge(sem("filter_taken"), g)
                    for j in range(2):
                        act.activation(win_f[j], bank[4 * (g % 2) + 2 + j][:, :], ACT.Exp).then_inc(sem("window"), 1)
                for o in range(8):
                    act.wait_ge(sem("spectrum_full"), 8 * n + o + 1)
                    c, f, half = o // 4, o // 2 % 2, o % 2
                    act.copy(KSP[:, 4 * n + 2 * c + f, half * 512:half * 512 + 512], bank[o][:, :])\
                        .then_inc(sem("spectrum_taken"), 1)

            def modulation(layer):
                dst = [mod_rows0, mod_rows1][layer]
                act.sem_inc(sem("mod_taken"), 6)

                def round_(c0, j):
                    act.wait_ge(sem("mod_full"), c0 + j + 1 + 24 * layer)
                    b = (ring_start[layer] + j) % RN
                    act.copy(dst[0:2, bass.ds((c0 + j) * 256, 256)], bank[b][0:2, 0:256]).then_inc(sem("mod_taken"), 1)
                if layer == 1:
                    for j in range(RN):
                        round_(0, j)
                    ln_squares(2)
                    for j in range(RN):
                        round_(RN, j)
                    ln_scale(2, 0, 1)
                with act.Fori(2 * layer, 4) as i:
                    for j in range(RN):
                        round_(i * RN, j)
            modulation(0)

            def ln_squares(n, width=T):
                cols = slice(T - width, T)
                for k in range(KT):
                    act.wait_ge(sem("ln_centred"), 8 * (n - 1) + k + 1)
                    act.activation(SQ[:, k, 0:width], XT[:, k, cols], ACT.Square).then_inc(sem("ln_square"), 1)

            def ln_scale(n, layer, j, width=T):
                cols = slice(T - width, T)
                act.wait_ge(sem("ln_var"), n)
                act.activation(std[:, 0:width], bank[ln_banks(n)[1]][:, 0:width], ACT.Sqrt, bias=eps[:, 0:1]).then_inc(sem("ln_std"), 1)
                for k in range(KT):
                    act.wait_ge(sem("ln_scaled"), 8 * (n - 1) + k + 1)
                    act.activation(XT[:, k, cols], XT[:, k, cols], ACT.Identity,
                                   bias=col("ln_b", (2 * layer + j) * KT + k)).then_inc(sem("ln_done"), 1)

            def layer_norm(n, layer, j, width=T):
                ln_squares(n, width)
                ln_scale(n, layer, j, width)

            for m in range(24):
                act.wait_ge(sem("proj_full"), m + 1)
                if m >= 2:
                    act.wait_ge(sem("conv_done"), m - 1)
                act.activation(pad[m % 2][:, :, 1:SEQ + 1], bank[m % 4][:, :].rearrange("p (s t) -> p s t", s=2),
                               ACT.Identity, bias=col("hy_b_in", m)).then_inc(sem("proj_taken"), 1)
                if 1 <= m <= KT:
                    act.wait_ge(sem("v_turned"), m)
                    act.copy(ZT[:, :, (m - 1) * P:m * P], bank[4 + (m - 1) % 2][:, :].rearrange("p (t c) -> p t c", t=NB))\
                        .then_inc(sem("v_taken"), 1)
            for k in range(KT):
                act.wait_ge(sem("z_turned"), k + 1)
                act.copy(ZT[:, :, k * P:(k + 1) * P], bank[k % 4][:, :].rearrange("p (t c) -> p t c", t=NB))\
                    .then_inc(sem("z_taken"), 1)
            rw = Ring(act, w_loaded)
            rw.n = ffn_start

            def upper(f):
                s = rw.loaded_slot()
                act.wait_ge(up_loaded[s], rw.it16 + 16 * ((rw.n - 1 - ffn_start) // RN + 1))
                if not isinstance(f, int) or f >= 2:
                    act.wait_ge(sem("hidden_taken"), f + 1)
                act.copy(WH[s % 2], ring[s].rearrange("p (c n) -> p c n", n=P)).then_inc(sem("ffn_high"), 1)
                return s
            act.wait_ge(sem("long_taken"), 32)
            upper(0)
            layer_norm(1, 0, 0)
            for g in range(2):
                act.wait_ge(sem("u_ready"), 3 + g)
                act.copy(UH[g], UT[:, 4 * g:4 * g + 4, :]).then_inc(sem("u_high"), 1)
            def silu(f, j):
                act.wait_ge(sem("hidden_full"), f + 1)
                act.wait_ge(sem("sil_free"), f + 1)
                act.activation(sil[j % 2], bank[2 * ((ffn_start + j) % 2)][:, :], ACT.Silu).then_inc(sem("sil_ready"), 1)
            rw.read_loop(FT - 1, lambda f: silu(f, upper(f + 1) - 1 - ffn_start))
            silu(FT - 1, FT - 1)
            for c in range(FT // 2):
                s = rw.loaded_slot()
                act.wait_ge(sem("hidden_full"), FT + c - 1)
                act.copy(WH[s % 2], ring[s].rearrange("p (c n) -> p c n", n=P)).then_inc(sem("ffn_high"), 1)
                act.wait_ge(sem("hidden_mult"), 2 * c + 2)
                act.copy(HH[c % 2], H[:, 2 * c:2 * c + 2, :]).then_inc(sem("ffn_high"), 1)
            modulation(1)
            act.wait_ge(sem("lora_full"), 1)
            act.activation(HW, bank[0][:, :], ACT.Tanh).then_inc(sem("lora_taken"), 1)
            act.wait_ge(sem("lora_full"), 2)
            act.copy(HA, bank[1][:, :]).then_inc(sem("lora_taken"), 1)
            act.wait_ge(sem("lora_full"), 3)
            act.activation(G1a, bank[2][:, 0:SEQ], ACT.Sigmoid).then_inc(sem("lora_taken"), 1)
            act.activation(G1b[0:32, :], bank[3][0:32, 0:SEQ], ACT.Sigmoid).then_inc(sem("lora_taken"), 1)
            with act.Fori(0, KT) as i:
                w = waiter(act, i)
                w("proj", 1)
                w("pair_done", 1)
                act.copy(Kf, bank[0][:, :]).then_inc(sem("k_copied"), 1)
                for d in range(2):
                    w("proj", 2 * d + 2)
                    act.activation(SG[d], bank[3 + d][:, :], ACT.Sigmoid, bias=dcol("rw_w0", i + 8 * d))\
                        .then_inc(sem("sg"), 1)
                    w("proj", 2 * d + 3)
                    act.activation(AS[d], bank[5 + d][:, :], ACT.Sigmoid, bias=dcol("rw_a0", i + 8 * d))\
                        .then_inc(sem("rate"), 1)
                for d in range(2):
                    if d == 1:
                        w("proj", 6)
                        act.copy(Rf, bank[2][:, 0:SEQ]).then_inc(sem("r_copied"), 1)
                        w("ksum", 1)
                        act.activation(KS, bank[0][:, :], ACT.Ln, bias=eps[:, 2:3]).then_inc(sem("logs"), 1)
                        w("logs", 1)
                        act.activation(KS, KS, ACT.Exp, scale=-0.5).then_inc(sem("kstd"), 1)
                        w("proj", 7)
                        act.copy(Vf, bank[1][:, :]).then_inc(sem("v_copied"), 1)
                        w("proj", 8)
                        act.copy(Gf, bank[7][:, 0:SEQ]).then_inc(sem("g_copied"), 1)
                        w("vt_full", 1)
                        act.copy(Vt, b4(1)).then_inc(sem("vt_ready"), 1)
                    w("decayed", d + 1)
                    if d == 1:
                        w("k_t", 1)
                        w("r_t", 1)
                    act.activation(EP, CS, ACT.Exp, scale=-DECAY).then_inc(sem("e_incl"), 1)
                    act.activation(EN, CS, ACT.Exp, scale=DECAY).then_inc(sem("e_inv"), 1)
                    w("excl", d + 1)
                    act.activation(EX, SG[d], ACT.Exp, scale=-DECAY).then_inc(sem("e_excl"), 1)
                for d in range(2):
                    w("tr_full", 3 * d + 1)
                    for h in range(2):
                        if d == 1:
                            w("wu_full", h + 1)
                        act.copy(Q[h][:, :, 0:C], b4(2)[:, :, hd(h)]).then_inc(sem("q_ready"), 1)
                    w("tr_full", 3 * d + 2)
                    if d == 1:
                        w("n_full", 1)
                    act.copy(Btok, b4(3)).then_inc(sem("bk_ready"), 1)
                    w("tr_full", 3 * d + 3)
                    act.copy(Ktok, b4(4)).then_inc(sem("bk_ready"), 1)
                    for h in range(2):
                        w("sc_taken", 6 * d + h + 1)
                        for s_ in range(2):
                            late, early = quarter(2 * s_ + 1 - d), quarter(2 * s_ + d)
                            last = act.copy(Aoff[h][late, :, :], b4(h)[late, :, early])
                        last.then_inc(sem("off_ready"), 1)
                    for n in range(10 * d + 1, 10 * d + 11):
                        h = (n - 1) % 2
                        w("y_full", n)
                        if n > 2:
                            w("z_full", n - 2)
                        act.copy(Yp[h], packed(h)).then_inc(sem("y_ready"), 1)
                        if n == 10 * d + 2:
                            w("z1_full", 2 * d + 2)
                            for g in range(2):
                                act.copy(Q[g][:, :, C:P], bank[5][:, g * NB * C:(g + 1) * NB * C]
                                         .rearrange("p (b c) -> p b c", b=NB)).then_inc(sem("z1_ready"), 1)
                    for h in range(2):
                        w("wu_full", 2 * d + h + 1)
                        act.copy(WU[d][h], b4(2 + h)).then_inc(sem("wu_ready"), 1)
                w("out_y", 1)
                act.copy(YF, bank[7][:, 0:SEQ]).then_inc(sem("y_copied"), 1)
                w("gn_cent", 1)
                act.activation(YS, YN, ACT.Square).then_inc(sem("gn_sq"), 1)
                w("gn_var", 1)
                act.activation(YS, bank[1][:, 0:SEQ], ACT.Ln, bias=eps[:, 1:2]).then_inc(sem("logs"), 1)
                w("logs", 2)
                act.activation(YS, YS, ACT.Exp, scale=-0.5).then_inc(sem("gn_std"), 1)
            layer_norm(3, 1, 0, SEQ)
            for n in range(6):
                act.wait_ge(sem("row_full"), 4 * n + 4)
                row = (rowG, rowg, rowb)[n // 2]
                act.copy(row[:, (n % 2) * 512:(n % 2) * 512 + 512], bank[ROW_BANKS[n]][:, :]).then_inc(sem("row_taken"), 1)
            act.wait_ge(sem("tok_full"), 1)
            for tt in range(2):
                for h in range(2):
                    act.copy(XTOK[:, tt, h * 512:h * 512 + 512], bank[1 + 2 * tt + h][:, :]).then_inc(sem("tok_taken"), 1)
            act.wait_ge(sem("gap"), 1)
            act.activation(w12[:, :, 1:2], w12[:, :, 0:1], ACT.Exp).then_inc(sem("gap_exp"), 1)
            for tt in range(2):
                for h in range(2):
                    act.wait_ge(sem("tok_full"), 2 if 2 * tt + h < 3 else 3)
                    act.copy(UTOK[:, tt, h * 512:h * 512 + 512], bank[(5, 6, 7, 1)[2 * tt + h]][:, :])\
                        .then_inc(sem("tok_taken"), 1)
            def copy_gathered(item):
                step(act, "expert_products", "gathered", item - 1)
                for g in range(2):
                    last = act.copy(XGH[:, 4 * g:4 * g + 4, :].rearrange("p a b -> p (a b)"), bank[6 + g][:, :])
                last.then_inc(sem("expert_copies"), 1)

            def copy_hidden(j, item):
                step(act, "expert_products", f"turned{j}", item)
                act.copy(HT[j % 2].rearrange("p a b -> p (a b)"), bank[6][:, :]).then_inc(sem("expert_copies"), 1)

            def high_digits(j, r, item):
                s_, name = slot_of(3 * j + r), ("gate", "up")[r]
                act.wait_ge(sem(f"ew_loaded{s_}"), 48 * item + 16 * ((3 * j + r) // ERN + 1))
                for i_ in range(PIECES):
                    former = f"gate{j}_{i_}" if r else f"up{(j - 1) % EJ}_{i_}"
                    step(act, "expert_products", former, item - (1 if j == 0 and r == 0 else 0))
                    act.copy(high[i_], ering[s_][:, 2 * i_:2 * i_ + 2, :]).then_inc(sem("expert_copies"), 1)

            act.sem_inc(sem("expert_copies"), len(STEPS["expert_copies"]) - 1)
            copy_gathered(0)
            act.wait_ge(sem("routed"), 2)
            n_passes = act.value_load(passes[0:1, 0:1], min_val=1, max_val=2)
            with act.Fori(0, n_passes) as p:
                with act.Fori(0, N_EXP) as e:
                    item = p * N_EXP + e
                    high_digits(0, 0, item)
                    for j in range(EJ):
                        high_digits(j, 1, item)
                        step(act, "expert_products", f"gate{j}_{PIECES - 1}", item)
                        step(act, "expert_vectors", f"h{(j - 2) % EJ}", item - (1 if j < 2 else 0))
                        act.activation(sil2[j % 2], bank[2 * (j % 2)][:, :], ACT.Silu).then_inc(sem("expert_copies"), 1)
                        if j:
                            copy_hidden(j - 1, item)
                        if j == 4:
                            step(act, "expert_products", "shares_turned", item)
                            act.copy(shareT.rearrange("p a b -> p (a b)"), bank[7][:, 0:2 * P])\
                                .then_inc(sem("expert_copies"), 1)
                        if j < EJ - 1:
                            high_digits(j + 1, 0, item)
                    copy_hidden(EJ - 1, item)
                    copy_gathered(item + 1)
            for tt in range(2):
                act.wait_ge(sem("fin_centred"), tt + 1)
                act.activation(XTOK[:, tt, :], OUT[:, tt, :], ACT.Square, accum_out=stat[:, tt, 1:2])\
                    .then_inc(sem("fin_square"), 1)
                act.wait_ge(sem("fin_square"), tt + 1)
                act.activation(stat[:, tt, 2:3], stat[:, tt, 1:2], ACT.Sqrt, bias=eps[:, 0:1], scale=1.0 / D)\
                    .then_inc(sem("fin_std"), 1)

        @block.gpsimd
        def _(pool):
            for n in range(2):
                for q in range(4):
                    g = 4 * n + q
                    half, tt = q // 2, q % 2
                    pool.wait_ge(sem("taps"), g + 1)
                    if q == 0 and n == 1:
                        pool.wait_ge(sem("spectrum_full"), 8)
                    cs = slice(half * 512, half * 512 + 512)
                    pool.tensor_tensor(kcs[:, 0, tt, cs], pr[0], pr[1], ALU.add).then_inc(sem("pool_taps"), 1)
                    pool.tensor_tensor(kcs[:, 1, tt, cs], pr[0], pr[1], ALU.subtract).then_inc(sem("taps_ready"), 1)
            for g in range(8):
                for f in range(2):
                    pool.wait_ge(sem("bins_mult"), 4 * g + 2 * f + 1)
                    if f == 0 and g >= 2:
                        pool.wait_ge(sem("long_full"), 4 * (g - 1))
                    pool.tensor_tensor(Y[:, g % 2, f, :], pr[0], pr[1], ALU.subtract).then_inc(sem("pool_re"), 1)
                    pool.wait_ge(sem("bins_mult"), 4 * g + 2 * f + 2)
                    pool.tensor_tensor(Y[:, g % 2, 2 + f, :], pr[2], pr[3], ALU.add)\
                        .then_inc(sem("pool_im"), 1)
                pool.wait_ge(sem("pool_re"), 2 * g + 2)
                pool.wait_ge(sem("pool_im"), 2 * g + 2)
                pool.sem_inc(sem("product_ready"), 1)
            pool.wait_ge(sem("ld_table1"), 32)
            with pool.Fori(0, KT) as i:
                w = waiter(pool, i)
                w("kk_raw", 1)
                pool.tensor_tensor(KS, KK, KK, ALU.mult).then_inc(sem("ksq"), 1)
                for d in range(2):
                    w("decayed", d + 1)
                    pool.tensor_tensor(SG[d], CS, SG[d], ALU.subtract).then_inc(sem("excl"), 1)
                    w("kk_ready", 1)
                    w("rate_used", d + 1)
                    pool.tensor_tensor(AS[d], KK, AS[d], ALU.mult).then_inc(sem("b_raw"), 1)
            pool.wait_ge(sem("pair_done"), KT + 1)
            for n in range(24):
                k = n % 8
                c_ = (mv(1, 5, k, 1), col("ln_g", 24 + k), col("ln_b", 24 + k))[n // 8]
                if n >= 2:
                    pool.wait_ge(sem("row_full"), n - 1)
                pool.tensor_scalar(diag[n % 2], ident, c_, None, ALU.mult).then_inc(sem("diag_ready"), 1)

        @block.vector
        def _(dve):
            link = Chain(dve, sem("dve_chain"))
            link(dve.memset(eps[:, 0:1], LN_EPS))
            link(dve.memset(eps[:, 1:2], RW_GN_EPS))
            link(dve.memset(eps[:, 2:3], 1e-6))
            link(dve.memset(eps[:, 3:4], 0.0))
            dve.wait_ge(sem("rows_turned"), 1)
            for j, n in enumerate(ROW_FILL):
                last = dve.tensor_copy(vec[:, j * P:j * P + n], bank[0][:, j * P:j * P + n])
            last.then_inc(sem("vec_ready"), 1)
            dve.wait_ge(sem("ld_filter"), 16 * 9)
            dve.wait_ge(sem("ld_table"), 16)
            magic = float(1.5 * 2 ** 23)
            for j in range(2):
                dve.wait_ge(sem("sine_in"), j + 1)
                arg, t = hargs[0][0:HY_W, :], hargs[1][0:HY_W, :]
                if j == 1:
                    dve.wait_ge(sem("sine_out"), 1)
                link(dve.tensor_scalar(arg, bank[5 + j][0:HY_W, 0:SEQ], hcol[0:HY_W, j:j + 1],
                                       hcol[0:HY_W, 2 + j:3 + j], ALU.add, ALU.mult))
                link(dve.tensor_scalar(t, arg, 1.0 / (2 * math.pi), magic, ALU.mult, ALU.add))
                link(dve.tensor_scalar(t, t, magic, None, ALU.subtract))
                link(dve.scalar_tensor_tensor(out=arg, in0=t, scalar=-6.28125, in1=arg, op0=ALU.mult, op1=ALU.add))
                link(dve.scalar_tensor_tensor(out=arg, in0=t, scalar=-(2 * math.pi - 6.28125), in1=arg,
                                              op0=ALU.mult, op1=ALU.add))
                dve.tensor_scalar(t, arg, -3.1415925, 3.1415925, ALU.max, ALU.min).then_inc(sem("sine_arg"), 1)
            for n in range(2):
                for q in range(4):
                    g = 4 * n + q
                    half, tt = q // 2, q % 2
                    b = 4 * (g % 2)
                    dve.wait_ge(sem("window"), 2 * g + 2)
                    if g >= 1:
                        dve.wait_ge(sem("taps_ready"), g)
                        dve.wait_ge(sem("pool_taps"), g)
                    link(dve.tensor_tensor(pr[0], bank[b][:, :], win_f[0], ALU.mult))
                    if tt == 0:
                        link(dve.tensor_tensor(pr[0][0:1, :], pr[0][0:1, :],
                                               skip[0:1, n * D + half * 512:n * D + half * 512 + 512], ALU.add))
                        link(dve.scalar_tensor_tensor(out=pr[1], in0=bank[b + 1][:, :], scalar=notfirst,
                                                      in1=win_f[1], op0=ALU.mult, op1=ALU.mult))
                    else:
                        link(dve.tensor_tensor(pr[1], bank[b + 1][:, :], win_f[1], ALU.mult))
                    dve.sem_inc(sem("taps"), 1)
                    dve.sem_inc(sem("filter_taken"), 1)

            def modulation(layer):
                dve.wait_ge(sem("mod_turned"), layer + 1)
                name = f"mod_b{layer}"
                tile, first, n = ROWS[name]
                bias = vec[:, tile * P + first:tile * P + first + n]
                ps = bank[6][:, 0:96].rearrange("p (j s) -> p j s", s=2)
                for s in range(2):
                    link(dve.tensor_tensor(modv[layer][:, :, s], ps[:, :, s], bias, ALU.add))
                for ch in (1, 4):
                    v = modv[layer][:, ch * KT:(ch + 1) * KT, :]
                    link(dve.tensor_scalar(v, v, 1.0, None, ALU.add))
            modulation(0)

            def modulate(layer, first, streams=(0, 1)):
                for k in range(KT):
                    for s in streams:
                        last = dve.tensor_scalar(UT[:, k, seg[s]], XT[:, k, seg[s]], mv(layer, first + 1, k, s),
                                                 mv(layer, first, k, s), ALU.mult, ALU.add)
                    if k % (KT // 2) == KT // 2 - 1:
                        last.then_inc(sem("u_ready"), 1)

            def layer_norm(n, layer, j, width=T):
                cols = slice(T - width, T)
                dve.wait_ge(sem("ln_mean"), n)
                for k in range(KT):
                    dve.tensor_tensor(XT[:, k, cols], XT[:, k, cols], bank[ln_banks(n)[0]][:, 0:width], ALU.subtract)\
                        .then_inc(sem("ln_centred"), 1)
                dve.wait_ge(sem("ln_std"), n)
                dve.wait_ge(sem("ln_centred"), 8 * n)
                link(dve.reciprocal(rstd[:, 0:width], std[:, 0:width]))
                for k in range(KT):
                    dve.scalar_tensor_tensor(out=XT[:, k, cols], in0=XT[:, k, cols],
                                             scalar=col("ln_g", (2 * layer + j) * KT + k), in1=rstd[:, 0:width],
                                             op0=ALU.mult, op1=ALU.mult).then_inc(sem("ln_scaled"), 1)
                dve.wait_ge(sem("ln_done"), 8 * n)

            def residual(n, layer, gate, bias, b0, streams=(0, 1), banks=4):
                for m in range(KT):
                    dve.wait_ge(sem("out_full"), 8 * (n - 1) + m + 1)
                    t = rt[m % 2]
                    for s in streams:
                        g = mv(layer, gate, m, s)
                        ps = bank[b0 + m % banks][:, seg[s]]
                        if bias:
                            link(dve.tensor_scalar(t[:, seg[s]], ps, col(bias, m), g, ALU.add, ALU.mult))
                        else:
                            link(dve.tensor_scalar(t[:, seg[s]], ps, g, None, ALU.mult))
                    c = slice(SEQ * streams[0], T)
                    dve.scalar_tensor_tensor(out=XT[:, m, c], in0=XT[:, m, c], scalar=float(ALPHA), in1=t[:, c],
                                             op0=ALU.mult, op1=ALU.add).then_inc(sem("residual_done"), 1)

            dve.wait_ge(sem("spectrum_full"), 16)
            modulate(0, 0)
            for p_ in pad:
                link(dve.memset(p_[:, :, 0:1], 0.0))
                link(dve.memset(p_[:, :, SEQ + 1:SEQ + 2], 0.0))
            for m in range(24):
                dve.wait_ge(sem("proj_taken"), m + 1)
                dst = (cv[m % 2] if m < 8 else X1[:, m - 8, :] if m < 16 else X2[:, m - 16, :])
                dst = dst.rearrange("p (s t) -> p s t", s=2)
                pd = pad[m % 2]
                if 2 <= m < 8:
                    dve.wait_ge(sem("v_turned"), m - 1)
                link(dve.tensor_scalar(dst, pd[:, :, 1:SEQ + 1], col("hy_conv_w", 24 + m), col("hy_conv_b", m),
                                       ALU.mult, ALU.add))
                link(dve.scalar_tensor_tensor(out=dst, in0=pd[:, :, 0:SEQ], scalar=col("hy_conv_w", m), in1=dst,
                                              op0=ALU.mult, op1=ALU.add))
                dve.scalar_tensor_tensor(out=dst, in0=pd[:, :, 2:SEQ + 2], scalar=col("hy_conv_w", 48 + m), in1=dst,
                                         op0=ALU.mult, op1=ALU.add).then_inc(sem("conv_done"), 1)
            dve.wait_ge(sem("conv_done"), 24)

            def products(n, g):
                half, s = g // 2, g % 2
                cs = slice(half * 512, half * 512 + 512)
                dve.wait_ge(sem("bins_full"), 4 * n + g + 1)
                for f in range(2):
                    re, im = bank[f][:, :], bank[2 + f][:, :]
                    kr, ki = KSP[:, 4 * n + f, cs], KSP[:, 4 * n + 2 + f, cs]
                    u = 2 * (4 * n + g) + f
                    if u >= 1:
                        dve.wait_ge(sem("pool_re"), u)
                    dve.tensor_tensor(pr[0], re, kr, ALU.mult)
                    link(dve.tensor_tensor(pr[1], im, ki, ALU.mult))
                    dve.sem_inc(sem("bins_mult"), 1)
                    if u >= 1:
                        dve.wait_ge(sem("pool_im"), u)
                    dve.tensor_tensor(pr[2], re, ki, ALU.mult)
                    link(dve.tensor_tensor(pr[3], im, kr, ALU.mult))
                    dve.sem_inc(sem("bins_mult"), 1)
                dve.sem_inc(sem("bins_taken"), 1)

            def gating(n, g):
                half, s = g // 2, g % 2
                X = [X1, X2][n]
                for ct in range(4):
                    dve.wait_ge(sem("long_full"), 16 * n + 4 * g + ct + 1)
                    x = X[:, 4 * half + ct, seg[s]]
                    dve.tensor_tensor(x, x, bank[4 + ct][:, 0:SEQ], ALU.mult).then_inc(sem("long_taken"), 1)

            for n in range(2):
                for g in range(5):
                    if g < 4:
                        products(n, g)
                    if g >= 1:
                        gating(n, g - 1)
            residual(1, 0, 2, "hy_b_out", 0)

            def lower(f, j):
                s = (ffn_start + j) % RN
                dve.wait_ge(sem("ffn_high"), f + 1)
                dve.tensor_tensor(WL[s], ring[s].rearrange("p (c n) -> p c n", n=P), WH[s % 2].bitcast(F32),
                                  ALU.subtract).then_inc(sem("ffn_low"), 1)
            lower(0, 0)
            layer_norm(1, 0, 0)
            modulate(0, 3)
            for g in range(2):
                dve.wait_ge(sem("u_high"), g + 1)
                dve.tensor_tensor(UL[g], UT[:, 4 * g:4 * g + 4, :], UH[g].bitcast(F32), ALU.subtract)\
                    .then_inc(sem("ffn_low"), 1)

            dve.sem_inc(sem("hidden_taken"), 2)
            dve.sem_inc(sem("sil_free"), 2)

            def hid(f, j):
                dve.wait_ge(sem("sil_ready"), f + 1)
                dve.tensor_tensor(Hf[:, bass.ds(f * T, T)], sil[j % 2],
                                  bank[2 * ((ffn_start + j) % 2) + 1][:, :], ALU.mult).then_inc(sem("hidden_mult"), 1)
                dve.wait_ge(sem("hidden_mult"), f + 1)
                dve.sem_inc(sem("hidden_taken"), 1)
                dve.sem_inc(sem("sil_free"), 1)
            with_loop(dve, FT - 1, lambda f, j: (lower(f + 1, j + 1), hid(f, j)))
            hid(FT - 1, FT - 1)
            for c in range(FT // 2):
                s = (ffn_start + FT + c) % RN
                dve.wait_ge(sem("ffn_high"), FT + 2 * c + 1)
                dve.tensor_tensor(WL[s], ring[s].rearrange("p (c n) -> p c n", n=P), WH[s % 2].bitcast(F32),
                                  ALU.subtract).then_inc(sem("ffn_low"), 1)
                dve.wait_ge(sem("ffn_high"), FT + 2 * c + 2)
                dve.tensor_tensor(HL[c], H[:, 2 * c:2 * c + 2, :], HH[c % 2].bitcast(F32), ALU.subtract)\
                    .then_inc(sem("ffn_low"), 1)
            residual(2, 0, 5, None, 0, banks=8)
            layer_norm(2, 0, 1)
            modulation(1)
            for k in range(KT):
                for s in range(2):
                    dve.tensor_scalar(UP[:, k, s, 1:SEQ + 1], XT[:, k, seg[s]], mv(1, 1, k, s), mv(1, 0, k, s),
                                      ALU.mult, ALU.add)
            link(dve.memset(UP[:, :, :, 0:1], 0.0))
            link(dve.memset(UP[:, :, :, SEQ + 1:SEQ + 2], 0.0))

            def two(v):
                return v.rearrange("p (s t) -> p s t", s=2)
            for k in range(KT):
                dve.tensor_tensor(two(XX[:, k, :]), UP[:, k, :, 0:SEQ], UP[:, k, :, 2:SEQ + 2], ALU.add)
            link(dve.memset(eps[:, 3:4], 0.0))
            for k in range(KT):
                last = dve.scalar_tensor_tensor(out=two(XX[:, k, :]), in0=two(XX[:, k, :]), scalar=0.5,
                                                in1=UP[:, k, :, 1:SEQ + 1], op0=ALU.mult, op1=ALU.subtract)
            link(last)

            def mix_tile(dst, j, k):
                return dve.scalar_tensor_tensor(out=two(dst[:, k, :]), in0=two(XX[:, k, :]),
                                                scalar=col("rw_mu", j * KT + k), in1=UP[:, k, :, 1:SEQ + 1],
                                                op0=ALU.mult, op1=ALU.add)

            def mix(dst, j):
                for k in range(KT):
                    last = mix_tile(dst, j, k)
                return last

            def mix_x(dst, j):
                for k in range(KT):
                    last = dve.scalar_tensor_tensor(out=dst[:, k, 0:SEQ], in0=XX[:, k, seg[1]],
                                                    scalar=col("rw_mu", j * KT + k), in1=UP[:, k, 1, 1:SEQ + 1],
                                                    op0=ALU.mult, op1=ALU.add)
                return last
            for dst, which in ((XM, 1), (XV, 4)):
                for k in range(KT):
                    mix_tile(dst, which, k).then_inc(sem("xm_ready"), 1)
            mix(XK, 2)
            dve.wait_ge(sem("lora_full"), 1)
            mix_x(XM, 5).then_inc(sem("xm_ready"), 1)
            link(mix_x(XR, 0))
            dve.wait_ge(sem("lora_full"), 2)
            link(mix(XV, 3))
            tile, first, n = ROWS["rw_k_a"]
            link(dve.tensor_scalar(one_ka, vec[:, tile * P + first:tile * P + first + n], -1.0, 1.0, ALU.mult, ALU.add))
            dve.wait_ge(sem("lora_full"), 3)
            for d in range(2):
                for h in range(2):
                    last = dve.memset(TT[d][h], 0.0)
            link(last)
            dve.sem_inc(sem("pair_done"), 1)
            dve.wait_ge(sem("ld_table1"), 32)
            with dve.Fori(0, KT) as i:
                w = waiter(dve, i)
                link.enter(i, DVE_LINKS)
                w("k_copied", 1)
                dve.tensor_scalar(KK, Kf, dcol("rw_k_k", i), None, ALU.mult).then_inc(sem("kk_raw"), 1)
                for d in range(2):
                    w("sg", d + 1)
                    if d == 1:
                        w("e_inv", 1)
                        w("excl", 1)
                    if d == 0:
                        dve.tensor_tensor_scan(CS, reset[0], SG[0], 0.0, ALU.mult, ALU.add).then_inc(sem("decayed"), 1)
                    else:
                        dve.tensor_tensor_scan(CS[:, ::-1], reset[1][:, ::-1], SG[1][:, ::-1], 0.0, ALU.mult,
                                               ALU.add).then_inc(sem("decayed"), 1)
                    w("rate", d + 1)
                    dve.tensor_scalar(Kt[d], AS[d], dcol("rw_k_a", i), one_ka[:, bass.ds(i, 1)], ALU.mult, ALU.add)\
                        .then_inc(sem("rate_used"), 1)
                    w("rate_used", d + 1)
                    link(dve.tensor_tensor(Kt[d], Kt[d], Kf, ALU.mult))
                    if d == 0:
                        link(dve.tensor_copy(KD, Kt[0][:, seg[1]]))
                    else:
                        link(dve.tensor_tensor(KD, KD, Kt[1][:, seg[1]], ALU.add))
                    if d == 0:
                        w("kstd", 1)
                        w("kk_raw", 1)
                        dve.tensor_tensor(KK, KK, KS, ALU.mult).then_inc(sem("kk_ready"), 1)
                        w("kk_ready", 1)
                    w("e_incl", d + 1)
                    w("r_copied", 1)
                    last_col = C - 1 if d == 0 else 0
                    link(dve.tensor_copy(DC[d], EP.rearrange("p (c t) -> p c t", t=C)[:, :, last_col]))
                    dve.tensor_tensor(Rt[d], Rf, EP[:, seg[1]], ALU.mult).then_inc(sem("r_t"), 1)
                    w("e_inv", d + 1)
                    dve.tensor_tensor(Kt[d], Kt[d], EN, ALU.mult).then_inc(sem("k_t"), 1)
                    w("b_raw", d + 1)
                    dve.tensor_tensor(Bt[d], AS[d], EN, ALU.mult).then_inc(sem("b_t"), 1)
                    w("e_excl", d + 1)
                    dve.scalar_tensor_tensor(out=At[d], in0=KK, scalar=-1.0, in1=EX, op0=ALU.mult, op1=ALU.mult)\
                        .then_inc(sem("a_t"), 1)
                    w("b_t", d + 1)
                    w("k_t", d + 1)
                    w("r_t", d + 1)
                    w("a_t", d + 1)
                link(dve.tensor_tensor(KD, KD, Rf, ALU.mult))
                dve.tensor_scalar(KD, KD, dcol("rw_r_k", i), None, ALU.mult).then_inc(sem("bonus_in"), 1)
                for d in range(2):
                    for h in range(2):
                        w("sc", 6 * d + h + 1)
                        for q in range(4):
                            r = quarter(q)
                            last = dve.tensor_tensor(App[h][r, :, :], b4(h)[r, :, r], each4q(strict32[d][r, :]), ALU.mult)
                        last.then_inc(sem("sc_taken"), 1)
                        w("sc_taken", 6 * d + h + 1)
                        link(dve.tensor_tensor(TMp[h], App[h], each4q(join1[d]), ALU.mult))
                        link(dve.tensor_tensor(TMp[h], TMp[h], each4q(eye32), ALU.add))
                        dve.transpose(TTp[h].rearrange("p b c -> p (b c)"), TMp[h].rearrange("p b c -> p (b c)"))\
                            .then_inc(sem("tri_ready"), 1)
                    for h in range(2):
                        w("sc", 6 * d + 3 + h)
                        dve.tensor_tensor(AakT[h], b4(5 + h), each4(strict[1 - d]), ALU.mult)\
                            .then_inc(sem("sc_taken"), 1)
                    for h in range(2):
                        w("sc", 6 * d + 5 + h)
                        dve.tensor_tensor(ARR[h], b4(2 + h), each4(incl_t[d]), ALU.mult)\
                            .then_inc(sem("sc_taken"), 1)
                    for lv in range(len(LEVELS)):
                        for h in range(2):
                            n = 10 * d + 2 * lv + h + 1
                            w("z_full", n)
                            settle(dve)
                            link(dve.copy_predicated(TMp[h], each4q(bits[lv][d]), packed(JOINED[h])))
                            dve.transpose(TTp[h].rearrange("p b c -> p (b c)"), TMp[h].rearrange("p b c -> p (b c)"))\
                                .then_inc(sem("merged"), 1)
                    for h in range(2):
                        w("merged", 10 * d + 7 + h)
                        for q in range(4):
                            r = quarter(q)
                            dve.tensor_copy(TT[d][h][r, :, r], TTp[h][r, :, :])
                    for h in range(2):
                        w("z_full", 10 * d + 9 + h)
                        for s_ in range(2):
                            late, early = quarter(2 * s_ + 1 - d), quarter(2 * s_ + d)
                            last = dve.tensor_copy(TT[d][h][early, :, late], packed(JOINED[h])[early, :, :])
                        last.then_inc(sem("merged"), 1)
                    w("m_full", d + 1)
                    for o in range(2):
                        last = dve.tensor_tensor(MO[d][:, o::2, :], c4(4 + o), eye64.unsqueeze(1).to_broadcast([P, 4, C]),
                                                 ALU.add)
                    last.then_inc(sem("mo_ready"), 1)
                    w("n_full", d + 1)
                    for o in range(2):
                        last = dve.tensor_tensor(ND[d][:, o::2, :], c4(o),
                                                 DC[d][:, o::2].unsqueeze(2).to_broadcast([P, 4, C]), ALU.mult)
                    last.then_inc(sem("nd_ready"), 1)
                    w("g_full", d + 1)
                    dve.tensor_tensor(GT[d], bank[6][:, 0:SEQ], Rt[d], ALU.add).then_inc(sem("gt_ready"), 1)
                w("nd_ready", 2)
                for d in range(2):
                    dve.tensor_copy(ST[d][:, 1, :], ND[d][:, CHUNKS[d][0], :]).then_inc(sem("st_ready"), 1)
                for st in range(1, 7):
                    for d in range(2):
                        c = CHUNKS[d][st]
                        w("st_full", 2 * (st - 1) + d + 1)
                        dve.scalar_tensor_tensor(out=ST[d][:, st + 1, :], in0=bank[d][:, 0:C], scalar=DC[d][:, c:c + 1],
                                                 in1=ND[d][:, c, :], op0=ALU.mult, op1=ALU.add)\
                            .then_inc(sem("st_ready"), 1)
                w("bonus_full", 1)
                link(dve.tensor_tensor(KD, bank[2][:, 0:SEQ], Vf[:, seg[1]], ALU.mult))
                w("gn_mean", 1)
                dve.tensor_tensor(YN, YF, bank[3][:, 0:SEQ], ALU.subtract).then_inc(sem("gn_cent"), 1)
                w("gn_cent", 1)
                w("gn_std", 1)
                link(dve.scalar_tensor_tensor(out=YN, in0=YN, scalar=dcol("rw_lnx_g", i), in1=YS, op0=ALU.mult,
                                              op1=ALU.mult))
                link(dve.scalar_tensor_tensor(out=YN, in0=YN, scalar=dcol("rw_lnx_b", i), in1=KD, op0=ALU.add,
                                              op1=ALU.add))
                dve.tensor_tensor(YT.rearrange("p k t -> p (k t)")[:, bass.ds(i * SEQ, SEQ)], YN, Gf, ALU.mult)\
                    .then_inc(sem("pair_done"), 1)
                w("pair_done", 2)
            link.leave(KT)
            residual(3, 1, 2, None, 0, streams=(1,))
            layer_norm(3, 1, 0, SEQ)
            modulate(1, 3, streams=(1,))
            dve.wait_ge(sem("logits_full"), 1)
            lg = bank[0][:, 0:16].rearrange("p (t e) -> p t e", t=2)
            dve.tensor_copy(logit, lg).then_inc(sem("logits_taken"), 1)
            dve.wait_ge(sem("logits_taken"), 1)
            for tt in range(2):
                link(dve.max(mx[:, tt, :], logit[:, tt, :]))
                link(dve.max_index(ix.rearrange("p (t e) -> p t e", t=2)[:, tt, :],
                                   mx[:, tt, :], logit[:, tt, :]))
            link(dve.tensor_copy(ixf.rearrange("p t e -> p (t e)"), ix))
            dve.tensor_tensor(w12[:, :, 0:1], mx[:, :, 1:2], mx[:, :, 0:1], ALU.subtract).then_inc(sem("gap"), 1)
            dve.wait_ge(sem("gap_exp"), 1)
            link(dve.tensor_scalar(w12[:, :, 0:1], w12[:, :, 1:2], 1.0, None, ALU.add))
            link(dve.reciprocal(w12[:, :, 2:3], w12[:, :, 0:1]))
            link(dve.tensor_tensor(w12[:, :, 3:4], w12[:, :, 2:3], w12[:, :, 1:2], ALU.mult))
            for tt in range(2):
                link(dve.tensor_scalar(comb[:, tt, :], expert_no, ixf[:, tt, 0:1], w12[:, tt, 2:3], ALU.is_equal, ALU.mult))
                link(dve.tensor_scalar(hot[:, tt, :], expert_no, ixf[:, tt, 1:2], w12[:, tt, 3:4], ALU.is_equal, ALU.mult))
                link(dve.tensor_tensor(comb[:, tt, :], comb[:, tt, :], hot[:, tt, :], ALU.add))
                link(dve.tensor_scalar(hot[:, tt, :], expert_no, ixf[:, tt, 0:1], None, ALU.is_equal))
                link(dve.scalar_tensor_tensor(out=chosen[:, tt, :], in0=expert_no, scalar=ixf[:, tt, 1:2],
                                              in1=hot[:, tt, :], op0=ALU.is_equal, op1=ALU.add))
            dve.sem_inc(sem("routed"), 1)
            dve.memset(slots, -1.0)
            dve.memset(shares, 0.0)
            dve.wait_ge(sem("places_full"), 1)
            link(dve.scalar_tensor_tensor(out=place, in0=bank[0][:, 16:32].rearrange("p (t e) -> p t e", t=2), scalar=1.0,
                                          in1=chosen, op0=ALU.add, op1=ALU.mult))
            for q in range(2):
                dve.tensor_copy(shares[:, :, q * N_EXP:(q + 1) * N_EXP], comb)
                last = dve.tensor_scalar(slots[:, :, q * N_EXP:(q + 1) * N_EXP], place, 1.0 + q * P, None, ALU.subtract)
            link(last)
            link(dve.tensor_reduce(most, bank[0][:, 32:40], AXX, ALU.max))
            dve.tensor_scalar(passes, most, float(P), 1.0, ALU.is_gt, ALU.add).then_inc(sem("routed"), 1)

            def choose(item):
                for tt in range(2):
                    last = dve.tensor_scalar(pick[:, tt, :], slot_no, slots[:, tt, bass.ds(item, 1)], None, ALU.is_equal)
                last.then_inc(sem("expert_vectors"), 1)
            first = STEPS["expert_vectors"].index("pick")
            dve.sem_inc(sem("expert_vectors"), first)
            choose(0)

            def gathered_low(item):
                step(dve, "expert_copies", "xg_high", item - 1)
                for g in range(2):
                    last = dve.tensor_tensor(XGL[:, 4 * g:4 * g + 4, :].rearrange("p a b -> p (a b)"), bank[6 + g][:, :],
                                             XGH[:, 4 * g:4 * g + 4, :].bitcast(F32).rearrange("p a b -> p (a b)"),
                                             ALU.subtract)
                last.then_inc(sem("expert_vectors"), 1)

            def low_digits(j, r, item):
                s_, name = slot_of(3 * j + r), ("gate", "up")[r]
                for i_ in range(PIECES):
                    step(dve, "expert_copies", f"high_{name}{j}_{i_}", item)
                    w_ = ering[s_][:, 2 * i_:2 * i_ + 2, :]
                    dve.tensor_tensor(low[s_][:, 2 * i_:2 * i_ + 2, :], w_, high[i_].bitcast(F32), ALU.subtract)\
                        .then_inc(sem("expert_vectors"), 1)
            link(dve.memset(OUT, 0.0))
            lows = STEPS["expert_vectors"].index("xg_low")
            step(dve, "expert_vectors", "pick", -1)
            dve.sem_inc(sem("expert_vectors"), lows - first - 1)
            gathered_low(0)
            step(dve, "expert_vectors", "xg_low", -1)
            dve.sem_inc(sem("expert_vectors"), len(STEPS["expert_vectors"]) - lows - 1)
            dve.wait_ge(sem("routed"), 2)
            n_passes = dve.value_load(passes[0:1, 0:1], min_val=1, max_val=2)
            with dve.Fori(0, n_passes) as p:
                with dve.Fori(0, N_EXP) as e:
                    item = p * N_EXP + e
                    low_digits(0, 0, item)
                    for j in range(EJ):
                        low_digits(j, 1, item)
                        if j == 3:
                            for tt in range(2):
                                last = dve.tensor_scalar(share[:, tt, :], slot_no, slots[:, tt, bass.ds(item, 1)],
                                                         shares[:, tt, bass.ds(item, 1)], ALU.is_equal, ALU.mult)
                            last.then_inc(sem("expert_vectors"), 1)
                        step(dve, "expert_products", f"up{j}_{PIECES - 1}", item)
                        step(dve, "expert_copies", f"silu{j}", item)
                        dve.tensor_tensor(HTOK[j % 2], sil2[j % 2], bank[2 * (j % 2) + 1][:, :], ALU.mult)\
                            .then_inc(sem("expert_vectors"), 1)
                        if j == 4:
                            choose(item + 1)
                        if j < EJ - 1:
                            low_digits(j + 1, 0, item)
                    step(dve, "expert_products", f"y{EJ - 1}", item)
                    for half in range(2):
                        dve.tensor_copy(YG[:, half * 512:half * 512 + 512], bank[4 + half][:, :])\
                            .then_inc(sem("expert_vectors"), 1)
                    gathered_low(item + 1)
                    step(dve, "expert_vectors", "added3", item - 1)
                    for o in range(4):
                        tt, half = divmod(o, 2)
                        step(dve, "expert_products", f"spread{o}", item)
                        sums = OUT[:, tt, half * 512:half * 512 + 512]
                        dve.tensor_tensor(sums, sums, bank[o][:, :], ALU.add).then_inc(sem("expert_vectors"), 1)
            step(dve, "expert_vectors", "added3", n_passes * N_EXP - 1)
            for tt in range(2):
                o = OUT[:, tt, :]
                link(dve.tensor_tensor(o, o, rowG, ALU.mult))
                link(dve.scalar_tensor_tensor(out=o, in0=XTOK[:, tt, :], scalar=float(ALPHA), in1=o, op0=ALU.mult,
                                              op1=ALU.add))
                link(dve.tensor_reduce(stat[:, tt, 0:1], o, AXX, ALU.add))
                link(dve.tensor_scalar(stat[:, tt, 0:1], stat[:, tt, 0:1], 1.0 / D, None, ALU.mult))
                dve.tensor_scalar(o, o, stat[:, tt, 0:1], None, ALU.subtract).then_inc(sem("fin_centred"), 1)
            for tt in range(2):
                o = OUT[:, tt, :]
                dve.wait_ge(sem("fin_std"), tt + 1)
                link(dve.reciprocal(stat[:, tt, 3:4], stat[:, tt, 2:3]))
                link(dve.scalar_tensor_tensor(out=o, in0=o, scalar=stat[:, tt, 3:4], in1=rowg, op0=ALU.mult, op1=ALU.mult))
                dve.tensor_tensor(o, o, rowb, ALU.add).then_inc(sem("final"), 1)


_INS = ["x", "c", "ctx", "c_ctx", "mod_w", "mod_b", "ln_g", "ln_b", "hy_w_in", "hy_b_in", "hy_conv_w", "hy_conv_b",
        "hy_f_w1", "hy_f_b1", "hy_f_w2", "hy_f_b2", "hy_f_freq", "hy_f_w3", "hy_decay", "hy_skip", "hy_w_out",
        "hy_b_out", "rw_mu", "rw_w_rkv", "rw_w0", "rw_w1", "rw_w2", "rw_a0", "rw_a1", "rw_a2", "rw_g1", "rw_g2",
        "rw_k_k", "rw_k_a", "rw_r_k", "rw_lnx_g", "rw_lnx_b", "rw_w_out", "ffn_w13", "ffn_w2", "moe_router",
        "moe_w13", "moe_w2"]


def kernel(**inputs):
    import concourse.bacc as _bacc
    from concourse.bass_utils import run_bass_kernel_spmd as _run

    nc = _bacc.Bacc("TRN2", target_bir_lowering=False, num_devices=1)
    arrays, args = {}, {}
    for name in _INS:
        v = np.ascontiguousarray(inputs[name])
        arrays[f"in_{name}_dram"] = v
        args[name] = nc.dram_tensor(f"in_{name}_dram", v.shape, mybir.dt.from_np(v.dtype), kind="ExternalInput").ap()
    consts = []
    for n, v in enumerate(constants()):
        arrays[f"const_{n}_dram"] = v
        consts.append(nc.dram_tensor(f"const_{n}_dram", v.shape, mybir.dt.from_np(v.dtype), kind="ExternalInput").ap())
    out = nc.dram_tensor("out_0_dram", (1, SEQ, D), F32, kind="ExternalOutput").ap()
    build(nc, args, out, consts)
    r = _run(nc, [arrays], core_ids=[0])
    return r.results[0]["out_0_dram"]
```
